# Optimizing a Trainium2 kernel written in Bass

```python
import math
import jax
import jax.numpy as jnp
from jax import lax
import numpy as np

D_MODEL = 1024
BATCH = 1
SEQ = 256
DEPTH = 2

GRID_W = 64
CTX_LEN = 256
HEAD_DIM = 64
ROPE_THETA = 10000.0
NORM_EPS = 1e-6
NEG_INF = -1e30

SWA_HEADS = 8
SWA_KV_HEADS = 2
WINDOW = 128
BLOCK = 128

RWKV_HEADS = 8
RWKV_WIDTH = RWKV_HEADS * HEAD_DIM
DECAY_LORA = 64
AAA_LORA = 64
GATE_LORA = 128
RWKV_GN_EPS = 64e-5

DIFF_HEADS = 4
DIFF_V_DIM = 2 * HEAD_DIM
DIFF_SUBLN_EPS = 1e-5

N_BRANCHES = 3

D_FF = 2816
N_EXPERTS = 8
TOP_K = 2
D_FF_EXPERT = 3584
MOE_BLOCK = 128
N_DENSE = (DEPTH + 1) // 2
N_MOE = DEPTH // 2

SWA_Q = SWA_HEADS * HEAD_DIM
SWA_KV = SWA_KV_HEADS * HEAD_DIM
RWKV_SPLITS = (RWKV_WIDTH, RWKV_WIDTH, RWKV_WIDTH, DECAY_LORA, DECAY_LORA, AAA_LORA, AAA_LORA, GATE_LORA)
RWKV_COLS = 3 * RWKV_WIDTH + 2 * DECAY_LORA + 2 * AAA_LORA + GATE_LORA
DIFF_QK = DIFF_HEADS * 2 * HEAD_DIM
DIFF_V = DIFF_HEADS * DIFF_V_DIM
IN_SPLITS = (SWA_Q, SWA_KV, SWA_KV, RWKV_COLS, DIFF_QK, DIFF_QK, DIFF_V, N_BRANCHES * D_MODEL)
D_IN = SWA_Q + 2 * SWA_KV + RWKV_COLS + 2 * DIFF_QK + DIFF_V + N_BRANCHES * D_MODEL

kernel_name = 'hybrid_diffusion_trunk_swa_rwkv7_diffattn_moe'

def rmsnorm(x, g, eps=NORM_EPS):
    xf = x.astype(jnp.float32)
    y = xf * lax.rsqrt(jnp.mean(xf * xf, axis=-1, keepdims=True) + eps)
    return (y * g.astype(jnp.float32)).astype(x.dtype)

def modulate(h, shift, scale):
    return h * (1 + scale) + shift

def _split(t, sizes):
    out, start = [], 0
    for n in sizes:
        out.append(t[..., start:start + n])
        start += n
    return out

def axial_rope_tables(n_tokens):
    rows = n_tokens // GRID_W
    row = jnp.broadcast_to(jnp.arange(rows, dtype=jnp.float32)[:, None], (rows, GRID_W)).reshape(-1)
    col = jnp.broadcast_to(jnp.arange(GRID_W, dtype=jnp.float32)[None, :], (rows, GRID_W)).reshape(-1)
    axis_dim = HEAD_DIM // 2
    inv_freq = ROPE_THETA ** (-jnp.arange(0, axis_dim, 2, dtype=jnp.float32) / axis_dim)
    ang = jnp.stack([row[:, None] * inv_freq, col[:, None] * inv_freq], axis=1)
    return jnp.cos(ang), jnp.sin(ang)

def apply_rope(x, cos, sin):
    shp = x.shape
    xr = x.reshape(shp[:-1] + (2, 2, HEAD_DIM // 4))
    bshape = (shp[1],) + (1,) * (x.ndim - 3) + (2, HEAD_DIM // 4)
    cs = cos.reshape(bshape).astype(x.dtype)
    sn = sin.reshape(bshape).astype(x.dtype)
    x1, x2 = xr[..., 0, :], xr[..., 1, :]
    out = jnp.stack([x1 * cs - x2 * sn, x1 * sn + x2 * cs], axis=-2)
    return out.reshape(shp)

def swa_attention(q_l, k_l, v_l, q_c, k_c, v_c, sink, need_ctx):
    B, S = q_l.shape[:2]
    L = k_c.shape[1]
    nb = S // BLOCK
    G = SWA_HEADS // SWA_KV_HEADS
    scale = HEAD_DIM ** -0.5
    sink_f = sink.astype(jnp.float32).reshape(SWA_KV_HEADS, G)
    qb = q_l.reshape(B, nb, BLOCK, SWA_KV_HEADS, G, HEAD_DIM)

    def windows(t):
        tp = jnp.pad(t, ((0, 0), (BLOCK, BLOCK), (0, 0), (0, 0)))
        tb = tp.reshape(B, nb + 2, BLOCK, SWA_KV_HEADS, HEAD_DIM)
        return jnp.concatenate([tb[:, :-2], tb[:, 1:-1], tb[:, 2:]], axis=2)

    kw, vw = windows(k_l), windows(v_l)
    qpos = (jnp.arange(nb)[:, None] * BLOCK + jnp.arange(BLOCK)[None, :])[:, :, None]
    kpos = ((jnp.arange(nb)[:, None] - 1) * BLOCK + jnp.arange(3 * BLOCK)[None, :])[:, None, :]
    valid = (jnp.abs(kpos - qpos) <= WINDOW) & (kpos >= 0) & (kpos < S)
    s_loc = jnp.einsum('bnqhgd,bnkhd->bnhgqk', qb, kw, preferred_element_type=jnp.float32) * scale
    s_loc = jnp.where(valid[None, :, None, None], s_loc, NEG_INF)
    s_ctx = jnp.einsum('bnqhgd,blhd->bnhgql', qb, k_c, preferred_element_type=jnp.float32) * scale
    s_sink = jnp.broadcast_to(sink_f[None, None, :, :, None, None], s_loc.shape[:-1] + (1,))
    p = jax.nn.softmax(jnp.concatenate([s_loc, s_ctx, s_sink], axis=-1), axis=-1)
    nw = 3 * BLOCK
    o = (jnp.einsum('bnhgqk,bnkhd->bnqhgd', p[..., :nw].astype(v_l.dtype), vw)
         + jnp.einsum('bnhgql,blhd->bnqhgd', p[..., nw:nw + L].astype(v_l.dtype), v_c))
    o_lat = o.reshape(B, S, SWA_Q)
    if not need_ctx:
        return o_lat, None
    qcg = q_c.reshape(B, L, SWA_KV_HEADS, G, HEAD_DIM)
    sc = jnp.einsum('blhgd,bmhd->bhglm', qcg, k_c, preferred_element_type=jnp.float32) * scale
    sc_sink = jnp.broadcast_to(sink_f[None, :, :, None, None], sc.shape[:-1] + (1,))
    pc = jax.nn.softmax(jnp.concatenate([sc, sc_sink], axis=-1), axis=-1)
    oc = jnp.einsum('bhglm,bmhd->blhgd', pc[..., :L].astype(v_c.dtype), v_c)
    return o_lat, oc.reshape(B, L, SWA_Q)

def token_shift(p, mu_prev, mu_next):
    prev = jnp.pad(p[:, :-1], ((0, 0), (1, 0), (0, 0)))
    nxt = jnp.pad(p[:, 1:], ((0, 0), (0, 1), (0, 0)))
    return p + mu_prev * (prev - p) + mu_next * (nxt - p)

def rwkv_scan(s0, r, w, k, v, a_vec, b_vec, reverse, emit):
    xs = tuple(jnp.moveaxis(t, 1, 0) for t in (r, w, k, v, a_vec, b_vec))

    def step(s, inp):
        r_t, w_t, k_t, v_t, a_t, b_t = inp
        sa = jnp.einsum('bhvk,bhk->bhv', s, a_t)
        s = s * w_t[:, :, None, :] + sa[..., None] * b_t[:, :, None, :] + v_t[..., None] * k_t[:, :, None, :]
        y = jnp.einsum('bhvk,bhk->bhv', s, r_t) if emit else None
        return s, y

    s_fin, ys = lax.scan(step, s0, xs, reverse=reverse)
    return s_fin, (jnp.moveaxis(ys, 0, 1) if emit else None)

def _rwkv_prepare(p, lp):
    B, T = p.shape[:2]
    f32 = jnp.float32
    p = token_shift(p, lp['rwkv_mu_prev'], lp['rwkv_mu_next'])
    r, k, v, wd_f, wd_b, ad_f, ad_b, gd = _split(p, RWKV_SPLITS)
    hd = lambda t: t.astype(f32).reshape(B, T, RWKV_HEADS, HEAD_DIM)
    g = jax.nn.sigmoid(gd) @ lp['rwkv_g_up']
    k_h = hd(k)
    kk = k_h * lp['rwkv_k_k'].astype(f32).reshape(RWKV_HEADS, HEAD_DIM)
    kk = kk / jnp.maximum(jnp.sqrt(jnp.sum(kk * kk, axis=-1, keepdims=True)), 1e-12)
    k_a = lp['rwkv_k_a'].astype(f32).reshape(RWKV_HEADS, HEAD_DIM)
    dirs = []
    for d, (wd, ad) in enumerate(((wd_f, ad_f), (wd_b, ad_b))):
        w_raw = (lp['rwkv_w0'][d] + jnp.tanh(wd) @ lp['rwkv_w_up'][d]).astype(f32)
        w_log = -jax.nn.softplus(-w_raw) - 0.5
        decay = hd(jnp.exp(-jnp.exp(w_log)))
        a = hd(jax.nn.sigmoid((lp['rwkv_a0'][d] + ad @ lp['rwkv_a_up'][d]).astype(f32)))
        k_eff = k_h * (1 + (a - 1) * k_a)
        dirs.append((decay, k_eff, a))
    return hd(r), hd(v), kk, g, dirs

def _rwkv_output(ys, r, v, k_effs, g, lp, dtype):
    B, T = r.shape[:2]
    f32 = jnp.float32
    y = ys[0] + ys[1]
    mu = jnp.mean(y, axis=-1, keepdims=True)
    var = jnp.mean(jnp.square(y - mu), axis=-1, keepdims=True)
    y = ((y - mu) * lax.rsqrt(var + RWKV_GN_EPS)).reshape(B, T, RWKV_WIDTH)
    y = y * lp['rwkv_lnx_g'].astype(f32) + lp['rwkv_lnx_b'].astype(f32)
    r_k = lp['rwkv_r_k'].astype(f32)
    bonus = jnp.sum(r * (k_effs[0] + k_effs[1]) * r_k, axis=-1, keepdims=True) * v
    y = y + bonus.reshape(B, T, RWKV_WIDTH)
    return (y * g.astype(f32)).astype(dtype)

def rwkv7_bidirectional(p_lat, p_ctx, lp, need_ctx):
    B = p_lat.shape[0]
    r_l, v_l, kk_l, g_l, dirs_l = _rwkv_prepare(p_lat, lp)
    r_c, v_c, kk_c, g_c, dirs_c = _rwkv_prepare(p_ctx, lp)
    s0 = jnp.zeros((B, RWKV_HEADS, HEAD_DIM, HEAD_DIM), jnp.float32)
    y_lat, y_ctx = [], []
    for d, reverse in enumerate((False, True)):
        w_c, k_c, a_c = dirs_c[d]
        s_ctx, y_c = rwkv_scan(s0, r_c, w_c, k_c, v_c, -kk_c, kk_c * a_c, reverse, need_ctx)
        w_l, k_l, a_l = dirs_l[d]
        _, y_l = rwkv_scan(s_ctx, r_l, w_l, k_l, v_l, -kk_l, kk_l * a_l, reverse, True)
        y_lat.append(y_l)
        y_ctx.append(y_c)
    out_l = _rwkv_output(y_lat, r_l, v_l, [dd[1] for dd in dirs_l], g_l, lp, p_lat.dtype)
    if not need_ctx:
        return out_l, None
    out_c = _rwkv_output(y_ctx, r_c, v_c, [dd[1] for dd in dirs_c], g_c, lp, p_ctx.dtype)
    return out_l, out_c

def diff_attention(q_l, k_l, v_l, q_c, k_c, v_c, lam, subln_g, lam_init, need_ctx):
    B, S = q_l.shape[:2]
    nb = S // BLOCK
    scale = HEAD_DIM ** -0.5
    k_all = jnp.concatenate([k_l, k_c], axis=1)
    v_all = jnp.concatenate([v_l, v_c], axis=1)

    def attend(q, k, v):
        s = jnp.einsum('bqhcd,bkhcd->bhcqk', q, k, preferred_element_type=jnp.float32) * scale
        p = jax.nn.softmax(s, axis=-1)
        a = p[:, :, 0] - lam * p[:, :, 1]
        return jnp.einsum('bhqk,bkhe->bqhe', a.astype(v.dtype), v)

    def finish(o):
        return (rmsnorm(o, subln_g, DIFF_SUBLN_EPS) * (1.0 - lam_init)).reshape(o.shape[0], o.shape[1], DIFF_V)

    q_blocks = jnp.moveaxis(q_l.reshape(B, nb, BLOCK, DIFF_HEADS, 2, HEAD_DIM), 1, 0)
    o = lax.map(lambda qb: attend(qb, k_all, v_all), q_blocks)
    o_lat = finish(jnp.moveaxis(o, 0, 1).reshape(B, S, DIFF_HEADS, DIFF_V_DIM))
    if not need_ctx:
        return o_lat, None
    return o_lat, finish(attend(q_c, k_c, v_c))

def token_mixer(h_l, h_c, lp, layer, need_ctx, cos, sin):
    pl = _split(h_l @ lp['w_in'], IN_SPLITS)
    pc = _split(h_c @ lp['w_in'], IN_SPLITS)
    heads = lambda t, n: t.reshape(t.shape[0], t.shape[1], n, HEAD_DIM)
    pair = lambda t: t.reshape(t.shape[0], t.shape[1], DIFF_HEADS, 2, HEAD_DIM)
    vh = lambda t: t.reshape(t.shape[0], t.shape[1], DIFF_HEADS, DIFF_V_DIM)
    ya_l, ya_c = swa_attention(
        apply_rope(heads(pl[0], SWA_HEADS), cos, sin), apply_rope(heads(pl[1], SWA_KV_HEADS), cos, sin),
        heads(pl[2], SWA_KV_HEADS), heads(pc[0], SWA_HEADS), heads(pc[1], SWA_KV_HEADS),
        heads(pc[2], SWA_KV_HEADS), lp['swa_sink'], need_ctx)
    yb_l, yb_c = rwkv7_bidirectional(pl[3], pc[3], lp, need_ctx)
    lam_vec = lp['diff_lambda'].astype(jnp.float32)
    lam_init = 0.8 - 0.6 * math.exp(-0.3 * layer)
    lam = jnp.exp(jnp.sum(lam_vec[0] * lam_vec[1])) - jnp.exp(jnp.sum(lam_vec[2] * lam_vec[3])) + lam_init
    yc_l, yc_c = diff_attention(
        apply_rope(pair(pl[4]), cos, sin), apply_rope(pair(pl[5]), cos, sin), vh(pl[6]),
        pair(pc[4]), pair(pc[5]), vh(pc[6]), lam, lp['diff_subln_g'], lam_init, need_ctx)

    def merge(ya, yb, yc, gate_cols):
        gates = jax.nn.sigmoid(gate_cols.astype(jnp.float32)).astype(ya.dtype)
        g_a, g_b, g_c = _split(gates, (D_MODEL, D_MODEL, D_MODEL))
        merged = g_a * (ya @ lp['proj_swa']) + g_b * (yb @ lp['proj_rwkv']) + g_c * (yc @ lp['proj_diff'])
        return merged @ lp['w_out']

    out_l = merge(ya_l, yb_l, yc_l, pl[7])
    out_c = merge(ya_c, yb_c, yc_c, pc[7]) if need_ctx else None
    return out_l, out_c

def swiglu(h, w_gate, w_up, w_down):
    return (jax.nn.silu(h @ w_gate) * (h @ w_up)) @ w_down

def moe_swiglu(h, router_w, w_gate, w_up, w_down):
    N, D = h.shape
    logits = (h @ router_w).astype(jnp.float32)
    top_v, top_i = lax.top_k(logits, TOP_K)
    top_w = jax.nn.softmax(top_v, axis=-1)
    A = N * TOP_K
    e_flat = top_i.reshape(A)
    t_flat = jnp.repeat(jnp.arange(N, dtype=jnp.int32), TOP_K)
    w_flat = top_w.reshape(A)
    order = jnp.argsort(e_flat)
    e_sorted, t_sorted, w_sorted = e_flat[order], t_flat[order], w_flat[order]
    counts = jnp.zeros((N_EXPERTS,), jnp.int32).at[e_flat].add(1)
    starts = jnp.cumsum(counts) - counts
    padded = (counts + MOE_BLOCK - 1) // MOE_BLOCK * MOE_BLOCK
    pends = jnp.cumsum(padded)
    pstarts = pends - padded
    dest = pstarts[e_sorted] + jnp.arange(A, dtype=jnp.int32) - starts[e_sorted]
    n_blocks = -(-A // MOE_BLOCK) + N_EXPERTS
    P = n_blocks * MOE_BLOCK
    tok = jnp.zeros((P,), jnp.int32).at[dest].set(t_sorted)
    wts = jnp.zeros((P,), jnp.float32).at[dest].set(w_sorted)
    block_start = jnp.arange(n_blocks, dtype=jnp.int32) * MOE_BLOCK
    blk_e = jnp.minimum(jnp.searchsorted(pends, block_start, side='right'), N_EXPERTS - 1)

    def run(args):
        tb, wb, e = args
        xb = h[tb]
        hid = jax.nn.silu(xb @ w_gate[e]) * (xb @ w_up[e])
        return (hid @ w_down[e]) * wb[:, None].astype(h.dtype)

    yb = lax.map(run, (tok.reshape(n_blocks, MOE_BLOCK), wts.reshape(n_blocks, MOE_BLOCK), blk_e))
    return jnp.zeros_like(h).at[tok].add(yb.reshape(P, D))

def setup_inputs(seed: int = 0) -> dict:
    key = jax.random.key(seed)
    ks = iter(jax.random.split(key, 40))
    f32 = jnp.float32
    Dm = D_MODEL

    def nrm(shape, scale):
        return jax.random.normal(next(ks), shape, f32) * scale

    def gain(shape):
        return 1.0 + 0.02 * jax.random.normal(next(ks), shape, f32)

    def unif(shape, lo, hi):
        return jax.random.uniform(next(ks), shape, f32, lo, hi)

    return {
        'x': nrm((BATCH, SEQ, Dm), 1.0),
        'c': nrm((BATCH, Dm), 1.0),
        'ctx': nrm((BATCH, CTX_LEN, Dm), 1.0),
        'c_ctx': nrm((Dm,), 1.0),
        'ada_w': nrm((DEPTH, Dm, 6 * Dm), 0.5 * Dm ** -0.5),
        'ada_b': nrm((DEPTH, 6 * Dm), 0.02),
        'pre_mix_g': gain((DEPTH, Dm)),
        'post_mix_g': gain((DEPTH, Dm)),
        'pre_ffn_g': gain((DEPTH, Dm)),
        'post_ffn_g': gain((DEPTH, Dm)),
        'w_in': nrm((DEPTH, Dm, D_IN), Dm ** -0.5),
        'swa_sink': nrm((DEPTH, SWA_HEADS), 0.5),
        'rwkv_mu_prev': unif((DEPTH, RWKV_COLS), 0.0, 0.5),
        'rwkv_mu_next': unif((DEPTH, RWKV_COLS), 0.0, 0.5),
        'rwkv_w0': unif((DEPTH, 2, RWKV_WIDTH), -6.0, 1.0),
        'rwkv_w_up': nrm((DEPTH, 2, DECAY_LORA, RWKV_WIDTH), 0.1 * DECAY_LORA ** -0.5),
        'rwkv_a0': nrm((DEPTH, 2, RWKV_WIDTH), 0.1),
        'rwkv_a_up': nrm((DEPTH, 2, AAA_LORA, RWKV_WIDTH), 0.1 * AAA_LORA ** -0.5),
        'rwkv_g_up': nrm((DEPTH, GATE_LORA, RWKV_WIDTH), GATE_LORA ** -0.5),
        'rwkv_k_k': 0.85 + nrm((DEPTH, RWKV_WIDTH), 0.05),
        'rwkv_k_a': 1.0 + nrm((DEPTH, RWKV_WIDTH), 0.05),
        'rwkv_r_k': nrm((DEPTH, RWKV_HEADS, HEAD_DIM), 0.1),
        'rwkv_lnx_g': gain((DEPTH, RWKV_WIDTH)),
        'rwkv_lnx_b': nrm((DEPTH, RWKV_WIDTH), 0.02),
        'diff_lambda': nrm((DEPTH, 4, HEAD_DIM), 0.1),
        'diff_subln_g': gain((DEPTH, DIFF_V_DIM)),
        'proj_swa': nrm((DEPTH, SWA_Q, Dm), SWA_Q ** -0.5),
        'proj_rwkv': nrm((DEPTH, RWKV_WIDTH, Dm), RWKV_WIDTH ** -0.5),
        'proj_diff': nrm((DEPTH, DIFF_V, Dm), DIFF_V ** -0.5),
        'w_out': nrm((DEPTH, Dm, Dm), Dm ** -0.5),
        'ffn_w_gate': nrm((N_DENSE, Dm, D_FF), Dm ** -0.5),
        'ffn_w_up': nrm((N_DENSE, Dm, D_FF), Dm ** -0.5),
        'ffn_w_down': nrm((N_DENSE, D_FF, Dm), D_FF ** -0.5),
        'router_w': nrm((N_MOE, Dm, N_EXPERTS), Dm ** -0.5),
        'moe_w_gate': nrm((N_MOE, N_EXPERTS, Dm, D_FF_EXPERT), Dm ** -0.5),
        'moe_w_up': nrm((N_MOE, N_EXPERTS, Dm, D_FF_EXPERT), Dm ** -0.5),
        'moe_w_down': nrm((N_MOE, N_EXPERTS, D_FF_EXPERT, Dm), D_FF_EXPERT ** -0.5),
    }

def reference(x, c, ctx, c_ctx, ada_w, ada_b, pre_mix_g, post_mix_g, pre_ffn_g, post_ffn_g,
              w_in, swa_sink, rwkv_mu_prev, rwkv_mu_next, rwkv_w0, rwkv_w_up, rwkv_a0, rwkv_a_up,
              rwkv_g_up, rwkv_k_k, rwkv_k_a, rwkv_r_k, rwkv_lnx_g, rwkv_lnx_b, diff_lambda,
              diff_subln_g, proj_swa, proj_rwkv, proj_diff, w_out, ffn_w_gate, ffn_w_up,
              ffn_w_down, router_w, moe_w_gate, moe_w_up, moe_w_down):
    B, S, D = x.shape
    L = ctx.shape[1]
    cos, sin = axial_rope_tables(S)
    h_lat, h_ctx = x, ctx
    for layer in range(DEPTH):
        need_ctx = layer < DEPTH - 1
        lp = {
            'w_in': w_in[layer], 'swa_sink': swa_sink[layer],
            'rwkv_mu_prev': rwkv_mu_prev[layer], 'rwkv_mu_next': rwkv_mu_next[layer],
            'rwkv_w0': rwkv_w0[layer], 'rwkv_w_up': rwkv_w_up[layer],
            'rwkv_a0': rwkv_a0[layer], 'rwkv_a_up': rwkv_a_up[layer], 'rwkv_g_up': rwkv_g_up[layer],
            'rwkv_k_k': rwkv_k_k[layer], 'rwkv_k_a': rwkv_k_a[layer], 'rwkv_r_k': rwkv_r_k[layer],
            'rwkv_lnx_g': rwkv_lnx_g[layer], 'rwkv_lnx_b': rwkv_lnx_b[layer],
            'diff_lambda': diff_lambda[layer], 'diff_subln_g': diff_subln_g[layer],
            'proj_swa': proj_swa[layer], 'proj_rwkv': proj_rwkv[layer], 'proj_diff': proj_diff[layer],
            'w_out': w_out[layer],
        }
        mod_l = jnp.split((jax.nn.silu(c) @ ada_w[layer] + ada_b[layer])[:, None, :], 6, axis=-1)
        mod_c = jnp.split((jax.nn.silu(c_ctx) @ ada_w[layer] + ada_b[layer])[None, None, :], 6, axis=-1)

        a_l = modulate(rmsnorm(h_lat, pre_mix_g[layer]), mod_l[0], mod_l[1])
        a_c = modulate(rmsnorm(h_ctx, pre_mix_g[layer]), mod_c[0], mod_c[1])
        m_l, m_c = token_mixer(a_l, a_c, lp, layer, need_ctx, cos, sin)
        h_lat = h_lat + mod_l[2] * rmsnorm(m_l, post_mix_g[layer])
        if need_ctx:
            h_ctx = h_ctx + mod_c[2] * rmsnorm(m_c, post_mix_g[layer])

        f_l = modulate(rmsnorm(h_lat, pre_ffn_g[layer]), mod_l[3], mod_l[4]).reshape(B * S, D)
        if need_ctx:
            f_c = modulate(rmsnorm(h_ctx, pre_ffn_g[layer]), mod_c[3], mod_c[4]).reshape(B * L, D)
            toks = jnp.concatenate([f_l, f_c], axis=0)
        else:
            toks = f_l
        j = layer // 2
        if layer % 2 == 0:
            f = swiglu(toks, ffn_w_gate[j], ffn_w_up[j], ffn_w_down[j])
        else:
            f = moe_swiglu(toks, router_w[j], moe_w_gate[j], moe_w_up[j], moe_w_down[j])
        h_lat = h_lat + mod_l[5] * rmsnorm(f[:B * S].reshape(B, S, D), post_ffn_g[layer])
        if need_ctx:
            h_ctx = h_ctx + mod_c[5] * rmsnorm(f[B * S:].reshape(B, L, D), post_ffn_g[layer])
    return h_lat


_drawn_inputs = setup_inputs


def setup_inputs(seed=0):
    import zlib

    import numpy as np

    out = dict(_drawn_inputs(seed))
    spreads = {}
    factors = {'pre_mix_g': 3.473,
     'post_mix_g': 3.679,
     'post_ffn_g': 5.547,
     'swa_sink': 64.0,
     'rwkv_w_up': 5.224,
     'rwkv_a_up': 3.167,
     'rwkv_lnx_g': 3.883,
     'rwkv_lnx_b': 4.081,
     'diff_subln_g': 4.517}
    for name, (base, spread) in spreads.items():
        noise = np.random.default_rng([zlib.crc32(name.encode()), seed]).standard_normal(out[name].shape)
        drawn = base * np.exp(spread * noise) if base else spread * noise
        out[name] = jnp.asarray(drawn.astype(out[name].dtype))
    for name, factor in factors.items():
        out[name] = (out[name] * factor).astype(out[name].dtype)
    return out
```

```python
import math
from contextlib import ExitStack

import numpy as np

import concourse.bass as bass
from concourse import mybir

D = 1024
T = 512
SEQ = 256
KT = D // 128
HD = 64
CH = 64
NCH = T // CH
FF = 2816
FT = FF // 128
EF = 3584
ET = EF // 128
NE = 8
SW_COLS, RW_COLS, DF_COLS = 768, 1920, 1536
C_RW = SW_COLS
C_DF = SW_COLS + RW_COLS
C_GATE = C_DF + DF_COLS
RT_TILES = RW_COLS // 128
KAPPA = math.exp(-0.5)
BWD = [3, 2, 1, 0, 7, 6, 5, 4]
NEG = -1e30

VEC = {}
_at = 0
for _n, _w in [("pre_mix", 8), ("post_mix", 8), ("pre_ffn", 8), ("post_ffn", 8), ("ada_b", 48), ("mu_p", 15),
               ("mu_n", 15), ("w0", 8), ("a0", 8), ("k_k", 4), ("k_a", 4), ("r_k", 4), ("ln_g", 4), ("ln_b", 4),
               ("subln", 1)]:
    VEC[_n] = (_at, _w)
    _at += _w
VEC_L = _at


def tables():
    f = np.float32
    n = np.arange(SEQ)
    row, col = (n // 64).astype(f), (n % 64).astype(f)
    inv = (np.float32(10000.0) ** (-np.arange(0, 32, 2, dtype=f) / f(32))).astype(f)
    cosT, sinT = np.zeros((128, SEQ), f), np.zeros((128, SEQ), f)
    perm, swap = np.zeros((128, 128), f), np.zeros((128, 128), f)
    for p in range(128):
        q = p % 64
        axis, half, i = q // 32, (q % 32) // 16, q % 16
        ang = ((row if axis == 0 else col) * inv[i]).astype(f)
        cosT[p], sinT[p] = np.cos(ang), np.sin(ang)
        if half == 0:
            perm[p + 16, p] = -1.0
        else:
            perm[p - 16, p] = 1.0
        swap[(p + 64) % 128, p] = 1.0
    eye = np.eye(128, dtype=f)
    blk = np.kron(np.eye(2), np.full((64, 64), 1 / 64)).astype(f)
    r, c = np.arange(128)[:, None], np.arange(128)[None, :]
    band = np.concatenate([np.where(c <= r, 0, NEG), np.where(c >= r, 0, NEG)], 1).astype(f)
    r, c = (np.arange(128) % 64)[:, None], np.arange(64)[None, :]
    later = [lambda a, b: a > b, lambda a, b: a < b]
    two = lambda g: np.stack([g(0), g(1)], 1).astype(f)
    masks = [two(lambda d: later[d](c, r)), two(lambda d: later[d](c, r) | (c == r))]
    for m in (1, 2, 4, 8, 16, 32):
        masks.append(two(lambda d: (r // (2 * m) == c // (2 * m)) & (r // m != c // m) & later[d](r, c)))
    masks.append(two(lambda d: (r // 2 == c // 2) & later[d](c, r)))
    masks.append(two(lambda d: (r == c)))
    masks = np.stack(masks, 1).reshape(128, -1)
    return np.concatenate([eye, perm, swap, blk, np.ones((128, 128), f), cosT, sinT, band, masks,
                           np.broadcast_to(np.arange(128, dtype=f), (128, 128))], 1)


TAB = {}
_at = 0
for _n, _w in [("eye", 128), ("perm", 128), ("swap", 128), ("blk", 128), ("ones", 128), ("cos", 256), ("sin", 256),
               ("band", 256), ("masks", 10 * 128), ("iota", 128)]:
    TAB[_n] = (_at, _w)
    _at += _w
TAB_W = _at
M_STRICT_T, M_INCL_T, M_LEVEL, M_PAIR_T, M_EYE = 0, 1, 2, 8, 9


class Ring:

    def __init__(self, banks, full, free):
        self.banks, self.full, self.free = banks, full, free
        self.made = self.taken = self.due = 0
        self.jobs = {}

    def claim(self):
        self.due = max(0, self.made - len(self.banks) + 1)
        return self.banks[self.made % len(self.banks)]

    def done(self, name=None):
        self.made += 1
        self.jobs[name] = self.made

    def take(self):
        self.taken += 1
        return self.banks[(self.taken - 1) % len(self.banks)]


class Seen:

    def __init__(self):
        self.n = {}

    def __call__(self, sem, k=1):
        self.n[sem.name] = self.n.get(sem.name, 0) + k
        return self.n[sem.name]


def trunk(nc, io, out, dbg=None, stop=None):
    f32 = mybir.dt.float32
    u32 = mybir.dt.uint32
    ALU = mybir.AluOpType
    ACT = mybir.ActivationFunctionType
    AX = mybir.AxisListType

    ctx = ExitStack()
    with ctx:
        def sb(name, shape, dt=f32):
            return ctx.enter_context(nc.sbuf_tensor(name, shape, dt))

        def sem(name):
            return ctx.enter_context(nc.semaphore(name))

        HT = sb("HT", [128, KT, T])
        AT = sb("AT", [128, KT, T])
        SLOTS, SLOT = 3, 4096
        WR = sb("WR", [128, SLOTS, SLOT])
        YA = sb("YA", [128, 4, T])
        YB = sb("YB", [128, 4, T])
        YC = sb("YC", [128, 4, T])
        tab = sb("tab", [128, TAB_W])
        vec = sb("vec", [128, 2 * VEC_L + 16])
        rep = sb("rep", [128, 2, 8 + 256])
        mods = sb("mods", [128, 48, 2])
        coef = sb("coef", [128, 4, KT, 2])
        silc = sb("silc", [128, KT, 2])
        muc = sb("muc", [128, RT_TILES])
        cvec = sb("cvec", [128, 32])
        sink8, cv2 = cvec[:, 8:16], cvec[:, 16:20]
        st = sb("st", [128, 4, 2, 4])
        RS = sb("RS", [128, 2, T])
        eS = sb("eS", [128, 2, 8])
        rt = sb("rt", [128, 2, 64])
        rti = sb("rti", [128, 2, 8], u32)
        AR_W = 21100
        ar = sb("ar", [128, AR_W])

        def V(l, name, i=None):
            a, w = VEC[name]
            a += l * VEC_L
            return vec[:, a:a + w] if i is None else vec[:, a + i:a + i + 1]

        def tb(name):
            a, w = TAB[name]
            return tab[:, a:a + w]

        eye, perm, swap, blk, ones = tb("eye"), tb("perm"), tb("swap"), tb("blk"), tb("ones")
        masks = tb("masks").rearrange("p (m d c) -> p m d c", m=10, d=2)

        def area(at, n, w=T):
            return ar[:, at:at + n * w].rearrange("p (n w) -> p n w", n=n)

        Rr, Rk, Rv, Rkk = area(0, 4), area(2048, 4), area(4096, 4), area(6144, 4)
        Ra = ar[:, 8192:12288].rearrange("p (d j t) -> p d j t", d=2, j=4)
        CW = CH + 1
        Rc = ar[:, 12288:12288 + 2 * 4 * NCH * CW].rearrange("p (d j c w) -> p d j c w", d=2, j=4, c=NCH)
        TR0 = 12288 + 2 * 4 * NCH * CW
        HTf = HT[:, :, :].rearrange("p k t -> p (k t)")
        names = ["E1", "E2", "E3", "ba", "ka", "LT", "X", "XT"]
        tr = {n: HTf[:, i * 512:i * 512 + 512] for i, n in enumerate(names)}
        names = ["MT", "RBT", "RKT", "bt", "kt", "at", "vt", "S"]
        tr.update({n: ar[:, TR0 + i * 512:TR0 + i * 512 + 512] for i, n in enumerate(names)})
        tr.update({"T1": RS[:, 0, :], "Sr": RS[:, 1, :], "ra": tr["E1"], "aa": tr["E2"]})
        CC = ar[:, TR0 + 8 * 512:TR0 + 8 * 512 + 8 * CW].rearrange("p (q w) -> p q w", q=8)
        assert TR0 + 8 * 512 + 8 * CW <= AR_W
        Gm, Zm, W1T, Um = tr["ka"], tr["E3"], tr["aa"], tr["X"]
        tmpT = [tr[n] for n in ("ba", "ka", "X", "XT", "MT", "RBT", "RKT", "bt", "kt")]
        tmpO = [tr["MT"], tr["RBT"]]
        thw, wdin, adin, gdin, sgd = tmpT[4:9]
        sgt = [tr["E1"], tr["E2"]]
        onesw = tr["E3"][:, 0:CH]
        rowb = area(0, 2)
        Qs, Qd = area(0, 4), area(2048, 4)
        Ks = area(4096, 2)
        Kd = area(5120, 4)
        Vt = area(7168, 4, 640)
        Pb = ar[:, 9728:9728 + 2048].rearrange("p (i c t) -> p i c t", i=2, c=2)
        PTb = area(11776, 2)
        rtmp = area(12800, 2)
        SQd = area(13824, 4)
        rope_tiles = [Qs[:, j, :] for j in range(4)] + [Ks[:, 0, :]] + [Qd[:, j, :] for j in range(4)] + \
                     [Kd[:, j, :] for j in range(4)]
        MG = area(0, KT)
        MO = area(4096, KT)
        SQ = area(8192, KT)
        sgb = area(12288, 2)
        mtmp = ar[:, 13312:13824]
        hid = area(8192, FT)
        hidm = area(8192, ET, SEQ)
        FA = area(8192 + ET * SEQ, KT, SEQ)
        wbc = area(8192 + ET * SEQ + KT * SEQ, 1, SEQ)
        tmm = area(8192 + ET * SEQ + KT * SEQ + SEQ, 2, SEQ)
        htmp = area(19456, 2)

        banks = [ctx.enter_context(nc.psum_tensor(f"bank{i}", [128, 512], f32))[:, :] for i in range(8)]
        A = Ring(banks[0:3], sem("a_full"), sem("a_free"))
        V_ = Ring(banks[3:6], sem("v_full"), sem("v_free"))
        S = Ring(banks[6:8], sem("s_full"), sem("s_free"))

        w_in = [sem(f"weights_in_{i}") for i in range(SLOTS)]
        consts_in = sem("consts_in")
        x_in = sem("x_in")
        spilled = sem("residual_spilled")
        reloaded = sem("residual_reloaded")
        stored = sem("stored")
        silc_ready = sem("silc_ready")
        coef_ready = sem("coef_ready")
        h_ready = sem("h_ready")
        sq_ready = sem("sq_ready")
        at_scaled = sem("at_scaled")
        at_ready = sem("at_ready")
        dve_step = sem("dve_step")
        act_step = sem("act_step")
        to_pe_a = sem("act_to_pe")
        to_pe_v = sem("vector_to_pe")
        to_act = sem("vector_to_act")
        to_dve = sem("act_to_vector")
        lam_in, lam_out = sem("exponent_ready"), sem("exponential_ready")
        to_pool = sem("vector_to_pool")
        p_ready = sem("p_ready")
        m_ready = sem("m_ready")
        es_ready = sem("es_ready")

        chunks = []

        def kxn(w, cols):
            return w.rearrange("(k p) n -> p k n", p=128)[:, :, cols]

        def chunk(*parts):
            at, res = 0, []
            for src in parts:
                n = src.shape[1] * src.shape[2]
                res.append((at, src))
                at += n
            assert at <= SLOT
            chunks.append(res)

        for l in range(2):
            wi = io["w_in"][l]
            for j in range(12):
                chunk(kxn(io["ada_w"][l], slice(512 * j, 512 * j + 512)))
            for j in range(4):
                chunk(kxn(wi, slice(C_RW + 512 * j, C_RW + min(512 * j + 512, RW_COLS))))
            small = lambda a: a.rearrange("p (o n) -> p o n", o=1)
            chunk(small(io["rwkv_w_up"][l].rearrange("d r n -> (d r) n")),
                  small(io["rwkv_a_up"][l].rearrange("d r n -> (d r) n")), small(io["rwkv_g_up"][l]))
            chunk(kxn(wi, slice(0, 512)))
            chunk(kxn(wi, slice(512, 768)))
            for j in range(3):
                chunk(kxn(wi, slice(C_DF + 512 * j, C_DF + 512 * j + 512)))
            for b, w in enumerate(("proj_swa", "proj_rwkv", "proj_diff")):
                chunk(kxn(wi, slice(C_GATE + D * b, C_GATE + D * b + 512)))
                chunk(kxn(io[w][l], slice(0, D)))
                chunk(kxn(wi, slice(C_GATE + D * b + 512, C_GATE + D * b + D)))
            for j in range(2):
                chunk(kxn(io["w_out"][l], slice(512 * j, 512 * j + 512)))
            if l == 0:
                for j in range(FT // 2):
                    c = slice(256 * j, 256 * j + 256)
                    chunk(kxn(io["ffn_w_gate"][0], c), kxn(io["ffn_w_up"][0], c))
                for j in range(KT):
                    chunk(kxn(io["ffn_w_down"][0], slice(128 * j, 128 * j + 128)))
            else:
                chunk(kxn(io["router_w"][0], slice(0, NE)))
                for e in range(NE):
                    for j in range(ET // 2):
                        c = slice(256 * j, 256 * j + 256)
                        chunk(kxn(io["moe_w_gate"][0, e], c), kxn(io["moe_w_up"][0, e], c))
                    for j in range(KT):
                        chunk(kxn(io["moe_w_down"][0, e], slice(128 * j, 128 * j + 128)))

        arrive_at = []
        total = [0] * SLOTS
        for n, parts in enumerate(chunks):
            total[n % SLOTS] += 16 * len(parts)
            arrive_at.append(total[n % SLOTS])
        released = []
        arrived = [0]

        def landed():
            return w_in[arrived[0] % SLOTS], arrive_at[arrived[0]]

        def arrive():
            arrived[0] += 1
            return WR[:, (arrived[0] - 1) % SLOTS, :]

        def release(ring):
            released.append((ring.full, ring.made))

        C0s = (0, SEQ)
        LAM = [0.8 - 0.6 * math.exp(-0.3 * l) for l in range(2)]
        hq = [(q, h) for q in range(8) for h in range(2)]

        def pair(x, q, h):
            return x[64 * h:64 * h + 64, 64 * q:64 * q + 64]

        def items(l):
            qbs = range(2 if l else 0, 4)
            return ([("s", u, qb) for u in range(8) for qb in qbs] + [("d", h, qb) for h in range(4) for qb in qbs])

        marks, pool_n = {}, [0]
        done, built = [False], set()

        def stage(name):
            if stop is not None and name == stop:
                done[0] = True
            if not done[0]:
                built.add(name)
            return not done[0]

        spill = nc.dram_tensor("residual_spill", (D, SEQ), f32, kind="Internal").ap()
        block = ctx.enter_context(nc.Block())

        @block.tensor
        def _(pe):
            seen = Seen()
            pe.wait_ge(consts_in, 64)

            def mm(o, lhsT, rhs, first, last):
                return pe.matmul(o, lhsT, rhs, start=first, stop=last)

            def ada(l):
                if l == 0:
                    pe.wait_ge(silc_ready, seen(silc_ready))
                jobs = []

                def turn(j):
                    pe.wait_ge(A.free, jobs[j])
                    bank = V_.claim()
                    pe.wait_ge(V_.free, V_.due)
                    for i in range(4):
                        last = pe.transpose(bank[:, 2 * i:2 * i + 2], rowb[0:2, j % 2, 128 * i:128 * i + 128],
                                            eye[0:2, 0:2])
                    last.then_inc(V_.full, 1)
                    V_.done(("turn", l, j))

                for j in range(12):
                    pe.wait_ge(*landed())
                    w = arrive().rearrange("p (k n) -> p k n", k=KT)
                    bank = A.claim()
                    pe.wait_ge(A.free, A.due)
                    for k in range(KT):
                        last = mm(bank[0:2, :], silc[:, k, :], w[:, k, :], k == 0, k == KT - 1)
                    last.then_inc(A.full, 1)
                    A.done()
                    release(A)
                    jobs.append(A.made)
                    if j:
                        turn(j - 1)
                turn(11)

            def squares_sum(l, n, c0, src, wait):
                bank = A.claim()
                pe.wait_ge(A.free, A.due)
                for k in range(n):
                    wait(k)
                    last = mm(bank[:, c0:T], ones, src[:, k, c0:T], k == 0, k == n - 1)
                last.then_inc(A.full, 1)
                A.done()

            def feature_major(w, n_tiles, c0, ring, tag, src=None):
                for i in range(n_tiles):
                    bank = ring.claim()
                    pe.wait_ge(ring.free, ring.due)
                    for k in range(KT):
                        last = mm(bank[:, c0:T], w[:, k, 128 * i:128 * i + 128], (AT if src is None else src)[:, k, c0:T], k == 0,
                                  k == KT - 1)
                    last.then_inc(ring.full, 1)
                    ring.done((tag, i))

            def recurrence_inputs(l):
                pe.wait_ge(at_ready, seen(at_ready, KT))
                for j in range(4):
                    n = 4 if j < 3 else 3
                    pe.wait_ge(*landed())
                    w = arrive()[:, 0:KT * 128 * n].rearrange("p (k n) -> p k n", k=KT)
                    feature_major(w, n, 0, V_, ("rw", l, j))
                    release(V_)
                pe.wait_ge(*landed())
                up = arrive()[:, 0:3 * 512].rearrange("p (i n) -> p i n", i=3)
                pe.wait_ge(to_pe_a, seen(to_pe_a))
                for d in range(2):
                    for j in range(4):
                        bank = A.claim()
                        pe.wait_ge(A.free, A.due)
                        last = mm(bank, up[64 * d:64 * d + 64, 0, 128 * j:128 * j + 128],
                                  thw[64 * d:64 * d + 64, :], True, True)
                        last.then_inc(A.full, 1)
                        A.done(("decay", l, d, j))
                pe.wait_ge(V_.free, V_.jobs[(("rw", l, 3), 1)])
                for d in range(2):
                    for j in range(4):
                        bank = A.claim()
                        pe.wait_ge(A.free, A.due)
                        last = mm(bank, up[64 * d:64 * d + 64, 1, 128 * j:128 * j + 128],
                                  adin[64 * d:64 * d + 64, :], True, True)
                        last.then_inc(A.full, 1)
                        A.done(("rate", l, d, j))
                pe.wait_ge(to_pe_a, seen(to_pe_a))
                for j in range(4):
                    bank = A.claim()
                    pe.wait_ge(A.free, A.due)
                    last = mm(bank, up[:, 2, 128 * j:128 * j + 128], sgd, True, True)
                    last.then_inc(A.full, 1)
                    A.done()
                release(A)
                for j in range(4):
                    pe.wait_ge(to_pe_v, seen(to_pe_v))
                    bank = A.claim()
                    pe.wait_ge(A.free, A.due)
                    last = mm(bank, blk, tmpT[j % 2], True, True)
                    last.then_inc(A.full, 1)
                    A.done(("kknorm", l, j))
                for j in range(4):
                    pe.wait_ge(to_pe_v, seen(to_pe_v))
                    bank = V_.claim()
                    pe.wait_ge(V_.free, V_.due)
                    last = mm(bank, blk, tmpT[2 + j % 2], True, True)
                    last.then_inc(V_.full, 1)
                    V_.done(("bonus", l, j))

            def grams(ring, lhs, rhs, name=None):
                bank = ring.claim()
                pe.wait_ge(ring.free, ring.due)
                for q, h in hq:
                    last = mm(pair(bank, q, h), pair(lhs, q, h), pair(rhs, q, h), True, True)
                last.then_inc(ring.full, 1)
                ring.done(name)

            def against_eye(ring, lhs, name=None):
                bank = ring.claim()
                pe.wait_ge(ring.free, ring.due)
                for q, h in hq:
                    last = mm(pair(bank, q, h), pair(lhs, q, h), eye[64 * h:64 * h + 64, 64 * h:64 * h + 64], True,
                              True)
                last.then_inc(ring.full, 1)
                ring.done(name)

            def recurrence_step(l, i):
                y = not (l == 1 and i < 4)
                pe.wait_ge(to_pe_v, seen(to_pe_v))
                grams(V_, tr["aa"], tr["ba"])
                grams(V_, tr["ba"], tr["aa"], ("LT", l, i))
                bank = A.claim()
                pe.wait_ge(A.free, A.due)
                for q, h in hq:
                    c = i if q < 4 else BWD[i]
                    last = mm(pair(bank, q, h), Rv[64 * h:64 * h + 64, q % 4, CH * c:CH * c + CH],
                              eye[64 * h:64 * h + 64, 64 * h:64 * h + 64], True, True)
                last.then_inc(A.full, 1)
                A.done(("vt", l, i))
                against_eye(A, tr["ba"])
                against_eye(A, tr["ka"])
                against_eye(A, tr["aa"], ("at", l, i))
                grams(V_, tr["ka"], tr["aa"], ("MT", l, i))
                if y:
                    grams(V_, tr["ba"], tr["ra"])
                    grams(V_, tr["ka"], tr["ra"], ("RKT", l, i))
                pe.wait_ge(A.free, A.jobs[("vt", l, i)])
                pe.wait_ge(V_.free, V_.jobs[("MT", l, i)])
                grams(A, tr["MT"], tr["vt"], ("MV", l, i))
                for n in range(5):
                    pe.wait_ge(to_pe_v, seen(to_pe_v))
                    grams(V_, tr["LT"], tr["X"], ("T1", l, i, n))
                    pe.wait_ge(V_.free, V_.jobs[("T1", l, i, n)])
                    if n < 4:
                        grams(V_, tr["XT"], tr["T1"])
                    grams(V_, tr["T1"], tr["XT"], ("XT", l, i, n))
                pe.wait_ge(V_.free, V_.jobs[("XT", l, i, 4)])
                pe.wait_ge(A.free, A.jobs[("MV", l, i)])
                grams(A, tr["XT"], Gm)
                grams(A, tr["at"], tr["XT"], ("W1T", l, i))
                pe.wait_ge(A.free, A.jobs[("W1T", l, i)])
                pe.wait_ge(to_pe_v, seen(to_pe_v))
                grams(V_, W1T, tr["Sr"], ("U", l, i))
                pe.wait_ge(V_.free, V_.jobs[("U", l, i)])
                bank = V_.claim()
                pe.wait_ge(V_.free, V_.due)
                for q, h in hq:
                    mm(pair(bank, q, h), pair(tr["bt"], q, h), pair(Um, q, h), True, False)
                    last = mm(pair(bank, q, h), pair(tr["kt"], q, h), pair(tr["vt"], q, h), False, True)
                last.then_inc(V_.full, 1)
                V_.done(("S", l, i))
                if y:
                    bank = V_.claim()
                    pe.wait_ge(V_.free, V_.due)
                    for q, h in hq:
                        mm(pair(bank, q, h), pair(tr["Sr"], q, h), pair(tr["ra"], q, h), True, False)
                        mm(pair(bank, q, h), pair(Um, q, h), pair(tr["RBT"], q, h), False, False)
                        last = mm(pair(bank, q, h), pair(tr["vt"], q, h), pair(tr["RKT"], q, h), False, True)
                    last.then_inc(V_.full, 1)
                    V_.done(("Y", l, i))

            def recurrence_output(l):
                c0 = C0s[l]
                for what in ("mean", "var"):
                    for j in range(4):
                        pe.wait_ge(to_pe_v, seen(to_pe_v))
                        ring = V_ if what == "mean" else A
                        bank = ring.claim()
                        pe.wait_ge(ring.free, ring.due)
                        src = YA[:, j, c0:T] if what == "mean" else tmpO[j % 2][:, c0:T]
                        last = mm(bank[:, c0:T], blk, src, True, True)
                        last.then_inc(ring.full, 1)
                        ring.done(("gn" + what, l, j))

            def rope(l, tiles):
                for n, x in enumerate(tiles):
                    bank = V_.claim()
                    pe.wait_ge(V_.free, V_.due)
                    last = mm(bank[:, 0:SEQ], perm, x[:, SEQ:T], True, True)
                    last.then_inc(V_.full, 1)
                    V_.done(("rope", l, n))

            def attention_inputs(l):
                c0 = C0s[l]
                w8 = lambda w, n: w[:, 0:KT * n].rearrange("p (k n) -> p k n", k=KT)
                pe.wait_ge(*landed())
                feature_major(w8(arrive(), 512), 4, c0, A, ("qs", l))
                release(A)
                pe.wait_ge(*landed())
                w = w8(arrive(), 256)
                feature_major(w, 1, 0, A, ("ks", l))
                bank = V_.claim()
                pe.wait_ge(V_.free, V_.due)
                for b in range(4):
                    for k in range(KT):
                        last = mm(bank[:, 128 * b:128 * b + 128], AT[:, k, 128 * b:128 * b + 128], w[:, k, 128:256],
                                  k == 0, k == KT - 1)
                last.then_inc(V_.full, 1)
                V_.done()
                release(V_)
                pe.wait_ge(*landed())
                feature_major(w8(arrive(), 512), 4, c0, A, ("qd", l))
                release(A)
                pe.wait_ge(*landed())
                feature_major(w8(arrive(), 512), 4, 0, A, ("kd", l))
                release(A)
                pe.wait_ge(*landed())
                w = w8(arrive(), 512)
                for b in range(4):
                    bank = V_.claim()
                    pe.wait_ge(V_.free, V_.due)
                    for k in range(KT):
                        last = mm(bank, AT[:, k, 128 * b:128 * b + 128], w[:, k, :], k == 0, k == KT - 1)
                    last.then_inc(V_.full, 1)
                    V_.done()
                release(V_)
                pe.wait_ge(A.free, A.jobs[(("kd", l), 3)])
                rope(l, rope_tiles)
                pe.wait_ge(V_.free, V_.jobs[("rope", l, 4)])
                bank = A.claim()
                pe.wait_ge(A.free, A.due)
                last = mm(bank, swap, Ks[:, 0, :], True, True)
                last.then_inc(A.full, 1)
                A.done(("k2", l))
                pe.wait_ge(A.free, A.jobs[("k2", l)])
                pe.wait_ge(V_.free, V_.jobs[("rope", l, 12)])

            def attention(l):
                its = items(l)

                def scores(n):
                    kind, u, qb = its[n]
                    nk = SEQ if qb < 2 else T
                    qc = slice(128 * qb, 128 * qb + 128)
                    for c in range(1 if kind == "s" else 2):
                        h = u % 2 if kind == "s" else c
                        q = Qs[:, u // 2, qc] if kind == "s" else Qd[:, u, qc]
                        k = Ks[:, 0 if u // 4 == h else 1, 0:nk] if kind == "s" else Kd[:, u, 0:nk]
                        bank = S.claim()
                        pe.wait_ge(S.free, S.due)
                        last = mm(bank[:, 0:nk], q[64 * h:64 * h + 64, :], k[64 * h:64 * h + 64, :], True, True)
                        last.then_inc(S.full, 1)
                        S.done(("sc", l, n, c))

                def turn(n):
                    kind, u, qb = its[n]
                    pe.wait_ge(p_ready, seen(p_ready))
                    bank = A.claim()
                    pe.wait_ge(A.free, A.due)
                    for b in range(2 if qb < 2 else 4):
                        last = pe.transpose(bank[:, 128 * b:128 * b + 128], Pb[:, n % 2, 0, 128 * b:128 * b + 128], eye)
                    last.then_inc(A.full, 1)
                    A.done(("pt", l, n))

                def values(n):
                    kind, u, qb = its[n]
                    pe.wait_ge(A.free, A.jobs[("pt", l, n)])
                    bank = V_.claim()
                    pe.wait_ge(V_.free, V_.due)
                    nb = 2 if qb < 2 else 4
                    for b in range(nb):
                        if kind == "s":
                            h, g = u % 2, u // 4
                            last = mm(bank[64 * h:64 * h + 64, 0:128], Vt[:, b, 64 * g:64 * g + 64],
                                      PTb[:, n % 2, 128 * b:128 * b + 128], b == 0, b == nb - 1)
                        else:
                            last = mm(bank[:, 0:128], Vt[:, b, 128 + 128 * u:256 + 128 * u],
                                      PTb[:, n % 2, 128 * b:128 * b + 128], b == 0, b == nb - 1)
                    last.then_inc(V_.full, 1)
                    V_.done(("pv", l, n))

                for n in range(len(its) + 2):
                    if n < len(its):
                        scores(n)
                    if 1 <= n <= len(its):
                        turn(n - 1)
                    if n >= 2:
                        values(n - 2)
                for j in range(4):
                    pe.wait_ge(to_pe_a, seen(to_pe_a))
                    bank = A.claim()
                    pe.wait_ge(A.free, A.due)
                    last = mm(bank[:, C0s[l]:T], ones, SQd[:, j, C0s[l]:T], True, True)
                    last.then_inc(A.full, 1)
                    A.done()

            def merge(l):
                c0 = C0s[l]
                pe.wait_ge(to_pe_v, seen(to_pe_v))
                for b, y in enumerate((YA, YB, YC)):
                    pe.wait_ge(*landed())
                    g = arrive().rearrange("p (k n) -> p k n", k=KT)
                    pe.wait_ge(*landed())
                    p = arrive().rearrange("p (k n) -> p k n", k=4)
                    for j in range(KT):
                        if j == 4:
                            release(V_)
                            pe.wait_ge(*landed())
                            g = arrive().rearrange("p (k n) -> p k n", k=KT)
                        bank = A.claim()
                        pe.wait_ge(A.free, A.due)
                        for k in range(KT):
                            last = mm(bank[:, c0:T], g[:, k, 128 * (j % 4):128 * (j % 4) + 128], AT[:, k, c0:T],
                                      k == 0, k == KT - 1)
                        last.then_inc(A.full, 1)
                        A.done()
                        bank = V_.claim()
                        pe.wait_ge(V_.free, V_.due)
                        for k in range(4):
                            last = mm(bank[:, c0:T], p[:, k, 128 * j:128 * j + 128], y[:, k, c0:T], k == 0, k == 3)
                        last.then_inc(V_.full, 1)
                        V_.done(("merge", l, b, j))
                    release(V_)
                    release(V_)
                pe.wait_ge(V_.free, V_.jobs[("merge", l, 2, KT - 1)])
                for j in range(2):
                    pe.wait_ge(*landed())
                    w = arrive().rearrange("p (k n) -> p k n", k=KT)
                    feature_major(w, 4, c0, A, ("wo", l, j), src=MG)
                    release(A)
                squares_sum(l, KT, c0, SQ, lambda k: pe.wait_ge(A.free, A.jobs[(("wo", l, k // 4), k % 4)]))

            def norm(c0):
                squares_sum(0, KT, c0, AT, lambda k: pe.wait_ge(sq_ready, seen(sq_ready)))

            def ffn(l):
                pe.wait_ge(at_ready, seen(at_ready, KT))
                for j in range(FT // 2):
                    pe.wait_ge(*landed())
                    w = arrive().rearrange("p (g k n) -> p g k n", g=2, k=KT)
                    for i in range(2):
                        for g, ring in enumerate((A, V_)):
                            bank = ring.claim()
                            pe.wait_ge(ring.free, ring.due)
                            for k in range(KT):
                                last = mm(bank, w[:, g, k, 128 * i:128 * i + 128], AT[:, k, :], k == 0, k == KT - 1)
                            last.then_inc(ring.full, 1)
                            ring.done(("hid", l, 2 * j + i))
                    release(V_)
                pe.wait_ge(V_.free, V_.jobs[("hid", l, FT - 1)])
                for j in range(KT):
                    pe.wait_ge(*landed())
                    w = arrive()[:, 0:FT * 128].rearrange("p (k n) -> p k n", k=FT)
                    bank = A.claim()
                    pe.wait_ge(A.free, A.due)
                    for k in range(FT):
                        last = mm(bank, w[:, k, :], hid[:, k, :], k == 0, k == FT - 1)
                    last.then_inc(A.full, 1)
                    A.done(("dn", l, j))
                    release(A)
                squares_sum(l, KT, 0, AT, lambda k: pe.wait_ge(A.free, A.jobs[("dn", l, k)]))

            def moe(l):
                pe.wait_ge(at_ready, seen(at_ready, KT))
                pe.wait_ge(*landed())
                w = arrive()[:, 0:KT * NE].rearrange("p (k n) -> p k n", k=KT)
                bank = V_.claim()
                pe.wait_ge(V_.free, V_.due)
                for b in range(2):
                    for k in range(KT):
                        last = mm(bank[:, NE * b:NE * b + NE], AT[:, k, SEQ + 128 * b:SEQ + 128 * b + 128], w[:, k, :],
                                  k == 0, k == KT - 1)
                last.then_inc(V_.full, 1)
                V_.done()
                release(V_)
                pe.wait_ge(to_pe_v, seen(to_pe_v))
                for e in range(NE):
                    bank = V_.claim()
                    pe.wait_ge(V_.free, V_.due)
                    for b in range(2):
                        last = mm(bank[:, 128 * b:128 * b + 128], rt[:, b, 8 + e:9 + e].to_broadcast([128, 128]), eye,
                                  True, True)
                    last.then_inc(V_.full, 1)
                    V_.done()
                    for j in range(ET // 2):
                        pe.wait_ge(*landed())
                        w = arrive().rearrange("p (g k n) -> p g k n", g=2, k=KT)
                        for i in range(2):
                            for g, ring in enumerate((A, V_)):
                                bank = ring.claim()
                                pe.wait_ge(ring.free, ring.due)
                                for k in range(KT):
                                    last = mm(bank[:, 0:SEQ], w[:, g, k, 128 * i:128 * i + 128], AT[:, k, SEQ:T],
                                              k == 0, k == KT - 1)
                                last.then_inc(ring.full, 1)
                                ring.done(("hidm", e, 2 * j + i))
                        release(V_)
                    pe.wait_ge(V_.free, V_.jobs[("hidm", e, ET - 1)])
                    for j in range(KT):
                        pe.wait_ge(*landed())
                        w = arrive()[:, 0:ET * 128].rearrange("p (k n) -> p k n", k=ET)
                        bank = V_.claim()
                        pe.wait_ge(V_.free, V_.due)
                        for k in range(ET):
                            last = mm(bank[:, 0:SEQ], w[:, k, :], hidm[:, k, :], k == 0, k == ET - 1)
                        last.then_inc(V_.full, 1)
                        V_.done(("dnm", e, j))
                        release(V_)
                bank = A.claim()
                pe.wait_ge(A.free, A.due)
                for k in range(KT):
                    pe.wait_ge(sq_ready, seen(sq_ready))
                    last = mm(bank[:, SEQ:T], ones, AT[:, k, SEQ:T], k == 0, k == KT - 1)
                last.then_inc(A.full, 1)
                A.done()

            for l in range(2):
                if stage(f"ada{l}"):
                    ada(l)
                    norm(0)
                if stage(f"rwin{l}"):
                    recurrence_inputs(l)
                if stage(f"rwstep{l}"):
                    for i in range(NCH):
                        recurrence_step(l, i)
                    recurrence_output(l)
                if stage(f"attn{l}"):
                    attention_inputs(l)
                    attention(l)
                if stage(f"merge{l}"):
                    merge(l)
                if stage(f"ffn{l}"):
                    norm(C0s[l])
                    (ffn if l == 0 else moe)(l)

        done[0] = False
        marks.clear()

        @block.scalar
        def _(act):
            seen = Seen()
            act.wait_ge(consts_in, 64)
            act.wait_ge(coef_ready, 1)
            own = {}

            def a(ins, s, wait=False):
                own[s.name] = own.get(s.name, 0) + 1
                ins.then_inc(s, 1)
                if wait:
                    act.wait_ge(s, own[s.name])

            def f(out, in_, func, **k):
                return act.activation(out, in_, func, **k)

            def free(ins, name=None):
                ins.then_inc(A.free, 1)
                if name is not None:
                    marks[name] = A.taken

            a(f(silc[:, :, :].rearrange("p k s -> p (k s)"), vec[:, 2 * VEC_L:2 * VEC_L + 16], ACT.Silu), silc_ready)

            def ada(l):
                for j in range(12):
                    bank = A.take()
                    act.wait_ge(A.full, A.taken)
                    if j >= 2:
                        act.wait_ge(V_.full, V_.jobs[("turn", l, j - 2)])
                    free(f(rowb[0:2, j % 2, :], bank[0:2, :], ACT.Copy))

            def root(c0, n, eps_col, name):
                bank = A.take()
                act.wait_ge(A.full, A.taken)
                free(f(RS[:, 0, c0:T], bank[:, c0:T], ACT.Sqrt, scale=1.0 / n, bias=cvec[:, eps_col:eps_col + 1]), name)

            def norm(l, c0, which):
                if l == 0 and which == "mix":
                    act.wait_ge(x_in, 16)
                for k in range(KT):
                    if l or which == "ffn":
                        act.wait_ge(h_ready, seen(h_ready))
                    a(f(AT[:, k, c0:T], HT[:, k, c0:T], ACT.Square), sq_ready)
                root(c0, D, 0, ("root", l, which))
                for k in range(KT):
                    for s in range(c0 // SEQ, 2):
                        act.wait_ge(at_scaled, seen(at_scaled))
                        ins = f(AT[:, k, SEQ * s:SEQ * s + SEQ], AT[:, k, SEQ * s:SEQ * s + SEQ], ACT.Identity,
                                bias=mods[:, (0 if which == "mix" else 24) + k, s:s + 1])
                    a(ins, at_ready)

            def recurrence_inputs(l):
                if l:
                    act.wait_ge(spilled, 16)
                act.wait_ge(V_.free, V_.jobs[(("rw", l, 3), 0)])
                a(f(thw, wdin, ACT.Tanh), to_pe_a)
                for d in range(2):
                    for j in range(4):
                        bank = A.take()
                        act.wait_ge(A.full, A.taken)
                        n = 4 * d + j
                        if n >= 2:
                            act.wait_ge(to_act, seen(to_act))
                        free(f(sgt[n % 2], bank[:, :], ACT.Sigmoid, bias=V(l, "w0", n)), ("sg", l, n))
                for d in range(2):
                    for j in range(4):
                        bank = A.take()
                        act.wait_ge(A.full, A.taken)
                        n = 4 * d + j
                        free(f(Ra[:, d, j, :], bank[:, :], ACT.Sigmoid, bias=V(l, "a0", n)), ("rate", l, n))
                act.wait_ge(V_.free, V_.jobs[(("rw", l, 3), 2)])
                a(f(sgd, gdin, ACT.Sigmoid), to_pe_a)
                for j in range(4):
                    bank = A.take()
                    act.wait_ge(A.full, A.taken)
                    free(f(YB[:, j, :], bank[:, :], ACT.Copy), ("g", l, j))
                act.wait_ge(to_act, seen(to_act, 2))
                for j in range(4):
                    bank = A.take()
                    act.wait_ge(A.full, A.taken)
                    if j:
                        act.wait_ge(to_act, seen(to_act))
                    free(f(RS[:, 0, :], bank[:, :], ACT.Sqrt, scale=64.0), ("kkroot", l, j))
                act.wait_ge(to_act, seen(to_act))

            def recurrence_step(l, i):
                y = not (l == 1 and i < 4)
                act.wait_ge(to_act, seen(to_act))
                for d in range(2):
                    qs = slice(4 * d, 4 * d + 4)
                    inc = slice(1, CW) if d == 0 else slice(0, CH)
                    exc = slice(0, CH) if d == 0 else slice(1, CW)
                    v = lambda x: x.rearrange("p (q w) -> p q w", q=8)[:, qs, :]
                    f(v(tr["E1"]), CC[:, qs, inc], ACT.Exp, scale=-KAPPA)
                    f(v(tr["E2"]), CC[:, qs, exc], ACT.Exp, scale=-KAPPA)
                    f(v(tr["E3"]), CC[:, qs, inc], ACT.Exp, scale=KAPPA)
                    c = i if d == 0 else BWD[i]
                    f(eS[:, 0, qs], Rc[:, d, :, c, 32], ACT.Exp, scale=-KAPPA)
                    e = CH if d == 0 else 0
                    ins = f(eS[:, 1, qs], CC[:, qs, e], ACT.Exp, scale=-KAPPA)
                a(ins, to_dve)
                for n in ("vt", "bt", "kt", "at"):
                    bank = A.take()
                    act.wait_ge(A.full, A.taken)
                    free(f(tr[n], bank[:, :], ACT.Copy))
                act.wait_ge(to_act, seen(to_act))
                bank = A.take()
                act.wait_ge(A.full, A.taken)
                free(f(Gm, bank[:, :], ACT.Copy))
                bank = A.take()
                act.wait_ge(A.full, A.taken)
                free(f(Zm, bank[:, :], ACT.Copy), ("Z", l, i))
                bank = A.take()
                act.wait_ge(A.full, A.taken)
                free(f(W1T, bank[:, :], ACT.Copy))

            def recurrence_output(l):
                c0 = C0s[l]
                for j in range(4):
                    bank = A.take()
                    act.wait_ge(A.full, A.taken)
                    if j:
                        act.wait_ge(to_act, seen(to_act))
                    free(f(RS[:, 0, c0:T], bank[:, c0:T], ACT.Sqrt, bias=cvec[:, 1:2]), ("gnroot", l, j))
                act.wait_ge(to_act, seen(to_act))

            def attention_inputs(l):
                c0 = C0s[l]
                for dst, c in [(Qs[:, j, :], c0) for j in range(4)] + [(Ks[:, 0, :], 0)] + \
                              [(Qd[:, j, :], c0) for j in range(4)] + [(Kd[:, j, :], 0) for j in range(4)]:
                    bank = A.take()
                    act.wait_ge(A.full, A.taken)
                    free(f(dst[:, c:T], bank[:, c:T], ACT.Copy))
                bank = A.take()
                act.wait_ge(A.full, A.taken)
                free(f(Ks[:, 1, :], bank[:, :], ACT.Copy))
                act.wait_ge(lam_in, seen(lam_in))
                a(f(cvec[:, 4:6], cvec[:, 4:6], ACT.Exp), lam_out)

            def attention(l):
                its = items(l)
                for n in range(len(its) + 1):
                    if n < len(its):
                        kind, u, qb = its[n]
                        nk = SEQ if qb < 2 else T
                        for c in range(1 if kind == "s" else 2):
                            bank = S.take()
                            act.wait_ge(S.full, S.taken)
                            act.wait_ge(m_ready, seen(m_ready))
                            if n >= 2:
                                act.wait_ge(A.full, A.jobs[("pt", l, n - 2)])
                            f(Pb[:, n % 2, c, 0:nk], bank[:, 0:nk], ACT.Exp, scale=HD ** -0.5,
                              bias=st[:, n % 4, c, 1:2], accum_out=st[:, n % 4, c, 2:3]).then_inc(S.free, 1)
                            marks[("exp", l, n, c)] = S.taken
                        if kind == "s":
                            a(f(st[:, n % 4, 0, 3:4], st[:, n % 4, 0, 1:2], ACT.Exp, bias=rep[:, l, u:u + 1]),
                              es_ready)
                    if n >= 1:
                        kind, u, qb = its[n - 1]
                        nk = SEQ if qb < 2 else T
                        bank = A.take()
                        act.wait_ge(A.full, A.taken)
                        if n >= 3:
                            act.wait_ge(V_.full, V_.jobs[("pv", l, n - 3)])
                        free(f(PTb[:, (n - 1) % 2, 0:nk], bank[:, 0:nk], ACT.Copy))
                c0 = C0s[l]
                for j in range(4):
                    if j == 0:
                        act.wait_ge(to_act, seen(to_act))
                    a(f(SQd[:, j, c0:T], YC[:, j, c0:T], ACT.Square), to_pe_a)
                for j in range(4):
                    bank = A.take()
                    act.wait_ge(A.full, A.taken)
                    if j:
                        act.wait_ge(to_act, seen(to_act))
                    free(f(RS[:, 0, c0:T], bank[:, c0:T], ACT.Sqrt, scale=1.0 / 128, bias=cvec[:, 2:3]),
                         ("dfroot", l, j))
                act.wait_ge(to_act, seen(to_act))

            def merge(l):
                c0 = C0s[l]
                n = 0
                for b in range(3):
                    for j in range(KT):
                        bank = A.take()
                        act.wait_ge(A.full, A.taken)
                        if n >= 2:
                            act.wait_ge(V_.free, V_.jobs[("merge", l, (n - 2) // KT, (n - 2) % KT)])
                        free(f(sgb[:, n % 2, c0:T], bank[:, c0:T], ACT.Sigmoid), ("sgb", l, n))
                        n += 1
                copies(l, c0, SQ, "mix")

            def copies(l, c0, sq, which):
                for k in range(KT):
                    bank = A.take()
                    act.wait_ge(A.full, A.taken)
                    f(MO[:, k, c0:T], bank[:, c0:T], ACT.Copy)
                    free(f(sq[:, k, c0:T], bank[:, c0:T], ACT.Square))
                root(c0, D, 0, ("postroot", l, which))

            def ffn(l):
                for n in range(FT):
                    bank = A.take()
                    act.wait_ge(A.full, A.taken)
                    if n >= 2:
                        act.wait_ge(V_.free, V_.jobs[("hid", l, n - 2)])
                    free(f(htmp[:, n % 2, :], bank[:, :], ACT.Silu), ("silu", l, n))
                copies(l, 0, AT, "ffn")

            def moe(l):
                for b in range(2):
                    act.wait_ge(lam_in, seen(lam_in))
                    a(f(rt[:, b, 27:28], rt[:, b, 26:27], ACT.Exp), lam_out)
                for e in range(NE):
                    for n in range(ET):
                        bank = A.take()
                        act.wait_ge(A.full, A.taken)
                        if n >= 2 or e:
                            m = e * ET + n - 2
                            act.wait_ge(V_.free, V_.jobs[("hidm", m // ET, m % ET)])
                        free(f(htmp[:, n % 2, 0:SEQ], bank[:, 0:SEQ], ACT.Silu), ("silum", e, n))
                act.wait_ge(to_act, seen(to_act))
                for k in range(KT):
                    a(f(AT[:, k, SEQ:T], FA[:, k, :], ACT.Square), sq_ready)
                root(SEQ, D, 0, ("postroot", l, "ffn"))

            for l in range(2):
                if stage(f"ada{l}"):
                    ada(l)
                    norm(l, 0, "mix")
                if stage(f"rwin{l}"):
                    recurrence_inputs(l)
                if stage(f"rwstep{l}"):
                    for i in range(NCH):
                        recurrence_step(l, i)
                    recurrence_output(l)
                if stage(f"attn{l}"):
                    attention_inputs(l)
                    attention(l)
                if stage(f"merge{l}"):
                    merge(l)
                if stage(f"ffn{l}"):
                    norm(l, C0s[l], "ffn")
                    (ffn if l == 0 else moe)(l)

            if done[0]:
                f(cvec[:, 30:31], cvec[:, 0:1], ACT.Copy).then_inc(act_step, 1)

        done[0] = False

        @block.vector
        def _(dve):
            seen = Seen()
            own = {}

            def v(ins, s=dve_step, wait=True):
                own[s.name] = own.get(s.name, 0) + 1
                ins.then_inc(s, 1)
                if wait:
                    dve.wait_ge(s, own[s.name])

            def vf(ins, wait=True):
                ins.then_inc(V_.free, 1)
                if wait:
                    dve.wait_ge(V_.free, V_.taken)

            TT, TS, STT = dve.tensor_tensor, dve.tensor_scalar, dve.scalar_tensor_tensor
            dve.wait_ge(consts_in, 64)
            v(dve.memset(cvec[:, 0:1], 1e-6))
            v(dve.memset(cvec[:, 1:2], 64e-5))
            if stop:
                for x in (YA, YB, YC):
                    v(dve.memset(x[:, :, :], 0.0))
            v(dve.memset(cvec[:, 2:3], 1e-5), coef_ready)
            dve.wait_ge(x_in, 16)

            def ada(l):
                for j in range(12):
                    bank = V_.take()
                    dve.wait_ge(V_.full, V_.taken)
                    vf(TT(mods[:, 4 * j:4 * j + 4, :], bank[:, 0:8].rearrange("p (i s) -> p i s", s=2),
                          V(l, "ada_b")[:, 4 * j:4 * j + 4].unsqueeze(2).to_broadcast([128, 4, 2]), ALU.add))
                for n, (m, g, add) in enumerate(((8, "pre_mix", 1.0), (16, "post_mix", 0.0), (32, "pre_ffn", 1.0),
                                                 (40, "post_ffn", 0.0))):
                    v(STT(coef[:, n, :, :], mods[:, m:m + 8, :], add,
                          V(l, g).unsqueeze(2).to_broadcast([128, 8, 2]), ALU.add, ALU.mult))

            def norm(l, c0, which):
                dve.wait_ge(A.free, marks[("root", l, which)])
                v(dve.reciprocal(RS[:, 1, c0:T], RS[:, 0, c0:T]))
                ci = 0 if which == "mix" else 2
                for k in range(KT):
                    for s in range(c0 // SEQ, 2):
                        c = slice(SEQ * s, SEQ * s + SEQ)
                        v(STT(AT[:, k, c], HT[:, k, c], coef[:, ci, k, s:s + 1], RS[:, 1, c], ALU.mult, ALU.mult),
                          at_scaled, wait=False)

            def recurrence_inputs(l):
                if l:
                    dve.wait_ge(spilled, 16)
                v(TT(muc[:, :], V(l, "mu_p"), V(l, "mu_n"), ALU.add))
                v(TS(muc[:, :], muc[:, :], -1.0, 1.0, ALU.mult, ALU.add))
                dst = [Rr[:, j, :] for j in range(4)] + [Rk[:, j, :] for j in range(4)] + \
                      [Rv[:, j, :] for j in range(4)] + [wdin, adin, gdin]
                for n in range(RT_TILES):
                    bank = V_.take()
                    dve.wait_ge(V_.full, V_.taken)
                    x = dst[n]
                    v(TS(x, bank[:, :], muc[:, n:n + 1], None, ALU.mult))
                    x2 = x.rearrange("p (s t) -> p s t", s=2)
                    b2 = bank[:, :].rearrange("p (s t) -> p s t", s=2)
                    v(STT(x2[:, :, 1:SEQ], b2[:, :, 0:SEQ - 1], V(l, "mu_p", n), x2[:, :, 1:SEQ], ALU.mult, ALU.add))
                    vf(STT(x2[:, :, 0:SEQ - 1], b2[:, :, 1:SEQ], V(l, "mu_n", n), x2[:, :, 0:SEQ - 1], ALU.mult,
                           ALU.add))
                v(dve.memset(onesw, 1.0))
                v(dve.memset(YA[:, :, :], 0.0))
                v(dve.memset(tr["S"], 0.0))
                for d in range(2):
                    v(dve.memset(Rc[:, d, :, :, 0 if d == 0 else CH], 0.0))
                for n in range(8):
                    d, j = n // 4, n % 4
                    dve.wait_ge(A.free, marks[("sg", l, n)])
                    sg = sgt[n % 2]
                    for c in range(NCH):
                        lo, hi = CH * c, CH * c + CH
                        if d == 0:
                            o, i_ = Rc[:, d, j, c, 1:CW], sg[:, lo:hi]
                        else:
                            o, i_ = Rc[:, d, j, c, CH - 1::-1], (sg[:, hi - 1:lo - 1:-1] if lo else sg[:, hi - 1::-1])
                        ins = dve.tensor_tensor_scan(o, onesw, i_, 0.0, ALU.mult, ALU.add)
                        if c < NCH - 1:
                            v(ins, wait=False)
                        else:
                            v(ins, to_act)
                for j in range(4):
                    v(TS(Rkk[:, j, :], Rk[:, j, :], V(l, "k_k", j), None, ALU.mult))
                    if j >= 2:
                        dve.wait_ge(A.full, A.jobs[("kknorm", l, j - 2)])
                    v(TT(tmpT[j % 2], Rkk[:, j, :], Rkk[:, j, :], ALU.mult), to_pe_v)
                for j in range(4):
                    dve.wait_ge(A.free, marks[("kkroot", l, j)])
                    v(TS(RS[:, 1, :], RS[:, 0, :], 1e-12, None, ALU.max), to_act)
                    v(dve.reciprocal(RS[:, 1, :], RS[:, 1, :]))
                    v(TT(Rkk[:, j, :], Rkk[:, j, :], RS[:, 1, :], ALU.mult))
                dve.wait_ge(A.free, marks[("rate", l, 7)])
                v(TS(cv2, V(l, "k_a"), -2.0, 2.0, ALU.mult, ALU.add))

                def bonus_in(j):
                    t = tmpT[2 + j % 2]
                    v(TT(t, Ra[:, 0, j, :], Ra[:, 1, j, :], ALU.add))
                    v(TS(t, t, V(l, "k_a", j), cv2[:, j:j + 1], ALU.mult, ALU.add))
                    v(TT(t, t, Rk[:, j, :], ALU.mult))
                    v(STT(t, t, V(l, "r_k", j), Rr[:, j, :], ALU.mult, ALU.mult), to_pe_v)

                def bonus_out(j):
                    bank = V_.take()
                    dve.wait_ge(V_.full, V_.taken)
                    vf(STT(YC[:, j, :], bank[:, :], 64.0, Rv[:, j, :], ALU.mult, ALU.mult))

                for j in range(5):
                    if j < 4:
                        bonus_in(j)
                    if j:
                        bonus_out(j - 1)

            def recurrence_step(l, i):
                y = not (l == 1 and i < 4)
                q3 = lambda x: x.rearrange("p (q w) -> p q w", q=8)
                d3 = lambda x: x.rearrange("p (d q w) -> p d q w", d=2, q=4)
                mk = lambda m: masks[:, m, :, :].unsqueeze(2).to_broadcast([128, 2, 4, 64])
                cs = (i, BWD[i])
                for d in range(2):
                    ins = TT(CC[:, 4 * d:4 * d + 4, :], Rc[:, d, :, cs[d], :],
                             Rc[:, d, :, cs[d], 32:33].to_broadcast([128, 4, CW]), ALU.subtract)
                    v(ins, dve_step if d == 0 else to_act)
                dve.wait_ge(to_dve, seen(to_dve))
                for d in range(2):
                    c = slice(CH * cs[d], CH * cs[d] + CH)
                    g = lambda n: q3(tr[n])[:, 4 * d:4 * d + 4, :]
                    ka = V(l, "k_a").unsqueeze(2).to_broadcast([128, 4, CH])
                    if y:
                        v(TT(g("ra"), Rr[:, :, c], g("E1"), ALU.mult), wait=False)
                    v(STT(g("aa"), Rkk[:, :, c], -1.0, g("E2"), ALU.mult, ALU.mult), wait=False)
                    v(TT(g("ba"), Rkk[:, :, c], Ra[:, d, :, c], ALU.mult), wait=False)
                    v(STT(g("ka"), Ra[:, d, :, c], -1.0, ka, ALU.add, ALU.mult))
                    v(STT(g("ka"), g("ka"), 1.0, Rk[:, :, c], ALU.add, ALU.mult), wait=False)
                    v(TT(g("ba"), g("ba"), g("E3"), ALU.mult))
                    v(TT(g("ka"), g("ka"), g("E3"), ALU.mult), dve_step if d == 0 else to_pe_v)
                v(TT(q3(tr["Sr"]), q3(tr["S"]), eS[:, 0, :].unsqueeze(2).to_broadcast([128, 8, 64]), ALU.mult))
                bank = V_.take()
                dve.wait_ge(V_.full, V_.taken)
                v(TT(d3(tr["X"]), d3(bank[:, :]), mk(M_LEVEL), ALU.mult), to_act)
                vf(TT(d3(tr["X"]), d3(tr["X"]), mk(M_EYE), ALU.add))
                bank = V_.take()
                dve.wait_ge(V_.full, V_.taken)
                v(TT(d3(tr["XT"]), d3(bank[:, :]), mk(M_PAIR_T), ALU.mult))
                v(TT(d3(tr["XT"]), d3(tr["XT"]), mk(M_EYE), ALU.add), wait=False)
                vf(TT(d3(tr["LT"]), d3(bank[:, :]), mk(M_STRICT_T), ALU.mult))
                bank = V_.take()
                dve.wait_ge(V_.full, V_.taken)
                vf(TT(d3(tr["MT"]), d3(bank[:, :]), mk(M_STRICT_T), ALU.mult), wait=False)
                if y:
                    for n in ("RBT", "RKT"):
                        bank = V_.take()
                        dve.wait_ge(V_.full, V_.taken)
                        vf(TT(d3(tr[n]), d3(bank[:, :]), mk(M_INCL_T), ALU.mult), wait=False)
                v(dve.memset(cvec[:, 3:4], 0.0), to_pe_v)
                for n in range(5):
                    bank = V_.take()
                    dve.wait_ge(V_.full, V_.taken)
                    vf(TT(d3(tr["T1"]), d3(bank[:, :]), mk(M_LEVEL + 1 + n), ALU.mult))
                    if n < 4:
                        bank = V_.take()
                        dve.wait_ge(V_.full, V_.taken)
                        vf(TT(tr["X"], bank[:, :], tr["X"], ALU.add), wait=False)
                    bank = V_.take()
                    dve.wait_ge(V_.full, V_.taken)
                    vf(TT(tr["XT"], bank[:, :], tr["XT"], ALU.add))
                    v(dve.memset(cvec[:, 3:4], 0.0), to_pe_v)
                dve.wait_ge(A.free, marks[("Z", l, i)])
                bank = V_.take()
                dve.wait_ge(V_.full, V_.taken)
                vf(TT(Um, bank[:, :], Zm, ALU.add))
                bank = V_.take()
                dve.wait_ge(V_.full, V_.taken)
                vf(TT(tr["S"], bank[:, :], tr["Sr"], ALU.add))
                v(TT(q3(tr["S"]), q3(tr["S"]), eS[:, 1, :].unsqueeze(2).to_broadcast([128, 8, 64]), ALU.mult))
                if y:
                    bank = V_.take()
                    dve.wait_ge(V_.full, V_.taken)
                    for d in range(2):
                        c = slice(CH * cs[d], CH * cs[d] + CH)
                        ins = TT(YA[:, :, c], q3(bank[:, :])[:, 4 * d:4 * d + 4, :], YA[:, :, c], ALU.add)
                        if d == 0:
                            v(ins)
                        else:
                            vf(ins)

            def recurrence_output(l):
                c0 = C0s[l]
                v(dve.memset(cvec[:, 3:4], 0.0), to_pool)
                for j in range(4):
                    v(dve.memset(cvec[:, 3:4], 0.0), to_pe_v)
                for j in range(4):
                    bank = V_.take()
                    dve.wait_ge(V_.full, V_.taken)
                    vf(TT(YA[:, j, c0:T], YA[:, j, c0:T], bank[:, c0:T], ALU.subtract))
                for j in range(4):
                    if j >= 2:
                        dve.wait_ge(A.full, A.jobs[("gnvar", l, j - 2)])
                    v(TT(tmpO[j % 2][:, c0:T], YA[:, j, c0:T], YA[:, j, c0:T], ALU.mult), to_pe_v)
                dve.wait_ge(A.free, marks[("g", l, 3)])
                for j in range(4):
                    y = YA[:, j, c0:T]
                    dve.wait_ge(A.free, marks[("gnroot", l, j)])
                    v(dve.reciprocal(RS[:, 1, c0:T], RS[:, 0, c0:T]), to_act)
                    v(TT(y, y, RS[:, 1, c0:T], ALU.mult))
                    v(TS(y, y, V(l, "ln_g", j), V(l, "ln_b", j), ALU.mult, ALU.add))
                    v(TT(y, y, YC[:, j, c0:T], ALU.add))
                    v(TT(YB[:, j, c0:T], y, YB[:, j, c0:T], ALU.mult))

            def attention_inputs(l):
                bank = V_.take()
                dve.wait_ge(V_.full, V_.taken)
                vf(dve.tensor_copy(Vt[:, :, 0:128], bank[:, :].rearrange("p (b n) -> p b n", b=4)), wait=False)
                for b in range(4):
                    bank = V_.take()
                    dve.wait_ge(V_.full, V_.taken)
                    vf(dve.tensor_copy(Vt[:, b, 128:640], bank[:, :]), wait=False)
                cs, sn = tb("cos"), tb("sin")
                for n, x in enumerate(rope_tiles):
                    bank = V_.take()
                    dve.wait_ge(V_.full, V_.taken)
                    v(TT(rtmp[:, 0, 0:SEQ], bank[:, 0:SEQ], sn, ALU.mult))
                    v(TT(x[:, SEQ:T], x[:, SEQ:T], cs, ALU.mult))
                    vf(TT(x[:, SEQ:T], x[:, SEQ:T], rtmp[:, 0, 0:SEQ], ALU.add))
                lv = rep[:, l, 8:264].rearrange("p (i n) -> p i n", i=4)
                for i in range(2):
                    v(TT(rtmp[:, 1, 0:64], lv[:, 2 * i, :], lv[:, 2 * i + 1, :], ALU.mult))
                    v(dve.tensor_reduce(cvec[:, 4 + i:5 + i], rtmp[:, 1, 0:64], AX.X, ALU.add))
                v(TS(sink8, rep[:, l, 0:8], HD ** 0.5, None, ALU.mult))
                v(TS(cvec[:, 7:8], V(l, "subln", 0), 1.0 - LAM[l], None, ALU.mult), lam_in)

            def attention(l):
                its = items(l)
                dve.wait_ge(lam_out, seen(lam_out))
                v(STT(cvec[:, 6:7], cvec[:, 4:5], LAM[l], cvec[:, 5:6], ALU.add, ALU.subtract))

                def maxima(n):
                    kind, u, qb = its[n]
                    nk = SEQ if qb < 2 else T
                    for c in range(1 if kind == "s" else 2):
                        dve.wait_ge(S.full, S.jobs[("sc", l, n, c)])
                        bank = S.banks[(S.jobs[("sc", l, n, c)] - 1) % 2]
                        if kind == "s" and qb >= 2:
                            k0 = 384 if qb == 2 else 256
                            w = slice(k0, k0 + 128)
                            b0 = 0 if qb == 2 else 128
                            v(TT(bank[:, w], bank[:, w], tb("band")[:, b0:b0 + 128], ALU.add))
                        m = st[:, n % 4, c, 0:1]
                        v(dve.tensor_reduce(m, bank[:, 0:nk], AX.X, ALU.max))
                        if kind == "s":
                            v(TT(m, m, sink8[:, u:u + 1], ALU.max))
                        v(TS(st[:, n % 4, c, 1:2], m, -(HD ** -0.5), None, ALU.mult), m_ready)

                def normalise(n):
                    kind, u, qb = its[n]
                    nk = SEQ if qb < 2 else T
                    s0, s1 = st[:, n % 4, 0, :], st[:, n % 4, 1, :]
                    p0, p1 = Pb[:, n % 2, 0, 0:nk], Pb[:, n % 2, 1, 0:nk]
                    dve.wait_ge(S.free, marks[("exp", l, n, 0 if kind == "s" else 1)])
                    if kind == "s":
                        dve.wait_ge(es_ready, seen(es_ready))
                        v(TT(s0[:, 2:3], s0[:, 2:3], s0[:, 3:4], ALU.add))
                        v(dve.reciprocal(s0[:, 3:4], s0[:, 2:3]))
                        v(TS(p0, p0, s0[:, 3:4], None, ALU.mult), p_ready)
                    else:
                        v(dve.reciprocal(s0[:, 3:4], s0[:, 2:3]), wait=False)
                        v(dve.reciprocal(s1[:, 3:4], s1[:, 2:3]))
                        v(TS(p1, p1, s1[:, 3:4], cvec[:, 6:7], ALU.mult, ALU.mult))
                        v(STT(p0, p0, s0[:, 3:4], p1, ALU.mult, ALU.subtract), p_ready)

                def empty(n):
                    kind, u, qb = its[n]
                    bank = V_.take()
                    dve.wait_ge(V_.full, V_.taken)
                    qc = slice(128 * qb, 128 * qb + 128)
                    if kind == "s":
                        h = u % 2
                        ins = dve.tensor_copy(YA[64 * h:64 * h + 64, u // 2, qc], bank[64 * h:64 * h + 64, 0:128])
                    else:
                        ins = dve.tensor_copy(YC[:, u, qc], bank[:, 0:128])
                    vf(ins, wait=False)

                for n in range(len(its) + 3):
                    if n < len(its):
                        maxima(n)
                    if 1 <= n <= len(its):
                        normalise(n - 1)
                    if n >= 3:
                        empty(n - 3)
                c0 = C0s[l]
                dve.wait_ge(V_.free, V_.taken)
                v(dve.memset(cvec[:, 3:4], 0.0), to_act)
                for j in range(4):
                    dve.wait_ge(A.free, marks[("dfroot", l, j)])
                    v(dve.reciprocal(RS[:, 1, c0:T], RS[:, 0, c0:T]), to_act)
                    ins = STT(YC[:, j, c0:T], YC[:, j, c0:T], cvec[:, 7:8], RS[:, 1, c0:T], ALU.mult, ALU.mult)
                    v(ins, dve_step if j < 3 else to_pe_v)

            def merge(l):
                c0 = C0s[l]
                n = 0
                for b in range(3):
                    for j in range(KT):
                        dve.wait_ge(A.free, marks[("sgb", l, n)])
                        bank = V_.take()
                        dve.wait_ge(V_.full, V_.taken)
                        if b == 0:
                            vf(TT(MG[:, j, c0:T], sgb[:, n % 2, c0:T], bank[:, c0:T], ALU.mult))
                        else:
                            v(TT(mtmp[:, c0:T], sgb[:, n % 2, c0:T], bank[:, c0:T], ALU.mult))
                            vf(TT(MG[:, j, c0:T], MG[:, j, c0:T], mtmp[:, c0:T], ALU.add))
                        n += 1
                dve.wait_ge(reloaded, 16 * (l + 1))
                post(l, c0, "mix", lambda k, c: MO[:, k, c])

            def post(l, c0, which, src):
                dve.wait_ge(A.free, marks[("postroot", l, which)])
                v(dve.reciprocal(RS[:, 1, c0:T], RS[:, 0, c0:T]))
                ci = 1 if which == "mix" else 3
                for k in range(KT):
                    for s in range(c0 // SEQ, 2):
                        c = slice(SEQ * s, SEQ * s + SEQ)
                        x = src(k, c)
                        v(STT(x, x, coef[:, ci, k, s:s + 1], RS[:, 1, c], ALU.mult, ALU.mult))
                        v(TT(HT[:, k, c], HT[:, k, c], x, ALU.add), dve_step if s == 0 else h_ready)

            def ffn(l):
                for n in range(FT):
                    dve.wait_ge(A.free, marks[("silu", l, n)])
                    bank = V_.take()
                    dve.wait_ge(V_.full, V_.taken)
                    vf(TT(hid[:, n, :], htmp[:, n % 2, :], bank[:, :], ALU.mult), wait=False)
                post(l, 0, "ffn", lambda k, c: MO[:, k, c])

            def moe(l):
                bank = V_.take()
                dve.wait_ge(V_.full, V_.taken)
                for b in range(2):
                    r = rt[:, b, :]
                    ins = dve.tensor_copy(r[:, 0:8], bank[:, NE * b:NE * b + NE])
                    if b == 0:
                        v(ins)
                    else:
                        vf(ins)
                for b in range(2):
                    r = rt[:, b, :]
                    v(dve.max(r[:, 16:24], r[:, 0:8]))
                    v(dve.max_index(rti[:, b, :], r[:, 16:24], r[:, 0:8]))
                    v(dve.tensor_copy(r[:, 24:26], rti[:, b, 0:2]))
                    v(TT(r[:, 26:27], r[:, 17:18], r[:, 16:17], ALU.subtract), lam_in)
                    dve.wait_ge(lam_out, seen(lam_out))
                    v(TS(r[:, 28:29], r[:, 27:28], 1.0, None, ALU.add))
                    v(dve.reciprocal(r[:, 29:30], r[:, 28:29]))
                    v(TT(r[:, 30:31], r[:, 29:30], r[:, 27:28], ALU.mult))
                    v(TS(r[:, 32:40], tb("iota")[:, 0:8], r[:, 24:25], r[:, 29:30], ALU.is_equal, ALU.mult))
                    v(TS(r[:, 40:48], tb("iota")[:, 0:8], r[:, 25:26], r[:, 30:31], ALU.is_equal, ALU.mult))
                    v(TT(r[:, 8:16], r[:, 32:40], r[:, 40:48], ALU.add), dve_step if b == 0 else to_pe_v)
                for e in range(NE):
                    bank = V_.take()
                    dve.wait_ge(V_.full, V_.taken)
                    vf(dve.tensor_copy(wbc[:, 0, :], bank[:, 0:SEQ]))
                    for n in range(ET):
                        dve.wait_ge(A.free, marks[("silum", e, n)])
                        bank = V_.take()
                        dve.wait_ge(V_.full, V_.taken)
                        vf(TT(hidm[:, n, :], htmp[:, n % 2, 0:SEQ], bank[:, 0:SEQ], ALU.mult), wait=False)
                    for j in range(KT):
                        bank = V_.take()
                        dve.wait_ge(V_.full, V_.taken)
                        if e == 0:
                            vf(TT(FA[:, j, :], wbc[:, 0, :], bank[:, 0:SEQ], ALU.mult))
                        else:
                            v(TT(tmm[:, 0, :], wbc[:, 0, :], bank[:, 0:SEQ], ALU.mult))
                            vf(TT(FA[:, j, :], FA[:, j, :], tmm[:, 0, :], ALU.add))
                v(dve.memset(cvec[:, 3:4], 0.0), to_act)
                post(l, SEQ, "ffn", lambda k, c: FA[:, k, :])

            for l in range(2):
                if stage(f"ada{l}"):
                    ada(l)
                    norm(l, 0, "mix")
                if stage(f"rwin{l}"):
                    recurrence_inputs(l)
                if stage(f"rwstep{l}"):
                    for i in range(NCH):
                        recurrence_step(l, i)
                    recurrence_output(l)
                if stage(f"attn{l}"):
                    attention_inputs(l)
                    attention(l)
                if stage(f"merge{l}"):
                    merge(l)
                if stage(f"ffn{l}"):
                    norm(l, C0s[l], "ffn")
                    (ffn if l == 0 else moe)(l)
            v(dve.memset(cvec[:, 3:4], 0.0), to_pool)
            pool_n[0] = own[to_pool.name]

        @block.gpsimd
        def _(pool):
            pool.dma_start(tab[:, :], io["tables"]).then_inc(consts_in, 16)
            pool.dma_start(vec[:, :], io["vectors"]).then_inc(consts_in, 16)
            pool.dma_start(rep[:, :, :], io["repeated"]).then_inc(consts_in, 32)
            xt = io["xt"].rearrange("(k p) t -> p k t", p=128)
            pool.dma_start(HT[:, :, :], xt).then_inc(x_in, 16)
            if "rwstep0" in built:
                pool.wait_ge(to_pool, 1)
                pool.dma_start(HT[:, :, :], xt).then_inc(reloaded, 16)
            if "rwin1" in built:
                pool.wait_ge(h_ready, 2 * KT)
                pool.dma_start(spill.rearrange("(k p) t -> p k t", p=128), HT[:, :, SEQ:T]).then_inc(spilled, 16)
            if "rwstep1" in built:
                pool.wait_ge(spilled, 16)
                pool.wait_ge(to_pool, 2)
                pool.dma_start(HT[:, :, SEQ:T], spill.rearrange("(k p) t -> p k t", p=128)).then_inc(reloaded, 16)
            if done[0]:
                pool.wait_ge(to_pool, pool_n[0])
                pool.wait_ge(act_step, 1)
                env = dict(HT=HT, AT=AT, YA=YA, YB=YB, YC=YC, ar=ar, mods=mods, coef=coef, cvec=cvec)
                for name, dst in (dbg or {}).items():
                    pool.dma_start(dst, env[name][:, :, :]).then_inc(stored, 16)
                pool.wait_ge(stored, 16 * len(dbg or {}))
                return
            pool.wait_ge(h_ready, 4 * KT)
            pool.dma_start(out.rearrange("(k p) t -> p k t", p=128), HT[:, :, SEQ:T]).then_inc(stored, 16)
            pool.wait_ge(stored, 16)

        @block.sync
        def _(sp):
            for n, parts in enumerate(chunks[:arrived[0]]):
                if n >= SLOTS:
                    s, value = released[n - SLOTS]
                    sp.wait_ge(s, value)
                for at, src in parts:
                    size = src.shape[1] * src.shape[2]
                    dst = WR[:, n % SLOTS, at:at + size].rearrange("p (k n) -> p k n", k=src.shape[1])
                    sp.dma_start(dst, src).then_inc(w_in[n % SLOTS], 16)


NAMES = ["w_in", "ada_w", "rwkv_w_up", "rwkv_a_up", "rwkv_g_up", "proj_swa", "proj_rwkv", "proj_diff", "w_out",
         "ffn_w_gate", "ffn_w_up", "ffn_w_down", "router_w", "moe_w_gate", "moe_w_up", "moe_w_down"]


def layout(inputs):
    a = {n: np.ascontiguousarray(inputs[n]) for n in NAMES}
    f = np.float32
    cols = lambda x: np.asarray(x, f).reshape(-1, 128).T
    vs = []
    for l in range(2):
        for n in ("pre_mix_g", "post_mix_g", "pre_ffn_g", "post_ffn_g", "ada_b", "rwkv_mu_prev", "rwkv_mu_next",
                  "rwkv_w0", "rwkv_a0", "rwkv_k_k", "rwkv_k_a", "rwkv_r_k", "rwkv_lnx_g", "rwkv_lnx_b",
                  "diff_subln_g"):
            vs.append(cols(inputs[n][l]))
    cc = np.stack([cols(inputs["c_ctx"]), cols(inputs["c"])], 2).reshape(128, 16)
    a["vectors"] = np.ascontiguousarray(np.concatenate(vs + [cc], 1))
    rep = np.concatenate([np.asarray(inputs["swa_sink"], f), np.asarray(inputs["diff_lambda"], f).reshape(2, 256)], 1)
    a["repeated"] = np.ascontiguousarray(np.broadcast_to(rep[None], (128, 2, 264)))
    a["xt"] = np.ascontiguousarray(np.concatenate([np.asarray(inputs["ctx"][0]).T, np.asarray(inputs["x"][0]).T], 1))
    a["tables"] = tables()
    return a


def kernel(**inputs):
    import concourse.bacc as bacc
    from concourse.bass_utils import run_bass_kernel_spmd

    nc = bacc.Bacc("TRN2", target_bir_lowering=False, num_devices=1)
    arrays = layout(inputs)
    io = {n: nc.dram_tensor("in_" + n, a.shape, mybir.dt.float32, kind="ExternalInput").ap() for n, a in arrays.items()}
    out = nc.dram_tensor("result", (D, SEQ), mybir.dt.float32, kind="ExternalOutput").ap()
    trunk(nc, io, out)
    r = run_bass_kernel_spmd(nc, [{"in_" + n: a for n, a in arrays.items()}], core_ids=[0])
    return np.ascontiguousarray(r.results[0]["result"].T)[None]
```

```python
import math
from contextlib import ExitStack

import numpy as np

import concourse.bass as bass
from concourse import mybir

D = 1024
T = 512
SEQ = 256
KT = D // 128
HD = 64
CH = 64
NCH = T // CH
FF = 2816
FT = FF // 128
EF = 3584
ET = EF // 128
NE = 8
SW_COLS, RW_COLS, DF_COLS = 768, 1920, 1536
C_RW = SW_COLS
C_DF = SW_COLS + RW_COLS
C_GATE = C_DF + DF_COLS
RT_TILES = RW_COLS // 128
KAPPA = math.exp(-0.5)
BWD = [3, 2, 1, 0, 7, 6, 5, 4]
NEG = -1e30

VEC = {}
_at = 0
for _n, _w in [("pre_mix", 8), ("post_mix", 8), ("pre_ffn", 8), ("post_ffn", 8), ("ada_b", 48), ("mu_p", 15),
               ("mu_n", 15), ("w0", 8), ("a0", 8), ("k_k", 4), ("k_a", 4), ("r_k", 4), ("ln_g", 4), ("ln_b", 4),
               ("subln", 1)]:
    VEC[_n] = (_at, _w)
    _at += _w
VEC_L = _at


def tables():
    f = np.float32
    n = np.arange(SEQ)
    row, col = (n // 64).astype(f), (n % 64).astype(f)
    inv = (np.float32(10000.0) ** (-np.arange(0, 32, 2, dtype=f) / f(32))).astype(f)
    cosT, sinT = np.zeros((128, SEQ), f), np.zeros((128, SEQ), f)
    perm, swap = np.zeros((128, 128), f), np.zeros((128, 128), f)
    for p in range(128):
        q = p % 64
        axis, half, i = q // 32, (q % 32) // 16, q % 16
        ang = ((row if axis == 0 else col) * inv[i]).astype(f)
        cosT[p], sinT[p] = np.cos(ang), np.sin(ang)
        if half == 0:
            perm[p + 16, p] = -1.0
        else:
            perm[p - 16, p] = 1.0
        swap[(p + 64) % 128, p] = 1.0
    eye = np.eye(128, dtype=f)
    blk = np.kron(np.eye(2), np.full((64, 64), 1 / 64)).astype(f)
    r, c = np.arange(128)[:, None], np.arange(128)[None, :]
    band = np.concatenate([np.where(c <= r, 0, NEG), np.where(c >= r, 0, NEG)], 1).astype(f)
    r, c = (np.arange(128) % 64)[:, None], np.arange(64)[None, :]
    later = [lambda a, b: a > b, lambda a, b: a < b]
    two = lambda g: np.stack([g(0), g(1)], 1).astype(f)
    masks = [two(lambda d: later[d](c, r)), two(lambda d: later[d](c, r) | (c == r))]
    for m in (1, 2, 4, 8, 16, 32):
        masks.append(two(lambda d: (r // (2 * m) == c // (2 * m)) & (r // m != c // m) & later[d](r, c)))
    masks.append(two(lambda d: (r // 2 == c // 2) & later[d](c, r)))
    masks.append(two(lambda d: (r == c)))
    masks = np.stack(masks, 1).reshape(128, -1)
    return np.concatenate([eye, perm, swap, blk, np.ones((128, 128), f), cosT, sinT, band, masks,
                           np.broadcast_to(np.arange(128, dtype=f), (128, 128)),
                           np.triu(np.ones((128, 128), f), 1)], 1)


TAB = {}
_at = 0
for _n, _w in [("eye", 128), ("perm", 128), ("swap", 128), ("blk", 128), ("ones", 128), ("cos", 256), ("sin", 256),
               ("band", 256), ("masks", 10 * 128), ("iota", 128),
               ("tri", 128)]:
    TAB[_n] = (_at, _w)
    _at += _w
TAB_W = _at
M_STRICT_T, M_INCL_T, M_LEVEL, M_PAIR_T, M_EYE = 0, 1, 2, 8, 9


class Ring:

    def __init__(self, banks, full, free):
        self.banks, self.full, self.free = banks, full, free
        self.made = self.taken = self.due = 0
        self.jobs = {}
        self.starts = {}

    def start(self, name):
        self.starts[name] = self.made

    def begin(self, name):
        self.taken = self.starts[name]

    def claim(self):
        self.due = max(0, self.made - len(self.banks) + 1)
        return self.banks[self.made % len(self.banks)]

    def done(self, name=None):
        self.made += 1
        self.jobs[name] = self.made

    def take(self):
        self.taken += 1
        return self.banks[(self.taken - 1) % len(self.banks)]


class Stream:

    def __init__(self, chunks, sems, slots):
        self.chunks, self.sems, self.slots = chunks, sems, slots
        self.in_count = []
        total = [0] * len(sems)
        for n, parts in enumerate(chunks):
            total[n % len(sems)] += 16 * len(parts)
            self.in_count.append(total[n % len(sems)])
        self.arrived = 0
        self.released = []

    def landed(self):
        return self.sems[self.arrived % len(self.sems)], self.in_count[self.arrived]

    def arrive(self):
        self.arrived += 1
        return self.slots[:, (self.arrived - 1) % len(self.sems), :]

    def release(self, ring):
        self.released.append((ring.full, ring.made))


class Seen:

    def __init__(self):
        self.n = {}

    def __call__(self, sem, k=1):
        self.n[sem.name] = self.n.get(sem.name, 0) + k
        return self.n[sem.name]


def trunk(nc, io, out, dbg=None, stop=None):
    f32 = mybir.dt.float32
    u32 = mybir.dt.uint32
    ALU = mybir.AluOpType
    ACT = mybir.ActivationFunctionType
    AX = mybir.AxisListType

    ctx = ExitStack()
    with ctx:
        def sb(name, shape, dt=f32):
            return ctx.enter_context(nc.sbuf_tensor(name, shape, dt))

        def sem(name):
            return ctx.enter_context(nc.semaphore(name))

        HT = sb("HT", [128, KT, T])
        AT = sb("AT", [128, KT, T])
        SLOTS, SLOT = 3, 4096
        WR = sb("WR", [128, SLOTS, SLOT])
        YA = sb("YA", [128, 4, T])
        YB = sb("YB", [128, 4, T])
        YC = sb("YC", [128, 4, T])
        tab = sb("tab", [128, TAB_W])
        vec = sb("vec", [128, 2 * VEC_L + 16])
        rep = sb("rep", [128, 2, 8 + 256])
        mods = sb("mods", [128, 48, 2])
        coef = sb("coef", [128, 4, KT, 2])
        silc = sb("silc", [128, KT, 2])
        muc = sb("muc", [128, RT_TILES])
        cvec = sb("cvec", [128, 32])
        sink8, cv2 = cvec[:, 8:16], cvec[:, 16:20]
        st = sb("st", [128, 4, 2, 4])
        RS = sb("RS", [128, 2, T])
        eS = sb("eS", [128, 2, 2, 8])
        rt = sb("rt", [128, 2, 64])
        rti = sb("rti", [128, 2, 8], u32)
        flag = sb("flag", [1, 1], mybir.dt.int32)
        AR_W = 21100
        ar = sb("ar", [128, AR_W])

        def V(l, name, i=None):
            a, w = VEC[name]
            a += l * VEC_L
            return vec[:, a:a + w] if i is None else vec[:, a + i:a + i + 1]

        def tb(name):
            a, w = TAB[name]
            return tab[:, a:a + w]

        eye, perm, swap, blk, ones = tb("eye"), tb("perm"), tb("swap"), tb("blk"), tb("ones")
        masks = tb("masks").rearrange("p (m d c) -> p m d c", m=10, d=2)

        def area(at, n, w=T):
            return ar[:, at:at + n * w].rearrange("p (n w) -> p n w", n=n)

        Rr, Rk, Rv, Rkk = area(0, 4), area(2048, 4), area(4096, 4), area(6144, 4)
        Ra = ar[:, 8192:12288].rearrange("p (d j t) -> p d j t", d=2, j=4)
        CW = CH + 1
        Rc = ar[:, 12288:12288 + 2 * 4 * NCH * CW].rearrange("p (d j c w) -> p d j c w", d=2, j=4, c=NCH)
        TR0 = 12288 + 2 * 4 * NCH * CW
        HTf = HT[:, :, :].rearrange("p k t -> p (k t)")
        ATf = AT[:, :, :].rearrange("p k t -> p (k t)")
        names = ["E10", "E20", "E30", "ba0", "ka0", "LT", "X", "XT"]
        tr = {n: HTf[:, i * 512:i * 512 + 512] for i, n in enumerate(names)}
        names = ["E11", "E21", "E31", "ba1", "ka1", "G", "U"]
        tr.update({n: ATf[:, i * 512:i * 512 + 512] for i, n in enumerate(names)})
        names = ["MT", "RBT", "RKT", "bt", "kt", "sq", "vt", "S"]
        tr.update({n: ar[:, TR0 + i * 512:TR0 + i * 512 + 512] for i, n in enumerate(names)})
        tr.update({"T1": RS[:, 0, :], "Sr": RS[:, 1, :]})
        for i in "01":
            tr["ra" + i], tr["aa" + i] = tr["E1" + i], tr["E2" + i]
        CC = ar[:, TR0 + 8 * 512:TR0 + 8 * 512 + 8 * CW].rearrange("p (q w) -> p q w", q=8)
        assert TR0 + 8 * 512 + 8 * CW <= AR_W
        tmpT = [tr[n] for n in ("ba0", "ka0", "X", "XT", "MT", "RBT", "RKT", "bt", "kt")]
        tmpO = [tr["MT"], tr["RBT"]]
        thw, wdin, adin, gdin, sgd = tmpT[4:9]
        sgt = [tr["E10"], tr["E20"]]
        onesw = tr["E30"][:, 0:CH]
        rowb = area(0, 2)
        Qs, Qd = area(0, 4), area(2048, 4)
        Ks = area(4096, 2)
        Kd = area(5120, 4)
        Vt = area(7168, 4, 640)
        Pb = ar[:, 9728:9728 + 2048].rearrange("p (i c t) -> p i c t", i=2, c=2)
        PTb = area(11776, 2)
        rtmp = area(12800, 2)
        SQd = area(13824, 4)
        rope_tiles = [Qs[:, j, :] for j in range(4)] + [Ks[:, 0, :]] + [Qd[:, j, :] for j in range(4)] + \
                     [Kd[:, j, :] for j in range(4)]
        MG = area(0, KT)
        MO = area(4096, KT)
        SQ = area(8192, KT)
        sgb = area(12288, 2)
        mtmp = ar[:, 13312:13824]
        hid = area(8192, FT)
        CAP = 128
        hidm = area(8192, ET, CAP)
        FA = area(11776, KT, SEQ)
        Atok = area(13824, 2, D)
        XE = ar[:, 15872:17920].rearrange("p (i k t) -> p i k t", i=2, k=KT)
        Psel = ar[:, 17920:18432].rearrange("p (i b t) -> p i b t", i=2, b=2)
        Pw = area(18432, 2, CAP)
        PwT = area(18688, 2, SEQ)
        htm = area(19200, 2, 256)
        Ysb = ar[:, 19712:20736]
        htmp = area(19456, 2)

        banks = [ctx.enter_context(nc.psum_tensor(f"bank{i}", [128, 512], f32))[:, :] for i in range(8)]
        A = Ring(banks[0:3], sem("a_full"), sem("a_free"))
        V_ = Ring(banks[3:6], sem("v_full"), sem("v_free"))
        S = Ring(banks[6:8], sem("s_full"), sem("s_free"))

        A2 = Ring(banks[0:3], sem("a2_full"), sem("a2_free"))
        V2 = Ring(banks[3:6], sem("v2_full"), sem("v2_free"))
        S2 = Ring(banks[6:8], sem("s2_full"), sem("s2_free"))

        flag_ready = sem("flag_ready")
        dve_step2 = sem("dve_step2")
        down_step = [sem("down_step_0"), sem("down_step_1")]
        w_in = [sem(f"weights_in_{i}") for i in range(SLOTS)]
        consts_in = sem("consts_in")
        x_in = sem("x_in")
        spilled = sem("residual_spilled")
        reloaded = sem("residual_reloaded")
        at_spilled, at_reloaded = sem("input_spilled"), sem("input_reloaded")
        stored = sem("stored")
        silc_ready = sem("silc_ready")
        coef_ready = sem("coef_ready")
        h_ready = sem("h_ready")
        sq_ready = sem("sq_ready")
        at_scaled = sem("at_scaled")
        at_ready = sem("at_ready")
        dve_step = sem("dve_step")
        act_step = sem("act_step")
        to_pe_a = sem("act_to_pe")
        to_pe_v = sem("vector_to_pe")
        to_act = sem("vector_to_act")
        to_dve = sem("act_to_vector")
        lam_in, lam_out = sem("exponent_ready"), sem("exponential_ready")
        to_pool = sem("vector_to_pool")
        p_ready = sem("p_ready")
        m_ready = sem("m_ready")
        es_ready = sem("es_ready")

        chunks = []

        def kxn(w, cols):
            return w.rearrange("(k p) n -> p k n", p=128)[:, :, cols]

        def chunk(*parts):
            at, res = 0, []
            for src in parts:
                n = src.shape[1] * src.shape[2]
                res.append((at, src))
                at += n
            assert at <= SLOT
            chunks.append(res)

        for l in range(2):
            wi = io["w_in"][l]
            for j in range(12):
                chunk(kxn(io["ada_w"][l], slice(512 * j, 512 * j + 512)))
            for j in range(4):
                chunk(kxn(wi, slice(C_RW + 512 * j, C_RW + min(512 * j + 512, RW_COLS))))
            small = lambda a: a.rearrange("p (o n) -> p o n", o=1)
            chunk(small(io["rwkv_w_up"][l].rearrange("d r n -> (d r) n")),
                  small(io["rwkv_a_up"][l].rearrange("d r n -> (d r) n")), small(io["rwkv_g_up"][l]))
            chunk(kxn(wi, slice(0, 512)))
            chunk(kxn(wi, slice(512, 768)))
            for j in range(3):
                chunk(kxn(wi, slice(C_DF + 512 * j, C_DF + 512 * j + 512)))
            for b, w in enumerate(("proj_swa", "proj_rwkv", "proj_diff")):
                chunk(kxn(wi, slice(C_GATE + D * b, C_GATE + D * b + 512)))
                chunk(kxn(io[w][l], slice(0, D)))
                chunk(kxn(wi, slice(C_GATE + D * b + 512, C_GATE + D * b + D)))
            for j in range(2):
                chunk(kxn(io["w_out"][l], slice(512 * j, 512 * j + 512)))
            if l == 0:
                for j in range(FT // 2):
                    c = slice(256 * j, 256 * j + 256)
                    chunk(kxn(io["ffn_w_gate"][0], c), kxn(io["ffn_w_up"][0], c))
                for j in range(KT):
                    chunk(kxn(io["ffn_w_down"][0], slice(128 * j, 128 * j + 128)))
            else:
                chunk(kxn(io["router_w"][0], slice(0, NE)))
                first_moe = len(chunks)
                for e in range(NE):
                    for j in range(ET // 2):
                        c = slice(256 * j, 256 * j + 256)
                        chunk(kxn(io["moe_w_gate"][0, e], c), kxn(io["moe_w_up"][0, e], c))
                    for j in range(ET // 4):
                        rows = slice(512 * j, 512 * j + 512)
                        chunk(kxn(io["moe_w_down"][0, e, rows, :], slice(0, D)))

        W = Stream(chunks, w_in, WR)
        W2 = Stream(chunks[first_moe:], [sem(f"overflow_weights_in_{i}") for i in range(SLOTS)], WR)
        landed, arrive, release = W.landed, W.arrive, W.release

        C0s = (0, SEQ)
        LAM = [0.8 - 0.6 * math.exp(-0.3 * l) for l in range(2)]
        hq = [(q, h) for q in range(8) for h in range(2)]

        def pair(x, q, h):
            return x[64 * h:64 * h + 64, 64 * q:64 * q + 64]

        def items(l):
            qbs = range(2 if l else 0, 4)
            return ([("s", u, qb) for u in range(8) for qb in qbs] + [("d", h, qb) for h in range(4) for qb in qbs])

        both = ((0, V_), (1, S))
        marks, pool_n = {}, [0]
        done, built = [False], set()

        def stage(name):
            if stop is not None and name == stop:
                done[0] = True
            if not done[0]:
                built.add(name)
            return not done[0]

        at_spill = nc.dram_tensor("input_spill", (D, T), f32, kind="Internal").ap()
        spill = nc.dram_tensor("residual_spill", (D, SEQ), f32, kind="Internal").ap()
        block = ctx.enter_context(nc.Block())

        @block.tensor
        def _(pe):
            seen = Seen()
            pe.wait_ge(consts_in, 64)

            def mm(o, lhsT, rhs, first, last):
                return pe.matmul(o, lhsT, rhs, start=first, stop=last)

            def ada(l):
                if l == 0:
                    pe.wait_ge(silc_ready, seen(silc_ready))
                jobs = []

                def turn(j):
                    pe.wait_ge(A.free, jobs[j])
                    bank = V_.claim()
                    pe.wait_ge(V_.free, V_.due)
                    for i in range(4):
                        last = pe.transpose(bank[:, 2 * i:2 * i + 2], rowb[0:2, j % 2, 128 * i:128 * i + 128],
                                            eye[0:2, 0:2])
                    last.then_inc(V_.full, 1)
                    V_.done(("turn", l, j))

                for j in range(12):
                    pe.wait_ge(*landed())
                    w = arrive().rearrange("p (k n) -> p k n", k=KT)
                    bank = A.claim()
                    pe.wait_ge(A.free, A.due)
                    for k in range(KT):
                        last = mm(bank[0:2, :], silc[:, k, :], w[:, k, :], k == 0, k == KT - 1)
                    last.then_inc(A.full, 1)
                    A.done()
                    release(A)
                    jobs.append(A.made)
                    if j:
                        turn(j - 1)
                turn(11)

            def squares_sum(l, n, c0, src, wait):
                bank = A.claim()
                pe.wait_ge(A.free, A.due)
                for k in range(n):
                    wait(k)
                    last = mm(bank[:, c0:T], ones, src[:, k, c0:T], k == 0, k == n - 1)
                last.then_inc(A.full, 1)
                A.done()

            def feature_major(w, n_tiles, c0, ring, tag, src=None):
                for i in range(n_tiles):
                    bank = ring.claim()
                    pe.wait_ge(ring.free, ring.due)
                    for k in range(KT):
                        last = mm(bank[:, c0:T], w[:, k, 128 * i:128 * i + 128], (AT if src is None else src)[:, k, c0:T], k == 0,
                                  k == KT - 1)
                    last.then_inc(ring.full, 1)
                    ring.done((tag, i))

            def recurrence_inputs(l):
                pe.wait_ge(at_ready, seen(at_ready, KT))
                for j in range(4):
                    n = 4 if j < 3 else 3
                    pe.wait_ge(*landed())
                    w = arrive()[:, 0:KT * 128 * n].rearrange("p (k n) -> p k n", k=KT)
                    feature_major(w, n, 0, V_, ("rw", l, j))
                    release(V_)
                pe.wait_ge(*landed())
                up = arrive()[:, 0:3 * 512].rearrange("p (i n) -> p i n", i=3)
                pe.wait_ge(to_pe_a, seen(to_pe_a))
                for d in range(2):
                    for j in range(4):
                        bank = A.claim()
                        pe.wait_ge(A.free, A.due)
                        last = mm(bank, up[64 * d:64 * d + 64, 0, 128 * j:128 * j + 128],
                                  thw[64 * d:64 * d + 64, :], True, True)
                        last.then_inc(A.full, 1)
                        A.done(("decay", l, d, j))
                pe.wait_ge(V_.free, V_.jobs[(("rw", l, 3), 1)])
                for d in range(2):
                    for j in range(4):
                        bank = A.claim()
                        pe.wait_ge(A.free, A.due)
                        last = mm(bank, up[64 * d:64 * d + 64, 1, 128 * j:128 * j + 128],
                                  adin[64 * d:64 * d + 64, :], True, True)
                        last.then_inc(A.full, 1)
                        A.done(("rate", l, d, j))
                pe.wait_ge(to_pe_a, seen(to_pe_a))
                for j in range(4):
                    bank = A.claim()
                    pe.wait_ge(A.free, A.due)
                    last = mm(bank, up[:, 2, 128 * j:128 * j + 128], sgd, True, True)
                    last.then_inc(A.full, 1)
                    A.done()
                release(A)
                for j in range(4):
                    pe.wait_ge(to_pe_v, seen(to_pe_v))
                    bank = A.claim()
                    pe.wait_ge(A.free, A.due)
                    last = mm(bank, blk, tmpT[j % 2], True, True)
                    last.then_inc(A.full, 1)
                    A.done(("kknorm", l, j))
                for j in range(4):
                    pe.wait_ge(to_pe_v, seen(to_pe_v))
                    bank = V_.claim()
                    pe.wait_ge(V_.free, V_.due)
                    last = mm(bank, blk, tmpT[2 + j % 2], True, True)
                    last.then_inc(V_.full, 1)
                    V_.done(("bonus", l, j))

            def products(ring, terms, d, name=None):
                bank = ring.claim()
                pe.wait_ge(ring.free, ring.due)
                for q, h in hq[8 * d:8 * d + 8]:
                    for n, (lhs, rhs) in enumerate(terms):
                        last = mm(pair(bank, q, h), pair(lhs, q, h), pair(rhs, q, h), n == 0, n == len(terms) - 1)
                last.then_inc(ring.full, 1)
                ring.done(name)

            def against_eye(lhs, name=None):
                bank = A.claim()
                pe.wait_ge(A.free, A.due)
                for q, h in hq:
                    last = mm(pair(bank, q, h), lhs(q, h), eye[64 * h:64 * h + 64, 64 * h:64 * h + 64], True, True)
                last.then_inc(A.full, 1)
                A.done(name)

            def recurrence_step(l, i):
                y = not (l == 1 and i < 4)
                ra, aa, ba, ka = (tr[n + str(i % 2)] for n in ("ra", "aa", "ba", "ka"))
                pe.wait_ge(to_pe_v, seen(to_pe_v))
                for d, ring in both:
                    products(ring, [(aa, ba)], d)
                for d, ring in both:
                    products(ring, [(ba, aa)], d, ("LT", l, i, d))
                chunk_of = lambda q: i if q < 4 else BWD[i]
                against_eye(lambda q, h: Rv[64 * h:64 * h + 64, q % 4, CH * chunk_of(q):CH * chunk_of(q) + CH],
                            ("vt", l, i))
                for d, ring in both:
                    products(ring, [(ka, aa)], d)
                against_eye(lambda q, h: pair(ba, q, h))
                against_eye(lambda q, h: pair(ka, q, h))
                if y:
                    for d, ring in both:
                        products(ring, [(ba, ra)], d)
                    for d, ring in both:
                        products(ring, [(ka, ra)], d)
                for n in range(5):
                    for d, ring in both:
                        pe.wait_ge(ring.free, ring.jobs[("XT", l, i, d, n - 1) if n else ("LT", l, i, d)])
                        products(ring, [(tr["LT"], tr["X"])], d, ("T1", l, i, d, n))
                    for d, ring in both:
                        pe.wait_ge(ring.free, ring.jobs[("T1", l, i, d, n)])
                        if n < 4:
                            products(ring, [(tr["XT"], tr["T1"])], d)
                        products(ring, [(tr["T1"], tr["XT"])], d, ("XT", l, i, d, n))
                pe.wait_ge(A.free, A.jobs[("vt", l, i)])
                for d, ring in both:
                    products(A, [(aa, tr["Sr"]), (tr["MT"], tr["vt"])], d, ("G", l, i, d))
                for d, ring in both:
                    pe.wait_ge(ring.free, ring.jobs[("XT", l, i, d, 4)])
                    pe.wait_ge(A.free, A.jobs[("G", l, i, d)])
                    products(A, [(tr["XT"], tr["G"])], d, ("U", l, i, d))
                for d, ring in both:
                    pe.wait_ge(A.free, A.jobs[("U", l, i, d)])
                    products(ring, [(tr["bt"], tr["U"]), (tr["kt"], tr["vt"])], d, ("S", l, i, d))
                if y:
                    for d, ring in both:
                        products(ring, [(tr["Sr"], ra), (tr["U"], tr["RBT"]), (tr["vt"], tr["RKT"])], d)

            def recurrence_output(l):
                c0 = C0s[l]
                for what in ("mean", "var"):
                    for j in range(4):
                        pe.wait_ge(to_pe_v, seen(to_pe_v))
                        ring = V_ if what == "mean" else A
                        bank = ring.claim()
                        pe.wait_ge(ring.free, ring.due)
                        src = YA[:, j, c0:T] if what == "mean" else tmpO[j % 2][:, c0:T]
                        last = mm(bank[:, c0:T], blk, src, True, True)
                        last.then_inc(ring.full, 1)
                        ring.done(("gn" + what, l, j))

            def rope(l, tiles):
                for n, x in enumerate(tiles):
                    bank = V_.claim()
                    pe.wait_ge(V_.free, V_.due)
                    last = mm(bank[:, 0:SEQ], perm, x[:, SEQ:T], True, True)
                    last.then_inc(V_.full, 1)
                    V_.done(("rope", l, n))

            def attention_inputs(l):
                c0 = C0s[l]
                w8 = lambda w, n: w[:, 0:KT * n].rearrange("p (k n) -> p k n", k=KT)
                pe.wait_ge(at_reloaded, 16 * (l + 1))
                pe.wait_ge(*landed())
                feature_major(w8(arrive(), 512), 4, c0, A, ("qs", l))
                release(A)
                pe.wait_ge(*landed())
                w = w8(arrive(), 256)
                feature_major(w, 1, 0, A, ("ks", l))
                bank = V_.claim()
                pe.wait_ge(V_.free, V_.due)
                for b in range(4):
                    for k in range(KT):
                        last = mm(bank[:, 128 * b:128 * b + 128], AT[:, k, 128 * b:128 * b + 128], w[:, k, 128:256],
                                  k == 0, k == KT - 1)
                last.then_inc(V_.full, 1)
                V_.done()
                release(V_)
                pe.wait_ge(*landed())
                feature_major(w8(arrive(), 512), 4, c0, A, ("qd", l))
                release(A)
                pe.wait_ge(*landed())
                feature_major(w8(arrive(), 512), 4, 0, A, ("kd", l))
                release(A)
                pe.wait_ge(*landed())
                w = w8(arrive(), 512)
                for b in range(4):
                    bank = V_.claim()
                    pe.wait_ge(V_.free, V_.due)
                    for k in range(KT):
                        last = mm(bank, AT[:, k, 128 * b:128 * b + 128], w[:, k, :], k == 0, k == KT - 1)
                    last.then_inc(V_.full, 1)
                    V_.done()
                release(V_)
                pe.wait_ge(A.free, A.jobs[(("kd", l), 3)])
                rope(l, rope_tiles)
                pe.wait_ge(V_.free, V_.jobs[("rope", l, 4)])
                bank = A.claim()
                pe.wait_ge(A.free, A.due)
                last = mm(bank, swap, Ks[:, 0, :], True, True)
                last.then_inc(A.full, 1)
                A.done(("k2", l))
                pe.wait_ge(A.free, A.jobs[("k2", l)])
                pe.wait_ge(V_.free, V_.jobs[("rope", l, 12)])

            def attention(l):
                its = items(l)

                def scores(n):
                    kind, u, qb = its[n]
                    nk = SEQ if qb < 2 else T
                    qc = slice(128 * qb, 128 * qb + 128)
                    for c in range(1 if kind == "s" else 2):
                        h = u % 2 if kind == "s" else c
                        q = Qs[:, u // 2, qc] if kind == "s" else Qd[:, u, qc]
                        k = Ks[:, 0 if u // 4 == h else 1, 0:nk] if kind == "s" else Kd[:, u, 0:nk]
                        bank = S.claim()
                        pe.wait_ge(S.free, S.due)
                        last = mm(bank[:, 0:nk], q[64 * h:64 * h + 64, :], k[64 * h:64 * h + 64, :], True, True)
                        last.then_inc(S.full, 1)
                        S.done(("sc", l, n, c))

                def turn(n):
                    kind, u, qb = its[n]
                    pe.wait_ge(p_ready, seen(p_ready))
                    bank = A.claim()
                    pe.wait_ge(A.free, A.due)
                    for b in range(2 if qb < 2 else 4):
                        last = pe.transpose(bank[:, 128 * b:128 * b + 128], Pb[:, n % 2, 0, 128 * b:128 * b + 128], eye)
                    last.then_inc(A.full, 1)
                    A.done(("pt", l, n))

                def values(n):
                    kind, u, qb = its[n]
                    pe.wait_ge(A.free, A.jobs[("pt", l, n)])
                    bank = V_.claim()
                    pe.wait_ge(V_.free, V_.due)
                    nb = 2 if qb < 2 else 4
                    for b in range(nb):
                        if kind == "s":
                            h, g = u % 2, u // 4
                            last = mm(bank[64 * h:64 * h + 64, 0:128], Vt[:, b, 64 * g:64 * g + 64],
                                      PTb[:, n % 2, 128 * b:128 * b + 128], b == 0, b == nb - 1)
                        else:
                            last = mm(bank[:, 0:128], Vt[:, b, 128 + 128 * u:256 + 128 * u],
                                      PTb[:, n % 2, 128 * b:128 * b + 128], b == 0, b == nb - 1)
                    last.then_inc(V_.full, 1)
                    V_.done(("pv", l, n))

                for n in range(len(its) + 2):
                    if n < len(its):
                        scores(n)
                    if 1 <= n <= len(its):
                        turn(n - 1)
                    if n >= 2:
                        values(n - 2)
                for j in range(4):
                    pe.wait_ge(to_pe_a, seen(to_pe_a))
                    bank = A.claim()
                    pe.wait_ge(A.free, A.due)
                    last = mm(bank[:, C0s[l]:T], ones, SQd[:, j, C0s[l]:T], True, True)
                    last.then_inc(A.full, 1)
                    A.done()

            def merge(l):
                c0 = C0s[l]
                pe.wait_ge(to_pe_v, seen(to_pe_v))
                for b, y in enumerate((YA, YB, YC)):
                    pe.wait_ge(*landed())
                    g = arrive().rearrange("p (k n) -> p k n", k=KT)
                    pe.wait_ge(*landed())
                    p = arrive().rearrange("p (k n) -> p k n", k=4)
                    for j in range(KT):
                        if j == 4:
                            release(V_)
                            pe.wait_ge(*landed())
                            g = arrive().rearrange("p (k n) -> p k n", k=KT)
                        bank = A.claim()
                        pe.wait_ge(A.free, A.due)
                        for k in range(KT):
                            last = mm(bank[:, c0:T], g[:, k, 128 * (j % 4):128 * (j % 4) + 128], AT[:, k, c0:T],
                                      k == 0, k == KT - 1)
                        last.then_inc(A.full, 1)
                        A.done()
                        bank = V_.claim()
                        pe.wait_ge(V_.free, V_.due)
                        for k in range(4):
                            last = mm(bank[:, c0:T], p[:, k, 128 * j:128 * j + 128], y[:, k, c0:T], k == 0, k == 3)
                        last.then_inc(V_.full, 1)
                        V_.done(("merge", l, b, j))
                    release(V_)
                    release(V_)
                pe.wait_ge(V_.free, V_.jobs[("merge", l, 2, KT - 1)])
                for j in range(2):
                    pe.wait_ge(*landed())
                    w = arrive().rearrange("p (k n) -> p k n", k=KT)
                    feature_major(w, 4, c0, A, ("wo", l, j), src=MG)
                    release(A)
                squares_sum(l, KT, c0, SQ, lambda k: pe.wait_ge(A.free, A.jobs[(("wo", l, k // 4), k % 4)]))

            def norm(c0):
                squares_sum(0, KT, c0, AT, lambda k: pe.wait_ge(sq_ready, seen(sq_ready)))

            def ffn(l):
                pe.wait_ge(at_ready, seen(at_ready, KT))
                for j in range(FT // 2):
                    pe.wait_ge(*landed())
                    w = arrive().rearrange("p (g k n) -> p g k n", g=2, k=KT)
                    for i in range(2):
                        for g, ring in enumerate((A, V_)):
                            bank = ring.claim()
                            pe.wait_ge(ring.free, ring.due)
                            for k in range(KT):
                                last = mm(bank, w[:, g, k, 128 * i:128 * i + 128], AT[:, k, :], k == 0, k == KT - 1)
                            last.then_inc(ring.full, 1)
                            ring.done(("hid", l, 2 * j + i))
                    release(V_)
                pe.wait_ge(V_.free, V_.jobs[("hid", l, FT - 1)])
                for j in range(KT):
                    pe.wait_ge(*landed())
                    w = arrive()[:, 0:FT * 128].rearrange("p (k n) -> p k n", k=FT)
                    bank = A.claim()
                    pe.wait_ge(A.free, A.due)
                    for k in range(FT):
                        last = mm(bank, w[:, k, :], hid[:, k, :], k == 0, k == FT - 1)
                    last.then_inc(A.full, 1)
                    A.done(("dn", l, j))
                    release(A)
                squares_sum(l, KT, 0, AT, lambda k: pe.wait_ge(A.free, A.jobs[("dn", l, k)]))

            def moe(l):
                pe.wait_ge(at_ready, seen(at_ready, KT))
                pe.wait_ge(*landed())
                w = arrive()[:, 0:KT * NE].rearrange("p (k n) -> p k n", k=KT)
                bank = V_.claim()
                pe.wait_ge(V_.free, V_.due)
                for b in range(2):
                    for k in range(KT):
                        last = mm(bank[:, NE * b:NE * b + NE], AT[:, k, SEQ + 128 * b:SEQ + 128 * b + 128], w[:, k, :],
                                  k == 0, k == KT - 1)
                last.then_inc(V_.full, 1)
                V_.done()
                release(V_)
                for b in range(2):
                    for k4 in range(2):
                        bank = V_.claim()
                        pe.wait_ge(V_.free, V_.due)
                        for k in range(4):
                            last = pe.transpose(bank[:, 128 * k:128 * k + 128],
                                                AT[:, 4 * k4 + k, SEQ + 128 * b:SEQ + 128 * b + 128], eye)
                        last.then_inc(V_.full, 1)
                        V_.done()
                pe.wait_ge(to_pe_v, seen(to_pe_v))
                sel = [rt[:, b, 48:56] for b in range(2)]
                bank = V_.claim()
                pe.wait_ge(V_.free, V_.due)
                mm(bank[:, 0:8], tb("tri"), sel[0], True, True)
                mm(bank[:, 8:16], ones, sel[0], True, False)
                mm(bank[:, 8:16], tb("tri"), sel[1], False, True)
                mm(bank[:, 16:24], ones, sel[0], True, False)
                last = mm(bank[:, 16:24], ones, sel[1], False, True)
                last.then_inc(V_.full, 1)
                V_.done()
                experts(0, A, V_, S, W)
                pe.wait_ge(flag_ready, 1)
                crowded = pe.value_load(flag[0:1, 0:1], min_val=0, max_val=1)
                with pe.If(crowded > 0):
                    pe.wait_ge(A.free, A.made)
                    pe.wait_ge(V_.free, V_.made)
                    pe.wait_ge(S.free, S.made)
                    experts(1, A2, V2, S2, W2)
                    pe.wait_ge(A2.free, A2.made)
                    pe.wait_ge(V2.free, V2.made)
                    pe.wait_ge(S2.free, S2.made)
                bank = A.claim()
                pe.wait_ge(A.free, A.due)
                for k in range(KT):
                    pe.wait_ge(sq_ready, seen(sq_ready))
                    last = mm(bank[:, SEQ:T], ones, AT[:, k, SEQ:T], k == 0, k == KT - 1)
                last.then_inc(A.full, 1)
                A.done()

            def experts(p, A, V_, S, W):
                def gather(e):
                    pe.wait_ge(to_pe_v, seen(to_pe_v))
                    for k4 in range(2):
                        bank = V_.claim()
                        pe.wait_ge(V_.free, V_.due)
                        for k in range(4):
                            for b in range(2):
                                c = 128 * (4 * k4 + k)
                                last = mm(bank[:, 128 * k:128 * k + 128], Atok[:, b, c:c + 128],
                                          Psel[:, e % 2, b, :], b == 0, b == 1)
                        last.then_inc(V_.full, 1)
                        V_.done(("gather", p, e))

                def turn(e):
                    bank = V_.claim()
                    pe.wait_ge(V_.free, V_.due)
                    for b in range(2):
                        last = pe.transpose(bank[:, 128 * b:128 * b + 128], Pw[:, b, :], eye)
                    last.then_inc(V_.full, 1)
                    V_.done(("pwt", p, e))

                def combine(e):
                    pe.wait_ge(S.free, S.jobs[("y", p, e)])
                    pe.wait_ge(V_.free, V_.jobs[("pwt", p, e)])
                    for k2 in range(4):
                        bank = V_.claim()
                        pe.wait_ge(V_.free, V_.due)
                        for k in range(2):
                            c = 128 * (2 * k2 + k)
                            last = mm(bank[:, SEQ * k:SEQ * k + SEQ], Ysb[:, c:c + 128], PwT[:, e % 2, :], True, True)
                        last.then_inc(V_.full, 1)
                        V_.done(("combine", p, e))

                gather(0)
                for e in range(NE):
                    pe.wait_ge(V_.free, V_.jobs[("gather", p, e)])
                    for j in range(ET // 2):
                        pe.wait_ge(*W.landed())
                        w = W.arrive().rearrange("p (g k n) -> p g k n", g=2, k=KT)
                        for g, ring in enumerate((A, V_)):
                            bank = ring.claim()
                            pe.wait_ge(ring.free, ring.due)
                            for i in range(2):
                                for k in range(KT):
                                    last = mm(bank[:, CAP * i:CAP * i + CAP], w[:, g, k, 128 * i:128 * i + 128],
                                              XE[:, e % 2, k, :], k == 0, k == KT - 1)
                            last.then_inc(ring.full, 1)
                            ring.done(("hid", p, e, j))
                        W.release(V_)
                        if e and j == 1:
                            combine(e - 1)
                    if e < NE - 1:
                        gather(e + 1)
                    pe.wait_ge(to_pe_v, seen(to_pe_v))
                    turn(e)
                    pe.wait_ge(V_.free, V_.jobs[("hid", p, e, ET // 2 - 1)])
                    ys = []
                    for h in range(2):
                        ys.append(S.banks[(S.made + h) % 2])
                        pe.wait_ge(S.free, max(0, S.made + h - 1))
                    for j in range(ET // 4):
                        pe.wait_ge(*W.landed())
                        w = W.arrive().rearrange("p (k n) -> p k n", k=4)
                        for k in range(4):
                            f_ = 4 * j + k
                            for h in range(2):
                                last = mm(ys[h], hidm[:, f_, :], w[:, k, 512 * h:512 * h + 512], f_ == 0, f_ == ET - 1)
                                if f_ == ET - 1:
                                    last.then_inc(S.full, 1)
                                    S.done(("y", p, e))
                        if j < ET // 4 - 1:
                            last.then_inc(down_step[p], 1)
                            W.released.append((down_step[p], (ET // 4 - 1) * e + j + 1))
                        else:
                            W.release(S)
                combine(NE - 1)
            for l in range(2):
                if stage(f"ada{l}"):
                    ada(l)
                    norm(0)
                if stage(f"rwin{l}"):
                    recurrence_inputs(l)
                if stage(f"rwstep{l}"):
                    S.start(("steps", l))
                    for i in range(NCH):
                        recurrence_step(l, i)
                    recurrence_output(l)
                if stage(f"attn{l}"):
                    attention_inputs(l)
                    S.start(("scores", l))
                    attention(l)
                if stage(f"merge{l}"):
                    merge(l)
                if stage(f"ffn{l}"):
                    norm(C0s[l])
                    (ffn if l == 0 else moe)(l)

        done[0] = False
        marks.clear()

        @block.scalar
        def _(act):
            seen = Seen()
            act.wait_ge(consts_in, 64)
            act.wait_ge(coef_ready, 1)
            own = {}

            def a(ins, s, wait=False):
                own[s.name] = own.get(s.name, 0) + 1
                ins.then_inc(s, 1)
                if wait:
                    act.wait_ge(s, own[s.name])

            def f(out, in_, func, **k):
                return act.activation(out, in_, func, **k)

            def free(ins, name=None):
                ins.then_inc(A.free, 1)
                if name is not None:
                    marks[name] = A.taken

            a(f(silc[:, :, :].rearrange("p k s -> p (k s)"), vec[:, 2 * VEC_L:2 * VEC_L + 16], ACT.Silu), silc_ready)

            def ada(l):
                for j in range(12):
                    bank = A.take()
                    act.wait_ge(A.full, A.taken)
                    if j >= 2:
                        act.wait_ge(V_.full, V_.jobs[("turn", l, j - 2)])
                    free(f(rowb[0:2, j % 2, :], bank[0:2, :], ACT.Copy))

            def root(c0, n, eps_col, name):
                bank = A.take()
                act.wait_ge(A.full, A.taken)
                free(f(RS[:, 0, c0:T], bank[:, c0:T], ACT.Sqrt, scale=1.0 / n, bias=cvec[:, eps_col:eps_col + 1]), name)

            def norm(l, c0, which):
                if l == 0 and which == "mix":
                    act.wait_ge(x_in, 16)
                for k in range(KT):
                    if l or which == "ffn":
                        act.wait_ge(h_ready, seen(h_ready))
                    a(f(AT[:, k, c0:T], HT[:, k, c0:T], ACT.Square), sq_ready)
                root(c0, D, 0, ("root", l, which))
                for k in range(KT):
                    for s in range(c0 // SEQ, 2):
                        act.wait_ge(at_scaled, seen(at_scaled))
                        ins = f(AT[:, k, SEQ * s:SEQ * s + SEQ], AT[:, k, SEQ * s:SEQ * s + SEQ], ACT.Identity,
                                bias=mods[:, (0 if which == "mix" else 24) + k, s:s + 1])
                    a(ins, at_ready)

            def recurrence_inputs(l):
                if l:
                    act.wait_ge(spilled, 16)
                act.wait_ge(V_.free, V_.jobs[(("rw", l, 3), 0)])
                a(f(thw, wdin, ACT.Tanh), to_pe_a)
                for d in range(2):
                    for j in range(4):
                        bank = A.take()
                        act.wait_ge(A.full, A.taken)
                        n = 4 * d + j
                        if n >= 2:
                            act.wait_ge(to_act, seen(to_act))
                        free(f(sgt[n % 2], bank[:, :], ACT.Sigmoid, bias=V(l, "w0", n)), ("sg", l, n))
                for d in range(2):
                    for j in range(4):
                        bank = A.take()
                        act.wait_ge(A.full, A.taken)
                        n = 4 * d + j
                        free(f(Ra[:, d, j, :], bank[:, :], ACT.Sigmoid, bias=V(l, "a0", n)), ("rate", l, n))
                act.wait_ge(V_.free, V_.jobs[(("rw", l, 3), 2)])
                a(f(sgd, gdin, ACT.Sigmoid), to_pe_a)
                for j in range(4):
                    bank = A.take()
                    act.wait_ge(A.full, A.taken)
                    free(f(YB[:, j, :], bank[:, :], ACT.Copy), ("g", l, j))
                act.wait_ge(to_act, seen(to_act, 2))
                for j in range(4):
                    bank = A.take()
                    act.wait_ge(A.full, A.taken)
                    if j:
                        act.wait_ge(to_act, seen(to_act))
                    free(f(RS[:, 0, :], bank[:, :], ACT.Sqrt, scale=64.0), ("kkroot", l, j))
                act.wait_ge(to_act, seen(to_act))

            def decays(l, i):
                act.wait_ge(to_act, seen(to_act))
                for d in range(2):
                    qs = slice(4 * d, 4 * d + 4)
                    inc = slice(1, CW) if d == 0 else slice(0, CH)
                    exc = slice(0, CH) if d == 0 else slice(1, CW)
                    v = lambda n: tr[n + str(i % 2)].rearrange("p (q w) -> p q w", q=8)[:, qs, :]
                    f(v("E1"), CC[:, qs, inc], ACT.Exp, scale=-KAPPA)
                    f(v("E2"), CC[:, qs, exc], ACT.Exp, scale=-KAPPA)
                    f(v("E3"), CC[:, qs, inc], ACT.Exp, scale=KAPPA)
                    c = i if d == 0 else BWD[i]
                    f(eS[:, i % 2, 0, qs], Rc[:, d, :, c, 32], ACT.Exp, scale=-KAPPA)
                    e = CH if d == 0 else 0
                    ins = f(eS[:, i % 2, 1, qs], CC[:, qs, e], ACT.Exp, scale=-KAPPA)
                a(ins, to_dve)

            def recurrence_step(l, i):
                if i == 0:
                    decays(l, 0)
                    act.wait_ge(at_spilled, 16 * (l + 1))
                for n in ("vt", "bt", "kt"):
                    bank = A.take()
                    act.wait_ge(A.full, A.taken)
                    free(f(tr[n], bank[:, :], ACT.Copy))
                if i < NCH - 1:
                    decays(l, i + 1)
                for n in ("G", "U"):
                    for d in range(2):
                        bank = A.take()
                        act.wait_ge(A.full, A.taken)
                        c = slice(256 * d, 256 * d + 256)
                        free(f(tr[n][:, c], bank[:, c], ACT.Copy))
            def recurrence_output(l):
                c0 = C0s[l]
                for j in range(4):
                    bank = A.take()
                    act.wait_ge(A.full, A.taken)
                    if j:
                        act.wait_ge(to_act, seen(to_act))
                    free(f(RS[:, 0, c0:T], bank[:, c0:T], ACT.Sqrt, bias=cvec[:, 1:2]), ("gnroot", l, j))
                act.wait_ge(to_act, seen(to_act))

            def attention_inputs(l):
                c0 = C0s[l]
                for dst, c in [(Qs[:, j, :], c0) for j in range(4)] + [(Ks[:, 0, :], 0)] + \
                              [(Qd[:, j, :], c0) for j in range(4)] + [(Kd[:, j, :], 0) for j in range(4)]:
                    bank = A.take()
                    act.wait_ge(A.full, A.taken)
                    free(f(dst[:, c:T], bank[:, c:T], ACT.Copy))
                bank = A.take()
                act.wait_ge(A.full, A.taken)
                free(f(Ks[:, 1, :], bank[:, :], ACT.Copy))
                act.wait_ge(lam_in, seen(lam_in))
                a(f(cvec[:, 4:6], cvec[:, 4:6], ACT.Exp), lam_out)

            def attention(l):
                its = items(l)
                for n in range(len(its) + 1):
                    if n < len(its):
                        kind, u, qb = its[n]
                        nk = SEQ if qb < 2 else T
                        for c in range(1 if kind == "s" else 2):
                            bank = S.take()
                            act.wait_ge(S.full, S.taken)
                            act.wait_ge(m_ready, seen(m_ready))
                            if n >= 2:
                                act.wait_ge(A.full, A.jobs[("pt", l, n - 2)])
                            f(Pb[:, n % 2, c, 0:nk], bank[:, 0:nk], ACT.Exp, scale=HD ** -0.5,
                              bias=st[:, n % 4, c, 1:2], accum_out=st[:, n % 4, c, 2:3]).then_inc(S.free, 1)
                            marks[("exp", l, n, c)] = S.taken
                        if kind == "s":
                            a(f(st[:, n % 4, 0, 3:4], st[:, n % 4, 0, 1:2], ACT.Exp, bias=rep[:, l, u:u + 1]),
                              es_ready)
                    if n >= 1:
                        kind, u, qb = its[n - 1]
                        nk = SEQ if qb < 2 else T
                        bank = A.take()
                        act.wait_ge(A.full, A.taken)
                        if n >= 3:
                            act.wait_ge(V_.full, V_.jobs[("pv", l, n - 3)])
                        free(f(PTb[:, (n - 1) % 2, 0:nk], bank[:, 0:nk], ACT.Copy))
                c0 = C0s[l]
                for j in range(4):
                    if j == 0:
                        act.wait_ge(to_act, seen(to_act))
                    a(f(SQd[:, j, c0:T], YC[:, j, c0:T], ACT.Square), to_pe_a)
                for j in range(4):
                    bank = A.take()
                    act.wait_ge(A.full, A.taken)
                    if j:
                        act.wait_ge(to_act, seen(to_act))
                    free(f(RS[:, 0, c0:T], bank[:, c0:T], ACT.Sqrt, scale=1.0 / 128, bias=cvec[:, 2:3]),
                         ("dfroot", l, j))
                act.wait_ge(to_act, seen(to_act))

            def merge(l):
                c0 = C0s[l]
                n = 0
                for b in range(3):
                    for j in range(KT):
                        bank = A.take()
                        act.wait_ge(A.full, A.taken)
                        if n >= 2:
                            act.wait_ge(V_.free, V_.jobs[("merge", l, (n - 2) // KT, (n - 2) % KT)])
                        free(f(sgb[:, n % 2, c0:T], bank[:, c0:T], ACT.Sigmoid), ("sgb", l, n))
                        n += 1
                copies(l, c0, SQ, "mix")

            def copies(l, c0, sq, which):
                for k in range(KT):
                    bank = A.take()
                    act.wait_ge(A.full, A.taken)
                    f(MO[:, k, c0:T], bank[:, c0:T], ACT.Copy)
                    free(f(sq[:, k, c0:T], bank[:, c0:T], ACT.Square))
                root(c0, D, 0, ("postroot", l, which))

            def ffn(l):
                for n in range(FT):
                    bank = A.take()
                    act.wait_ge(A.full, A.taken)
                    if n >= 2:
                        act.wait_ge(V_.free, V_.jobs[("hid", l, n - 2)])
                    free(f(htmp[:, n % 2, :], bank[:, :], ACT.Silu), ("silu", l, n))
                copies(l, 0, AT, "ffn")

            def moe(l):
                for b in range(2):
                    act.wait_ge(lam_in, seen(lam_in))
                    a(f(rt[:, b, 27:28], rt[:, b, 26:27], ACT.Exp), lam_out)
                experts(0, A, V_, S)
                act.wait_ge(flag_ready, 1)
                crowded = act.value_load(flag[0:1, 0:1], min_val=0, max_val=1)
                with act.If(crowded > 0):
                    experts(1, A2, V2, S2)
                act.wait_ge(to_act, seen(to_act))
                for k in range(KT):
                    a(f(AT[:, k, SEQ:T], FA[:, k, :], ACT.Square), sq_ready)
                root(SEQ, D, 0, ("postroot", l, "ffn"))

            def experts(p, A, V_, S):
                for e in range(NE):
                    for j in range(ET // 2):
                        bank = A.take()
                        act.wait_ge(A.full, A.taken)
                        m = e * (ET // 2) + j - 2
                        if m >= 0:
                            act.wait_ge(V_.free, V_.jobs[("hid", p, m // (ET // 2), m % (ET // 2))])
                        f(htm[:, j % 2, :], bank[:, 0:2 * CAP], ACT.Silu).then_inc(A.free, 1)
                        marks[("silu", p, e, j)] = A.taken
                    if e:
                        act.wait_ge(V_.full, V_.jobs[("combine", p, e - 1)])
                    for h in range(2):
                        bank = S.take()
                        act.wait_ge(S.full, S.taken)
                        f(Ysb[:, 512 * h:512 * h + 512], bank[:, :], ACT.Copy).then_inc(S.free, 1)
            for l in range(2):
                if stage(f"ada{l}"):
                    ada(l)
                    norm(l, 0, "mix")
                if stage(f"rwin{l}"):
                    recurrence_inputs(l)
                if stage(f"rwstep{l}"):
                    for i in range(NCH):
                        recurrence_step(l, i)
                    recurrence_output(l)
                if stage(f"attn{l}"):
                    attention_inputs(l)
                    S.begin(("scores", l))
                    attention(l)
                if stage(f"merge{l}"):
                    merge(l)
                if stage(f"ffn{l}"):
                    norm(l, C0s[l], "ffn")
                    (ffn if l == 0 else moe)(l)

            if done[0]:
                f(cvec[:, 30:31], cvec[:, 0:1], ACT.Copy).then_inc(act_step, 1)

        done[0] = False

        @block.vector
        def _(dve):
            seen = Seen()
            own = {}

            chain = [dve_step]

            def v(ins, s=None, wait=True):
                s = s or chain[0]
                own[s.name] = own.get(s.name, 0) + 1
                ins.then_inc(s, 1)
                if wait:
                    dve.wait_ge(s, own[s.name])

            def vf(ins, wait=True):
                ins.then_inc(V_.free, 1)
                if wait:
                    dve.wait_ge(V_.free, V_.taken)

            TT, TS, STT = dve.tensor_tensor, dve.tensor_scalar, dve.scalar_tensor_tensor
            dve.wait_ge(consts_in, 64)
            v(dve.memset(cvec[:, 0:1], 1e-6))
            v(dve.memset(cvec[:, 1:2], 64e-5))
            if stop:
                for x in (YA, YB, YC):
                    v(dve.memset(x[:, :, :], 0.0))
            v(dve.memset(cvec[:, 2:3], 1e-5), coef_ready)
            dve.wait_ge(x_in, 16)

            def ada(l):
                for j in range(12):
                    bank = V_.take()
                    dve.wait_ge(V_.full, V_.taken)
                    vf(TT(mods[:, 4 * j:4 * j + 4, :], bank[:, 0:8].rearrange("p (i s) -> p i s", s=2),
                          V(l, "ada_b")[:, 4 * j:4 * j + 4].unsqueeze(2).to_broadcast([128, 4, 2]), ALU.add))
                for n, (m, g, add) in enumerate(((8, "pre_mix", 1.0), (16, "post_mix", 0.0), (32, "pre_ffn", 1.0),
                                                 (40, "post_ffn", 0.0))):
                    v(STT(coef[:, n, :, :], mods[:, m:m + 8, :], add,
                          V(l, g).unsqueeze(2).to_broadcast([128, 8, 2]), ALU.add, ALU.mult))

            def norm(l, c0, which):
                dve.wait_ge(A.free, marks[("root", l, which)])
                v(dve.reciprocal(RS[:, 1, c0:T], RS[:, 0, c0:T]))
                ci = 0 if which == "mix" else 2
                for k in range(KT):
                    for s in range(c0 // SEQ, 2):
                        c = slice(SEQ * s, SEQ * s + SEQ)
                        v(STT(AT[:, k, c], HT[:, k, c], coef[:, ci, k, s:s + 1], RS[:, 1, c], ALU.mult, ALU.mult),
                          at_scaled, wait=False)

            def recurrence_inputs(l):
                if l:
                    dve.wait_ge(spilled, 16)
                v(TT(muc[:, :], V(l, "mu_p"), V(l, "mu_n"), ALU.add))
                v(TS(muc[:, :], muc[:, :], -1.0, 1.0, ALU.mult, ALU.add))
                dst = [Rr[:, j, :] for j in range(4)] + [Rk[:, j, :] for j in range(4)] + \
                      [Rv[:, j, :] for j in range(4)] + [wdin, adin, gdin]
                for n in range(RT_TILES):
                    bank = V_.take()
                    dve.wait_ge(V_.full, V_.taken)
                    x = dst[n]
                    v(TS(x, bank[:, :], muc[:, n:n + 1], None, ALU.mult))
                    x2 = x.rearrange("p (s t) -> p s t", s=2)
                    b2 = bank[:, :].rearrange("p (s t) -> p s t", s=2)
                    v(STT(x2[:, :, 1:SEQ], b2[:, :, 0:SEQ - 1], V(l, "mu_p", n), x2[:, :, 1:SEQ], ALU.mult, ALU.add))
                    vf(STT(x2[:, :, 0:SEQ - 1], b2[:, :, 1:SEQ], V(l, "mu_n", n), x2[:, :, 0:SEQ - 1], ALU.mult,
                           ALU.add))
                v(dve.memset(onesw, 1.0))
                v(dve.memset(YA[:, :, :], 0.0))
                v(dve.memset(tr["S"], 0.0))
                for d in range(2):
                    v(dve.memset(Rc[:, d, :, :, 0 if d == 0 else CH], 0.0))
                for n in range(8):
                    d, j = n // 4, n % 4
                    dve.wait_ge(A.free, marks[("sg", l, n)])
                    sg = sgt[n % 2]
                    for c in range(NCH):
                        lo, hi = CH * c, CH * c + CH
                        if d == 0:
                            o, i_ = Rc[:, d, j, c, 1:CW], sg[:, lo:hi]
                        else:
                            o, i_ = Rc[:, d, j, c, CH - 1::-1], (sg[:, hi - 1:lo - 1:-1] if lo else sg[:, hi - 1::-1])
                        ins = dve.tensor_tensor_scan(o, onesw, i_, 0.0, ALU.mult, ALU.add)
                        if c < NCH - 1:
                            v(ins, wait=False)
                        else:
                            v(ins, to_act)
                for j in range(4):
                    v(TS(Rkk[:, j, :], Rk[:, j, :], V(l, "k_k", j), None, ALU.mult))
                    if j >= 2:
                        dve.wait_ge(A.full, A.jobs[("kknorm", l, j - 2)])
                    v(TT(tmpT[j % 2], Rkk[:, j, :], Rkk[:, j, :], ALU.mult), to_pe_v)
                for j in range(4):
                    dve.wait_ge(A.free, marks[("kkroot", l, j)])
                    v(TS(RS[:, 1, :], RS[:, 0, :], 1e-12, None, ALU.max), to_act)
                    v(dve.reciprocal(RS[:, 1, :], RS[:, 1, :]))
                    v(TT(Rkk[:, j, :], Rkk[:, j, :], RS[:, 1, :], ALU.mult))
                dve.wait_ge(A.free, marks[("rate", l, 7)])
                v(TS(cv2, V(l, "k_a"), -2.0, 2.0, ALU.mult, ALU.add))

                def bonus_in(j):
                    t = tmpT[2 + j % 2]
                    v(TT(t, Ra[:, 0, j, :], Ra[:, 1, j, :], ALU.add))
                    v(TS(t, t, V(l, "k_a", j), cv2[:, j:j + 1], ALU.mult, ALU.add))
                    v(TT(t, t, Rk[:, j, :], ALU.mult))
                    v(STT(t, t, V(l, "r_k", j), Rr[:, j, :], ALU.mult, ALU.mult), to_pe_v)

                def bonus_out(j):
                    bank = V_.take()
                    dve.wait_ge(V_.full, V_.taken)
                    vf(STT(YC[:, j, :], bank[:, :], 64.0, Rv[:, j, :], ALU.mult, ALU.mult))

                for j in range(5):
                    if j < 4:
                        bonus_in(j)
                    if j:
                        bonus_out(j - 1)

            def chunks_of(i):
                return i, BWD[i]

            def centre(l, i):
                for d in range(2):
                    c = chunks_of(i)[d]
                    ins = TT(CC[:, 4 * d:4 * d + 4, :], Rc[:, d, :, c, :],
                             Rc[:, d, :, c, 32:33].to_broadcast([128, 4, CW]), ALU.subtract)
                    v(ins, dve_step if d == 0 else to_act)

            def operands(l, i):
                y = not (l == 1 and i < 4)
                dve.wait_ge(to_dve, seen(to_dve))
                q3 = lambda n: tr[n + str(i % 2)].rearrange("p (q w) -> p q w", q=8)
                ka = V(l, "k_a").unsqueeze(2).to_broadcast([128, 4, CH])
                for d in range(2):
                    c = slice(CH * chunks_of(i)[d], CH * chunks_of(i)[d] + CH)
                    g = lambda n: q3(n)[:, 4 * d:4 * d + 4, :]
                    v(STT(g("ka"), Ra[:, d, :, c], -1.0, ka, ALU.add, ALU.mult), wait=False)
                    v(TT(g("ba"), Rkk[:, :, c], Ra[:, d, :, c], ALU.mult))
                    v(STT(g("ka"), g("ka"), 1.0, Rk[:, :, c], ALU.add, ALU.mult), wait=False)
                    v(TT(g("ba"), g("ba"), g("E3"), ALU.mult))
                    if y:
                        v(TT(g("ra"), Rr[:, :, c], g("E1"), ALU.mult), wait=False)
                    v(STT(g("aa"), Rkk[:, :, c], -1.0, g("E2"), ALU.mult, ALU.mult))
                    v(TT(g("ka"), g("ka"), g("E3"), ALU.mult), dve_step if d == 0 else to_pe_v, wait=(d == 0))

            def recurrence_step(l, i):
                y = not (l == 1 and i < 4)
                q3 = lambda x: x.rearrange("p (q w) -> p q w", q=8)
                mk = lambda m, d: masks[:, m, d, :].unsqueeze(1).to_broadcast([128, 4, 64])

                def half(x, d):
                    return x.rearrange("p (q w) -> p q w", q=8)[:, 4 * d:4 * d + 4, :]

                def take(ring):
                    return ring.take()

                def masked(n, m):
                    for d, ring in both:
                        bank = take(ring)
                        dve.wait_ge(ring.full, ring.taken)
                        TT(half(tr[n], d), half(bank, d), mk(m, d), ALU.mult).then_inc(ring.free, 1)

                if i == 0:
                    centre(l, 0)
                    dve.wait_ge(at_spilled, 16 * (l + 1))
                    operands(l, 0)
                v(TT(q3(tr["Sr"]), q3(tr["S"]), eS[:, i % 2, 0, :].unsqueeze(2).to_broadcast([128, 8, 64]), ALU.mult))
                for d, ring in both:
                    bank = take(ring)
                    dve.wait_ge(ring.full, ring.taken)
                    v(TT(half(tr["X"], d), half(bank, d), mk(M_LEVEL, d), ALU.mult))
                    TT(half(tr["X"], d), half(tr["X"], d), mk(M_EYE, d), ALU.add).then_inc(ring.free, 1)
                for d, ring in both:
                    bank = take(ring)
                    dve.wait_ge(ring.full, ring.taken)
                    v(TT(half(tr["XT"], d), half(bank, d), mk(M_PAIR_T, d), ALU.mult))
                    v(TT(half(tr["XT"], d), half(tr["XT"], d), mk(M_EYE, d), ALU.add), wait=False)
                    TT(half(tr["LT"], d), half(bank, d), mk(M_STRICT_T, d), ALU.mult).then_inc(ring.free, 1)
                masked("MT", M_STRICT_T)
                if y:
                    masked("RBT", M_INCL_T)
                    masked("RKT", M_INCL_T)
                if i < NCH - 1:
                    centre(l, i + 1)
                for n in range(5):
                    masked("T1", M_LEVEL + 1 + n)
                    for d, ring in both:
                        if n < 4:
                            bank = take(ring)
                            dve.wait_ge(ring.full, ring.taken)
                            TT(half(tr["X"], d), half(bank, d), half(tr["X"], d), ALU.add).then_inc(ring.free, 1)
                        bank = take(ring)
                        dve.wait_ge(ring.full, ring.taken)
                        TT(half(tr["XT"], d), half(bank, d), half(tr["XT"], d), ALU.add).then_inc(ring.free, 1)
                    if n == 2 and i < NCH - 1:
                        operands(l, i + 1)
                for d, ring in both:
                    bank = take(ring)
                    dve.wait_ge(ring.full, ring.taken)
                    TT(half(tr["S"], d), half(bank, d), half(tr["Sr"], d), ALU.add).then_inc(ring.free, 1)
                for d, ring in both:
                    dve.wait_ge(ring.free, ring.taken)
                v(TT(q3(tr["S"]), q3(tr["S"]), eS[:, i % 2, 1, :].unsqueeze(2).to_broadcast([128, 8, 64]), ALU.mult))
                if y:
                    for d, ring in both:
                        c = slice(CH * chunks_of(i)[d], CH * chunks_of(i)[d] + CH)
                        bank = take(ring)
                        dve.wait_ge(ring.full, ring.taken)
                        TT(YA[:, :, c], half(bank, d), YA[:, :, c], ALU.add).then_inc(ring.free, 1)
            def recurrence_output(l):
                c0 = C0s[l]
                dve.wait_ge(V_.free, V_.taken)
                dve.wait_ge(S.free, S.taken)
                v(dve.memset(cvec[:, 3:4], 0.0), to_pool)
                for j in range(4):
                    v(dve.memset(cvec[:, 3:4], 0.0), to_pe_v)
                for j in range(4):
                    bank = V_.take()
                    dve.wait_ge(V_.full, V_.taken)
                    vf(TT(YA[:, j, c0:T], YA[:, j, c0:T], bank[:, c0:T], ALU.subtract))
                for j in range(4):
                    if j >= 2:
                        dve.wait_ge(A.full, A.jobs[("gnvar", l, j - 2)])
                    v(TT(tmpO[j % 2][:, c0:T], YA[:, j, c0:T], YA[:, j, c0:T], ALU.mult), to_pe_v)
                dve.wait_ge(A.free, marks[("g", l, 3)])
                for j in range(4):
                    y = YA[:, j, c0:T]
                    dve.wait_ge(A.free, marks[("gnroot", l, j)])
                    v(dve.reciprocal(RS[:, 1, c0:T], RS[:, 0, c0:T]), to_act)
                    v(TT(y, y, RS[:, 1, c0:T], ALU.mult))
                    v(TS(y, y, V(l, "ln_g", j), V(l, "ln_b", j), ALU.mult, ALU.add))
                    v(TT(y, y, YC[:, j, c0:T], ALU.add))
                    v(TT(YB[:, j, c0:T], y, YB[:, j, c0:T], ALU.mult))

            def attention_inputs(l):
                bank = V_.take()
                dve.wait_ge(V_.full, V_.taken)
                vf(dve.tensor_copy(Vt[:, :, 0:128], bank[:, :].rearrange("p (b n) -> p b n", b=4)), wait=False)
                for b in range(4):
                    bank = V_.take()
                    dve.wait_ge(V_.full, V_.taken)
                    vf(dve.tensor_copy(Vt[:, b, 128:640], bank[:, :]), wait=False)
                cs, sn = tb("cos"), tb("sin")
                for n, x in enumerate(rope_tiles):
                    bank = V_.take()
                    dve.wait_ge(V_.full, V_.taken)
                    v(TT(rtmp[:, 0, 0:SEQ], bank[:, 0:SEQ], sn, ALU.mult))
                    v(TT(x[:, SEQ:T], x[:, SEQ:T], cs, ALU.mult))
                    vf(TT(x[:, SEQ:T], x[:, SEQ:T], rtmp[:, 0, 0:SEQ], ALU.add))
                lv = rep[:, l, 8:264].rearrange("p (i n) -> p i n", i=4)
                for i in range(2):
                    v(TT(rtmp[:, 1, 0:64], lv[:, 2 * i, :], lv[:, 2 * i + 1, :], ALU.mult))
                    v(dve.tensor_reduce(cvec[:, 4 + i:5 + i], rtmp[:, 1, 0:64], AX.X, ALU.add))
                v(TS(sink8, rep[:, l, 0:8], HD ** 0.5, None, ALU.mult))
                v(TS(cvec[:, 7:8], V(l, "subln", 0), 1.0 - LAM[l], None, ALU.mult), lam_in)

            def attention(l):
                its = items(l)
                dve.wait_ge(lam_out, seen(lam_out))
                v(STT(cvec[:, 6:7], cvec[:, 4:5], LAM[l], cvec[:, 5:6], ALU.add, ALU.subtract))

                def maxima(n):
                    kind, u, qb = its[n]
                    nk = SEQ if qb < 2 else T
                    for c in range(1 if kind == "s" else 2):
                        dve.wait_ge(S.full, S.jobs[("sc", l, n, c)])
                        bank = S.banks[(S.jobs[("sc", l, n, c)] - 1) % 2]
                        if kind == "s" and qb >= 2:
                            k0 = 384 if qb == 2 else 256
                            w = slice(k0, k0 + 128)
                            b0 = 0 if qb == 2 else 128
                            v(TT(bank[:, w], bank[:, w], tb("band")[:, b0:b0 + 128], ALU.add))
                        m = st[:, n % 4, c, 0:1]
                        v(dve.tensor_reduce(m, bank[:, 0:nk], AX.X, ALU.max))
                        if kind == "s":
                            v(TT(m, m, sink8[:, u:u + 1], ALU.max))
                        v(TS(st[:, n % 4, c, 1:2], m, -(HD ** -0.5), None, ALU.mult), m_ready)

                def normalise(n):
                    kind, u, qb = its[n]
                    nk = SEQ if qb < 2 else T
                    s0, s1 = st[:, n % 4, 0, :], st[:, n % 4, 1, :]
                    p0, p1 = Pb[:, n % 2, 0, 0:nk], Pb[:, n % 2, 1, 0:nk]
                    dve.wait_ge(S.free, marks[("exp", l, n, 0 if kind == "s" else 1)])
                    if kind == "s":
                        dve.wait_ge(es_ready, seen(es_ready))
                        v(TT(s0[:, 2:3], s0[:, 2:3], s0[:, 3:4], ALU.add))
                        v(dve.reciprocal(s0[:, 3:4], s0[:, 2:3]))
                        v(TS(p0, p0, s0[:, 3:4], None, ALU.mult), p_ready)
                    else:
                        v(dve.reciprocal(s0[:, 3:4], s0[:, 2:3]), wait=False)
                        v(dve.reciprocal(s1[:, 3:4], s1[:, 2:3]))
                        v(TS(p1, p1, s1[:, 3:4], cvec[:, 6:7], ALU.mult, ALU.mult))
                        v(STT(p0, p0, s0[:, 3:4], p1, ALU.mult, ALU.subtract), p_ready)

                def empty(n):
                    kind, u, qb = its[n]
                    bank = V_.take()
                    dve.wait_ge(V_.full, V_.taken)
                    qc = slice(128 * qb, 128 * qb + 128)
                    if kind == "s":
                        h = u % 2
                        ins = dve.tensor_copy(YA[64 * h:64 * h + 64, u // 2, qc], bank[64 * h:64 * h + 64, 0:128])
                    else:
                        ins = dve.tensor_copy(YC[:, u, qc], bank[:, 0:128])
                    vf(ins, wait=False)

                for n in range(len(its) + 3):
                    if n < len(its):
                        maxima(n)
                    if 1 <= n <= len(its):
                        normalise(n - 1)
                    if n >= 3:
                        empty(n - 3)
                c0 = C0s[l]
                dve.wait_ge(V_.free, V_.taken)
                v(dve.memset(cvec[:, 3:4], 0.0), to_act)
                for j in range(4):
                    dve.wait_ge(A.free, marks[("dfroot", l, j)])
                    v(dve.reciprocal(RS[:, 1, c0:T], RS[:, 0, c0:T]), to_act)
                    ins = STT(YC[:, j, c0:T], YC[:, j, c0:T], cvec[:, 7:8], RS[:, 1, c0:T], ALU.mult, ALU.mult)
                    v(ins, dve_step if j < 3 else to_pe_v)

            def merge(l):
                c0 = C0s[l]
                n = 0
                for b in range(3):
                    for j in range(KT):
                        dve.wait_ge(A.free, marks[("sgb", l, n)])
                        bank = V_.take()
                        dve.wait_ge(V_.full, V_.taken)
                        if b == 0:
                            vf(TT(MG[:, j, c0:T], sgb[:, n % 2, c0:T], bank[:, c0:T], ALU.mult))
                        else:
                            v(TT(mtmp[:, c0:T], sgb[:, n % 2, c0:T], bank[:, c0:T], ALU.mult))
                            vf(TT(MG[:, j, c0:T], MG[:, j, c0:T], mtmp[:, c0:T], ALU.add))
                        n += 1
                dve.wait_ge(reloaded, 16 * (l + 1))
                post(l, c0, "mix", lambda k, c: MO[:, k, c])

            def post(l, c0, which, src):
                dve.wait_ge(A.free, marks[("postroot", l, which)])
                v(dve.reciprocal(RS[:, 1, c0:T], RS[:, 0, c0:T]))
                ci = 1 if which == "mix" else 3
                for k in range(KT):
                    for s in range(c0 // SEQ, 2):
                        c = slice(SEQ * s, SEQ * s + SEQ)
                        x = src(k, c)
                        v(STT(x, x, coef[:, ci, k, s:s + 1], RS[:, 1, c], ALU.mult, ALU.mult))
                        v(TT(HT[:, k, c], HT[:, k, c], x, ALU.add), dve_step if s == 0 else h_ready)

            def ffn(l):
                for n in range(FT):
                    dve.wait_ge(A.free, marks[("silu", l, n)])
                    bank = V_.take()
                    dve.wait_ge(V_.full, V_.taken)
                    vf(TT(hid[:, n, :], htmp[:, n % 2, :], bank[:, :], ALU.mult), wait=False)
                post(l, 0, "ffn", lambda k, c: MO[:, k, c])

            def moe(l):
                bank = V_.take()
                dve.wait_ge(V_.full, V_.taken)
                v(dve.tensor_copy(rt[:, 0, 0:8], bank[:, 0:NE]))
                vf(dve.tensor_copy(rt[:, 1, 0:8], bank[:, NE:2 * NE]))
                for b in range(2):
                    r = rt[:, b, :]
                    v(dve.max(r[:, 16:24], r[:, 0:8]))
                    v(dve.max_index(rti[:, b, :], r[:, 16:24], r[:, 0:8]))
                    v(dve.tensor_copy(r[:, 24:26], rti[:, b, 0:2]))
                    v(TT(r[:, 26:27], r[:, 17:18], r[:, 16:17], ALU.subtract), lam_in)
                    dve.wait_ge(lam_out, seen(lam_out))
                    v(TS(r[:, 28:29], r[:, 27:28], 1.0, None, ALU.add))
                    v(dve.reciprocal(r[:, 29:30], r[:, 28:29]))
                    v(TT(r[:, 30:31], r[:, 29:30], r[:, 27:28], ALU.mult))
                    v(TS(r[:, 32:40], tb("iota")[:, 0:8], r[:, 24:25], None, ALU.is_equal))
                    v(TS(r[:, 40:48], tb("iota")[:, 0:8], r[:, 25:26], None, ALU.is_equal))
                    v(TS(r[:, 8:16], r[:, 32:40], r[:, 29:30], None, ALU.mult))
                    v(STT(r[:, 8:16], r[:, 40:48], r[:, 30:31], r[:, 8:16], ALU.mult, ALU.add))
                    v(TT(r[:, 48:56], r[:, 32:40], r[:, 40:48], ALU.add), dve_step if b == 0 else to_pe_v)
                for b in range(2):
                    for k4 in range(2):
                        bank = V_.take()
                        dve.wait_ge(V_.full, V_.taken)
                        vf(dve.tensor_copy(Atok[:, b, 512 * k4:512 * k4 + 512], bank[:, :]), wait=False)
                bank = V_.take()
                dve.wait_ge(V_.full, V_.taken)
                v(dve.tensor_copy(rt[:, 0, 56:64], bank[:, 0:8]))
                v(dve.tensor_copy(rt[:, 1, 56:64], bank[:, 8:16]))
                vf(dve.tensor_reduce(cvec[:, 20:21], bank[:, 16:24], AX.X, ALU.max))
                v(TS(flag[0:1, 0:1], cvec[0:1, 20:21], float(CAP), None, ALU.is_gt), flag_ready)
                experts(0, A, V_)
                crowded = dve.value_load(flag[0:1, 0:1], min_val=0, max_val=1)
                with dve.If(crowded > 0):
                    chain[0] = dve_step2
                    for b in range(2):
                        v(TS(rt[:, b, 56:64], rt[:, b, 56:64], -float(CAP), None, ALU.add))
                    experts(1, A2, V2)
                    chain[0] = dve_step
                v(dve.memset(cvec[:, 3:4], 0.0), to_act)
                post(l, SEQ, "ffn", lambda k, c: FA[:, k, :])

            def experts(p, A, V_):
                def take():
                    return V_.take()

                def emptied(ins, wait=False):
                    ins.then_inc(V_.free, 1)
                    if wait:
                        dve.wait_ge(V_.free, V_.taken)

                def select(e):
                    for b in range(2):
                        r = rt[:, b, :]
                        ins = TS(Psel[:, e % 2, b, :], tb("iota"), r[:, 56 + e:57 + e], r[:, 48 + e:49 + e],
                                 ALU.is_equal, ALU.mult)
                        v(ins, chain[0] if b == 0 else to_pe_v)

                def weigh(e):
                    for b in range(2):
                        r = rt[:, b, :]
                        v(TS(Pw[:, b, :], tb("iota"), r[:, 56 + e:57 + e], r[:, 8 + e:9 + e], ALU.is_equal, ALU.mult),
                          chain[0] if b == 0 else to_pe_v)

                def gathered(e):
                    for k4 in range(2):
                        bank = take()
                        dve.wait_ge(V_.full, V_.taken)
                        emptied(dve.tensor_copy(XE[:, e % 2, 4 * k4:4 * k4 + 4, :],
                                                bank[:, :].rearrange("p (k t) -> p k t", k=4)))

                def combined(e):
                    for k2 in range(4):
                        bank = take()
                        dve.wait_ge(V_.full, V_.taken)
                        b3 = bank[:, :].rearrange("p (k t) -> p k t", k=2)
                        x = FA[:, 2 * k2:2 * k2 + 2, :]
                        if p == 0 and e == 0:
                            emptied(dve.tensor_copy(x, b3))
                        else:
                            emptied(TT(x, x, b3, ALU.add))

                select(0)
                gathered(0)
                for e in range(NE):
                    if e < NE - 1:
                        select(e + 1)
                    for j in range(ET // 2):
                        dve.wait_ge(A.free, marks[("silu", p, e, j)])
                        bank = take()
                        dve.wait_ge(V_.full, V_.taken)
                        emptied(TT(hidm[:, 2 * j:2 * j + 2, :], htm[:, j % 2, :].rearrange("p (i t) -> p i t", i=2),
                                   bank[:, 0:2 * CAP].rearrange("p (i t) -> p i t", i=2), ALU.mult))
                        if e and j == 1:
                            combined(e - 1)
                        if j == 2:
                            weigh(e)
                    if e < NE - 1:
                        gathered(e + 1)
                    bank = take()
                    dve.wait_ge(V_.full, V_.taken)
                    emptied(dve.tensor_copy(PwT[:, e % 2, :], bank[:, 0:SEQ]))
                combined(NE - 1)
                dve.wait_ge(V_.free, V_.taken)
            for l in range(2):
                if stage(f"ada{l}"):
                    ada(l)
                    norm(l, 0, "mix")
                if stage(f"rwin{l}"):
                    recurrence_inputs(l)
                if stage(f"rwstep{l}"):
                    S.begin(("steps", l))
                    for i in range(NCH):
                        recurrence_step(l, i)
                    recurrence_output(l)
                if stage(f"attn{l}"):
                    attention_inputs(l)
                    attention(l)
                if stage(f"merge{l}"):
                    merge(l)
                if stage(f"ffn{l}"):
                    norm(l, C0s[l], "ffn")
                    (ffn if l == 0 else moe)(l)
            v(dve.memset(cvec[:, 3:4], 0.0), to_pool)
            pool_n[0] = own[to_pool.name]

        @block.gpsimd
        def _(pool):
            pool.dma_start(tab[:, :], io["tables"]).then_inc(consts_in, 16)
            pool.dma_start(vec[:, :], io["vectors"]).then_inc(consts_in, 16)
            pool.dma_start(rep[:, :, :], io["repeated"]).then_inc(consts_in, 32)
            xt = io["xt"].rearrange("(k p) t -> p k t", p=128)
            pool.dma_start(HT[:, :, :], xt).then_inc(x_in, 16)
            at_dram = at_spill.rearrange("(k p) t -> p k t", p=128)

            def spill_input(l):
                pool.wait_ge(at_ready, KT * (1 + 2 * l))
                pool.dma_start(at_dram, AT[:, :, :]).then_inc(at_spilled, 16)

            def reload_input(l):
                pool.wait_ge(at_spilled, 16 * (l + 1))
                pool.dma_start(AT[:, :, :], at_dram).then_inc(at_reloaded, 16)

            if "rwin0" in built:
                spill_input(0)
            if "rwstep0" in built:
                pool.wait_ge(to_pool, 1)
                reload_input(0)
                pool.dma_start(HT[:, :, :], xt).then_inc(reloaded, 16)
            if "rwin1" in built:
                pool.wait_ge(h_ready, 2 * KT)
                pool.dma_start(spill.rearrange("(k p) t -> p k t", p=128), HT[:, :, SEQ:T]).then_inc(spilled, 16)
                spill_input(1)
            if "rwstep1" in built:
                pool.wait_ge(spilled, 16)
                pool.wait_ge(to_pool, 2)
                reload_input(1)
                pool.dma_start(HT[:, :, SEQ:T], spill.rearrange("(k p) t -> p k t", p=128)).then_inc(reloaded, 16)
            if done[0]:
                pool.wait_ge(to_pool, pool_n[0])
                if "rwstep0" in built:
                    pool.wait_ge(at_reloaded, 16 * (1 + ("rwstep1" in built)))
                    pool.wait_ge(reloaded, 16 * (1 + ("rwstep1" in built)))
                pool.wait_ge(act_step, 1)
                env = dict(HT=HT, AT=AT, YA=YA, YB=YB, YC=YC, ar=ar, mods=mods, coef=coef, cvec=cvec)
                for name, dst in (dbg or {}).items():
                    pool.dma_start(dst, env[name][:, :, :]).then_inc(stored, 16)
                pool.wait_ge(stored, 16 * len(dbg or {}))
                return
            pool.wait_ge(h_ready, 4 * KT)
            pool.dma_start(out.rearrange("(k p) t -> p k t", p=128), HT[:, :, SEQ:T]).then_inc(stored, 16)
            pool.wait_ge(stored, 16)

        @block.sync
        def _(sp):
            def load(W, count):
                for n in range(count):
                    if n >= SLOTS:
                        s, value = W.released[n - SLOTS]
                        sp.wait_ge(s, value)
                    for at, src in W.chunks[n]:
                        size = src.shape[1] * src.shape[2]
                        dst = WR[:, n % SLOTS, at:at + size].rearrange("p (k n) -> p k n", k=src.shape[1])
                        sp.dma_start(dst, src).then_inc(W.sems[n % SLOTS], 16)

            load(W, W.arrived)
            if not done[0]:
                sp.wait_ge(flag_ready, 1)
                crowded = sp.value_load(flag[0:1, 0:1], min_val=0, max_val=1)
                with sp.If(crowded > 0):
                    sp.wait_ge(*W.released[-1])
                    load(W2, W2.arrived)


NAMES = ["w_in", "ada_w", "rwkv_w_up", "rwkv_a_up", "rwkv_g_up", "proj_swa", "proj_rwkv", "proj_diff", "w_out",
         "ffn_w_gate", "ffn_w_up", "ffn_w_down", "router_w", "moe_w_gate", "moe_w_up", "moe_w_down"]


def layout(inputs):
    a = {n: np.ascontiguousarray(inputs[n]) for n in NAMES}
    f = np.float32
    cols = lambda x: np.asarray(x, f).reshape(-1, 128).T
    vs = []
    for l in range(2):
        for n in ("pre_mix_g", "post_mix_g", "pre_ffn_g", "post_ffn_g", "ada_b", "rwkv_mu_prev", "rwkv_mu_next",
                  "rwkv_w0", "rwkv_a0", "rwkv_k_k", "rwkv_k_a", "rwkv_r_k", "rwkv_lnx_g", "rwkv_lnx_b",
                  "diff_subln_g"):
            vs.append(cols(inputs[n][l]))
    cc = np.stack([cols(inputs["c_ctx"]), cols(inputs["c"])], 2).reshape(128, 16)
    a["vectors"] = np.ascontiguousarray(np.concatenate(vs + [cc], 1))
    rep = np.concatenate([np.asarray(inputs["swa_sink"], f), np.asarray(inputs["diff_lambda"], f).reshape(2, 256)], 1)
    a["repeated"] = np.ascontiguousarray(np.broadcast_to(rep[None], (128, 2, 264)))
    a["xt"] = np.ascontiguousarray(np.concatenate([np.asarray(inputs["ctx"][0]).T, np.asarray(inputs["x"][0]).T], 1))
    a["tables"] = tables()
    return a


def kernel(**inputs):
    import concourse.bacc as bacc
    from concourse.bass_utils import run_bass_kernel_spmd

    nc = bacc.Bacc("TRN2", target_bir_lowering=False, num_devices=1)
    arrays = layout(inputs)
    io = {n: nc.dram_tensor("in_" + n, a.shape, mybir.dt.float32, kind="ExternalInput").ap() for n, a in arrays.items()}
    out = nc.dram_tensor("result", (D, SEQ), mybir.dt.float32, kind="ExternalOutput").ap()
    trunk(nc, io, out)
    r = run_bass_kernel_spmd(nc, [{"in_" + n: a for n, a in arrays.items()}], core_ids=[0])
    return np.ascontiguousarray(r.results[0]["result"].T)[None]
```

```python
import math
from contextlib import ExitStack

import numpy as np

import concourse.bass as bass
from concourse import mybir

D = 1024
T = 512
SEQ = 256
KT = D // 128
HD = 64
CH = 64
NCH = T // CH
FF = 2816
FT = FF // 128
EF = 3584
ET = EF // 128
NE = 8
SW_COLS, RW_COLS, DF_COLS = 768, 1920, 1536
C_RW = SW_COLS
C_DF = SW_COLS + RW_COLS
C_GATE = C_DF + DF_COLS
RT_TILES = RW_COLS // 128
KAPPA = math.exp(-0.5)
BWD = [3, 2, 1, 0, 7, 6, 5, 4]
NEG = -1e30

VEC = {}
_at = 0
for _n, _w in [("pre_mix", 8), ("post_mix", 8), ("pre_ffn", 8), ("post_ffn", 8), ("ada_b", 48), ("mu_p", 15),
               ("mu_n", 15), ("w0", 8), ("a0", 8), ("k_k", 4), ("k_a", 4), ("r_k", 4), ("ln_g", 4), ("ln_b", 4),
               ("subln", 1)]:
    VEC[_n] = (_at, _w)
    _at += _w
VEC_L = _at


def tables():
    f = np.float32
    n = np.arange(SEQ)
    row, col = (n // 64).astype(f), (n % 64).astype(f)
    inv = (np.float32(10000.0) ** (-np.arange(0, 32, 2, dtype=f) / f(32))).astype(f)
    cosT, sinT = np.zeros((128, SEQ), f), np.zeros((128, SEQ), f)
    perm, swap = np.zeros((128, 128), f), np.zeros((128, 128), f)
    for p in range(128):
        q = p % 64
        axis, half, i = q // 32, (q % 32) // 16, q % 16
        ang = ((row if axis == 0 else col) * inv[i]).astype(f)
        cosT[p], sinT[p] = np.cos(ang), np.sin(ang)
        if half == 0:
            perm[p + 16, p] = -1.0
        else:
            perm[p - 16, p] = 1.0
        swap[(p + 64) % 128, p] = 1.0
    eye = np.eye(128, dtype=f)
    blk = np.kron(np.eye(2), np.full((64, 64), 1 / 64)).astype(f)
    r, c = np.arange(128)[:, None], np.arange(128)[None, :]
    band = np.concatenate([np.where(c <= r, 0, NEG), np.where(c >= r, 0, NEG)], 1).astype(f)
    r, c = (np.arange(128) % 64)[:, None], np.arange(64)[None, :]
    later = [lambda a, b: a > b, lambda a, b: a < b]
    two = lambda g: np.stack([g(0), g(1)], 1).astype(f)
    masks = [two(lambda d: later[d](c, r)), two(lambda d: later[d](c, r) | (c == r))]
    for m in (1, 2, 4, 8, 16, 32):
        masks.append(two(lambda d: (r // (2 * m) == c // (2 * m)) & (r // m != c // m) & later[d](r, c)))
    masks.append(two(lambda d: (r // 2 == c // 2) & later[d](c, r)))
    masks.append(two(lambda d: (r == c)))
    masks = np.stack(masks, 1).reshape(128, -1)
    return np.concatenate([eye, perm, swap, blk, np.ones((128, 128), f), cosT, sinT, band, masks,
                           np.broadcast_to(np.arange(128, dtype=f), (128, 128)),
                           np.triu(np.ones((128, 128), f), 1)], 1)


TAB = {}
_at = 0
for _n, _w in [("eye", 128), ("perm", 128), ("swap", 128), ("blk", 128), ("ones", 128), ("cos", 256), ("sin", 256),
               ("band", 256), ("masks", 10 * 128), ("iota", 128),
               ("tri", 128)]:
    TAB[_n] = (_at, _w)
    _at += _w
TAB_W = _at
M_STRICT_T, M_INCL_T, M_LEVEL, M_PAIR_T, M_EYE = 0, 1, 2, 8, 9


class Ring:

    def __init__(self, banks, full, free):
        self.banks, self.full, self.free = banks, full, free
        self.made = self.taken = self.due = 0
        self.jobs = {}
        self.starts = {}

    def start(self, name):
        self.starts[name] = self.made

    def begin(self, name):
        self.taken = self.starts[name]

    def claim(self):
        self.due = max(0, self.made - len(self.banks) + 1)
        return self.banks[self.made % len(self.banks)]

    def done(self, name=None):
        self.made += 1
        self.jobs[name] = self.made

    def take(self):
        self.taken += 1
        return self.banks[(self.taken - 1) % len(self.banks)]


class Stream:

    def __init__(self, chunks, sems, slots):
        self.chunks, self.sems, self.slots = chunks, sems, slots
        self.in_count = []
        total = [0] * len(sems)
        for n, parts in enumerate(chunks):
            total[n % len(sems)] += 16 * len(parts)
            self.in_count.append(total[n % len(sems)])
        self.arrived = 0
        self.released = []

    def landed(self):
        return self.sems[self.arrived % len(self.sems)], self.in_count[self.arrived]

    def arrive(self):
        self.arrived += 1
        return self.slots[:, (self.arrived - 1) % len(self.sems), :]

    def release(self, ring):
        self.released.append((ring.full, ring.made))


class Seen:

    def __init__(self):
        self.n = {}

    def __call__(self, sem, k=1):
        self.n[sem.name] = self.n.get(sem.name, 0) + k
        return self.n[sem.name]


def trunk(nc, io, out):
    f32 = mybir.dt.float32
    u32 = mybir.dt.uint32
    ALU = mybir.AluOpType
    ACT = mybir.ActivationFunctionType
    AX = mybir.AxisListType

    ctx = ExitStack()
    with ctx:
        def sb(name, shape, dt=f32):
            return ctx.enter_context(nc.sbuf_tensor(name, shape, dt))

        def sem(name):
            return ctx.enter_context(nc.semaphore(name))

        HT = sb("HT", [128, KT, T])
        AT = sb("AT", [128, KT, T])
        SLOTS, SLOT = 3, 4096
        WR = sb("WR", [128, SLOTS, SLOT])
        YA = sb("YA", [128, 4, T])
        YB = sb("YB", [128, 4, T])
        YC = sb("YC", [128, 4, T])
        tab = sb("tab", [128, TAB_W])
        vec = sb("vec", [128, 2 * VEC_L + 16])
        rep = sb("rep", [128, 2, 8 + 256])
        mods = sb("mods", [128, 48, 2])
        coef = sb("coef", [128, 4, KT, 2])
        silc = sb("silc", [128, KT, 2])
        muc = sb("muc", [128, RT_TILES])
        cvec = sb("cvec", [128, 32])
        sink8, cv2 = cvec[:, 8:16], cvec[:, 16:20]
        st = sb("st", [128, 4, 2, 4])
        RS = sb("RS", [128, 2, T])
        eS = sb("eS", [128, 2, 2, 8])
        rt = sb("rt", [128, 2, 64])
        rti = sb("rti", [128, 2, 8], u32)
        flag = sb("flag", [1, 1], mybir.dt.int32)
        AR_W = 21100
        ar = sb("ar", [128, AR_W])

        def V(l, name, i=None):
            a, w = VEC[name]
            a += l * VEC_L
            return vec[:, a:a + w] if i is None else vec[:, a + i:a + i + 1]

        def tb(name):
            a, w = TAB[name]
            return tab[:, a:a + w]

        eye, perm, swap, blk, ones = tb("eye"), tb("perm"), tb("swap"), tb("blk"), tb("ones")
        masks = tb("masks").rearrange("p (m d c) -> p m d c", m=10, d=2)

        def area(at, n, w=T):
            return ar[:, at:at + n * w].rearrange("p (n w) -> p n w", n=n)

        Rr, Rk, Rv, Rkk = area(0, 4), area(2048, 4), area(4096, 4), area(6144, 4)
        Ra = ar[:, 8192:12288].rearrange("p (d j t) -> p d j t", d=2, j=4)
        CW = CH + 1
        Rc = ar[:, 12288:12288 + 2 * 4 * NCH * CW].rearrange("p (d j c w) -> p d j c w", d=2, j=4, c=NCH)
        TR0 = 12288 + 2 * 4 * NCH * CW
        HTf = HT[:, :, :].rearrange("p k t -> p (k t)")
        ATf = AT[:, :, :].rearrange("p k t -> p (k t)")
        YBf = YB[:, :, :].rearrange("p j t -> p (j t)")
        tail = [ar[:, TR0 + i * 512:TR0 + i * 512 + 512] for i in range(8)]
        tr = {n: HTf[:, i * 1024:i * 1024 + 1024] for i, n in enumerate(("aa", "ba", "ka", "LT"))}
        tr.update({n: ATf[:, i * 1024:i * 1024 + 1024] for i, n in enumerate(("X", "XT", "T1", "bt"))})
        tr.update({n: ar[:, TR0 + i * 1024:TR0 + i * 1024 + 1024] for i, n in enumerate(("kt", "vt", "MT"))})
        tr["ra0"], tr["tmp"] = tail[6:8]
        tr.update({n: YBf[:, i * 512:i * 512 + 512] for i, n in enumerate(("ra1", "G", "RBT", "RKT"))})
        tr["S"] = RS[:, :, :].rearrange("p i t -> p (i t)")
        tr["E10"], tr["E11"], tr["E2"], tr["E3"] = tr["ra0"], tr["ra1"], tail[4], tail[5]
        tr["U"] = tr["X"]
        CC = ar[:, TR0 + 8 * 512:TR0 + 8 * 512 + 8 * CW].rearrange("p (q w) -> p q w", q=8)
        assert TR0 + 8 * 512 + 8 * CW <= AR_W
        tmpT = [HTf[:, i * 512:i * 512 + 512] for i in range(3, 7)] + tail[0:5]
        tmpO = tail[0:2]
        thw, wdin, adin, gdin = tmpT[4:8]
        sgd = thw
        thw1, adin1 = tmpT[0:2]
        sgt = [HTf[:, 0:512], HTf[:, 512:1024]]
        onesw = HTf[:, 1024:1024 + CH]
        rowb = area(0, 2)
        Qs, Qd = area(0, 4), area(2048, 4)
        Ks = area(4096, 2)
        Kd = area(5120, 4)
        Vt = area(7168, 4, 640)
        Pb = ar[:, 9728:9728 + 2048].rearrange("p (i c t) -> p i c t", i=2, c=2)
        PTb = area(11776, 2)
        rtmp = area(12800, 2)
        SQd = area(13824, 4)
        Q1s, Q1d = area(15872, 4), area(17920, 4)
        rope_tiles = [Qs[:, j, :] for j in range(4)] + [Ks[:, 0, :]] + [Qd[:, j, :] for j in range(4)] + \
                     [Kd[:, j, :] for j in range(4)]
        MG = area(0, KT)
        MO = area(4096, KT)
        SQ = area(8192, KT)
        sgb = area(12288, 2)
        mtmp = ar[:, 13312:13824]
        hid = area(8192, FT)
        CAP = 128
        hidm = area(8192, ET, CAP)
        FA = area(11776, KT, SEQ)
        Atok = area(13824, 2, D)
        XE = ar[:, 15872:17920].rearrange("p (i k t) -> p i k t", i=2, k=KT)
        Psel = ar[:, 17920:18432].rearrange("p (i b t) -> p i b t", i=2, b=2)
        Pw = area(18432, 2, CAP)
        PwT = area(18688, 2, SEQ)
        htm = area(19200, 2, 256)
        Ysb = ar[:, 19712:20736]
        htmp = area(19456, 2)

        banks = [ctx.enter_context(nc.psum_tensor(f"bank{i}", [128, 512], f32))[:, :] for i in range(8)]
        A = Ring(banks[0:3], sem("a_full"), sem("a_free"))
        V_ = Ring(banks[3:6], sem("v_full"), sem("v_free"))
        S = Ring(banks[6:8], sem("s_full"), sem("s_free"))

        A2 = Ring(banks[0:3], sem("a2_full"), sem("a2_free"))
        V2 = Ring(banks[3:6], sem("v2_full"), sem("v2_free"))
        S2 = Ring(banks[6:8], sem("s2_full"), sem("s2_free"))

        flag_ready = sem("flag_ready")
        dve_step2 = sem("dve_step2")
        down_step = [sem("down_step_0"), sem("down_step_1")]
        w_in = [sem(f"weights_in_{i}") for i in range(SLOTS)]
        vectors_in, consts_in = sem("vectors_in"), sem("consts_in")
        x_in = sem("x_in")
        spilled = sem("residual_spilled")
        reloaded = sem("residual_reloaded")
        at_spilled, at_reloaded = sem("input_spilled"), sem("input_reloaded")
        g_spilled, g_reloaded = sem("recurrence_gate_spilled"), sem("recurrence_gate_reloaded")
        stored = sem("stored")
        silc_ready = sem("silc_ready")
        coef_ready = sem("coef_ready")
        h_ready = sem("h_ready")
        sq_ready = sem("sq_ready")
        at_scaled = sem("at_scaled")
        at_ready = sem("at_ready")
        dve_step = sem("dve_step")
        to_pe_a = sem("act_to_pe")
        to_pe_v = sem("vector_to_pe")
        to_act = sem("vector_to_act")
        to_dve = sem("act_to_vector")
        lam_in, lam_out = sem("exponent_ready"), sem("exponential_ready")
        to_pool = sem("vector_to_pool")
        p_ready = sem("p_ready")
        m_ready = sem("m_ready")
        es_ready = sem("es_ready")

        chunks = []

        def kxn(w, cols):
            return w.rearrange("(k p) n -> p k n", p=128)[:, :, cols]

        def chunk(*parts):
            at, res = 0, []
            for src in parts:
                n = src.shape[1] * src.shape[2]
                res.append((at, src))
                at += n
            assert at <= SLOT
            chunks.append(res)

        for l in range(2):
            wi = io["w_in"][l]
            for j in range(12):
                chunk(kxn(io["ada_w"][l], slice(512 * j, 512 * j + 512)))
            for j in range(4):
                chunk(kxn(wi, slice(C_RW + 512 * j, C_RW + min(512 * j + 512, RW_COLS))))
            small = lambda a: a.rearrange("p (o n) -> p o n", o=1)
            chunk(small(io["rwkv_w_up"][l].rearrange("d r n -> (d r) n")),
                  small(io["rwkv_a_up"][l].rearrange("d r n -> (d r) n")), small(io["rwkv_g_up"][l]))
            chunk(kxn(wi, slice(0, 512)))
            chunk(kxn(wi, slice(512, 768)))
            for j in range(3):
                chunk(kxn(wi, slice(C_DF + 512 * j, C_DF + 512 * j + 512)))
            for b, w in enumerate(("proj_swa", "proj_rwkv", "proj_diff")):
                chunk(kxn(wi, slice(C_GATE + D * b, C_GATE + D * b + 512)))
                chunk(kxn(io[w][l], slice(0, D)))
                chunk(kxn(wi, slice(C_GATE + D * b + 512, C_GATE + D * b + D)))
            for j in range(2):
                chunk(kxn(io["w_out"][l], slice(512 * j, 512 * j + 512)))
            if l == 0:
                for j in range(FT // 2):
                    c = slice(256 * j, 256 * j + 256)
                    chunk(kxn(io["ffn_w_gate"][0], c), kxn(io["ffn_w_up"][0], c))
                for j in range(KT):
                    chunk(kxn(io["ffn_w_down"][0], slice(128 * j, 128 * j + 128)))
            else:
                chunk(kxn(io["router_w"][0], slice(0, NE)))
                first_moe = len(chunks)
                for e in range(NE):
                    for j in range(ET // 2):
                        c = slice(256 * j, 256 * j + 256)
                        chunk(kxn(io["moe_w_gate"][0, e], c), kxn(io["moe_w_up"][0, e], c))
                    for j in range(ET // 4):
                        rows = slice(512 * j, 512 * j + 512)
                        chunk(kxn(io["moe_w_down"][0, e, rows, :], slice(0, D)))

        W = Stream(chunks, w_in, WR)
        W2 = Stream(chunks[first_moe:], [sem(f"overflow_weights_in_{i}") for i in range(SLOTS)], WR)
        landed, arrive, release = W.landed, W.arrive, W.release

        C0s = (0, SEQ)
        LAM = [0.8 - 0.6 * math.exp(-0.3 * l) for l in range(2)]
        hq = [(q, h) for q in range(8) for h in range(2)]

        def pair(x, q, h):
            return x[64 * h:64 * h + 64, 64 * q:64 * q + 64]

        def wide(x, q):
            return x[:, 128 * q:128 * q + 128]

        def head_block(x, q, h):
            return x[64 * h:64 * h + 64, 128 * q + 64 * h:128 * q + 64 * h + 64]

        def head_blocks(x, h, q0, q1):
            return x.rearrange("p (q w) -> p q w", w=128)[64 * h:64 * h + 64, q0:q1, 64 * h:64 * h + 64]

        def items(l):
            qbs = range(2 if l else 0, 4)
            return ([("s", u, qb) for u in range(8) for qb in qbs] + [("d", h, qb) for h in range(4) for qb in qbs])

        both = ((0, V_), (1, S))
        marks = {}

        at_spill = nc.dram_tensor("input_spill", (D, T), f32, kind="Internal").ap()
        g_spill = nc.dram_tensor("recurrence_gate_spill", (512, T), f32, kind="Internal").ap()
        spill = nc.dram_tensor("residual_spill", (D, SEQ), f32, kind="Internal").ap()
        block = ctx.enter_context(nc.Block())

        @block.tensor
        def _(pe):
            seen = Seen()
            pe.wait_ge(vectors_in, 16)

            def mm(o, lhsT, rhs, first, last):
                return pe.matmul(o, lhsT, rhs, start=first, stop=last)

            def ada(l):
                if l == 0:
                    pe.wait_ge(silc_ready, seen(silc_ready))
                jobs = []

                def turn(j):
                    if l == 0 and j == 0:
                        pe.wait_ge(consts_in, 32)
                    pe.wait_ge(A.free, jobs[j])
                    bank = V_.claim()
                    pe.wait_ge(V_.free, V_.due)
                    for i in range(4):
                        last = pe.transpose(bank[:, 2 * i:2 * i + 2], rowb[0:2, j % 2, 128 * i:128 * i + 128],
                                            eye[0:2, 0:2])
                    last.then_inc(V_.full, 1)
                    V_.done(("turn", l, j))

                for j in range(12):
                    pe.wait_ge(*landed())
                    w = arrive().rearrange("p (k n) -> p k n", k=KT)
                    bank = A.claim()
                    pe.wait_ge(A.free, A.due)
                    for k in range(KT):
                        last = mm(bank[0:2, :], silc[:, k, :], w[:, k, :], k == 0, k == KT - 1)
                    last.then_inc(A.full, 1)
                    A.done()
                    release(A)
                    jobs.append(A.made)
                    if j:
                        turn(j - 1)
                turn(11)

            def squares_sum(l, n, c0, src, wait):
                bank = A.claim()
                pe.wait_ge(A.free, A.due)
                for k in range(n):
                    wait(k)
                    last = mm(bank[:, c0:T], ones, src[:, k, c0:T], k == 0, k == n - 1)
                last.then_inc(A.full, 1)
                A.done()

            def feature_major(w, n_tiles, c0, ring, tag, src=None, first=False):
                for i in range(n_tiles):
                    bank = ring.claim()
                    pe.wait_ge(ring.free, ring.due)
                    for k in range(KT):
                        if first and i == 0:
                            pe.wait_ge(at_ready, seen(at_ready))
                        last = mm(bank[:, c0:T], w[:, k, 128 * i:128 * i + 128], (AT if src is None else src)[:, k, c0:T], k == 0,
                                  k == KT - 1)
                    last.then_inc(ring.full, 1)
                    ring.done((tag, i))

            def recurrence_inputs(l):
                for j in range(4):
                    n = 4 if j < 3 else 3
                    pe.wait_ge(*landed())
                    w = arrive()[:, 0:KT * 128 * n].rearrange("p (k n) -> p k n", k=KT)
                    feature_major(w, n, 0, V_, ("rw", l, j), first=(j == 0))
                    release(V_)
                    if j == 2:
                        for m in range(4):
                            pe.wait_ge(to_pe_v, seen(to_pe_v))
                            bank = A.claim()
                            pe.wait_ge(A.free, A.due)
                            last = mm(bank, blk, tmpT[m], True, True)
                            last.then_inc(A.full, 1)
                            A.done(("kknorm", l, m))
                pe.wait_ge(*landed())
                up = arrive()[:, 0:3 * 512].rearrange("p (i n) -> p i n", i=3)
                pe.wait_ge(to_pe_a, seen(to_pe_a))
                for d in range(2):
                    for j in range(4):
                        bank = A.claim()
                        pe.wait_ge(A.free, A.due)
                        last = mm(bank, up[:, 0, 128 * j:128 * j + 128], (thw, thw1)[d], True, True)
                        last.then_inc(A.full, 1)
                        A.done(("decay", l, d, j))
                pe.wait_ge(V_.free, V_.jobs[(("rw", l, 3), 2)])
                for d in range(2):
                    for j in range(4):
                        bank = A.claim()
                        pe.wait_ge(A.free, A.due)
                        last = mm(bank, up[:, 1, 128 * j:128 * j + 128], (adin, adin1)[d], True, True)
                        last.then_inc(A.full, 1)
                        A.done(("rate", l, d, j))
                pe.wait_ge(to_pe_a, seen(to_pe_a))
                for j in range(4):
                    bank = A.claim()
                    pe.wait_ge(A.free, A.due)
                    last = mm(bank, up[:, 2, 128 * j:128 * j + 128], sgd, True, True)
                    last.then_inc(A.full, 1)
                    A.done()
                release(A)

            def products(ring, terms, d, name=None):
                bank = ring.claim()
                pe.wait_ge(ring.free, ring.due)
                for q in range(4):
                    for n, (lhs, rhs) in enumerate(terms):
                        last = mm(wide(bank, q), wide(lhs, 4 * d + q), wide(rhs, 4 * d + q), n == 0,
                                  n == len(terms) - 1)
                last.then_inc(ring.full, 1)
                ring.done(name)

            def narrow_products(ring, terms, d, name=None):
                bank = ring.claim()
                pe.wait_ge(ring.free, ring.due)
                for q, h in hq[8 * d:8 * d + 8]:
                    for n, (lhs, rhs) in enumerate(terms):
                        last = mm(pair(bank, q, h), head_block(lhs, q, h), pair(rhs, q, h), n == 0, n == len(terms) - 1)
                last.then_inc(ring.full, 1)
                ring.done(name)

            def transposes(lhs):
                for d in range(2):
                    bank = A.claim()
                    pe.wait_ge(A.free, A.due)
                    for q in range(4):
                        last = mm(wide(bank, q), wide(lhs, 4 * d + q), eye, True, True)
                    last.then_inc(A.full, 1)
                    A.done()

            def recurrence_step(l, i):
                y = not (l == 1 and i < 4)
                ra = tr["ra" + str(i % 2)]
                pe.wait_ge(to_pe_v, seen(to_pe_v))
                for d, ring in both:
                    products(ring, [(tr["aa"], tr["ba"])], d)
                for d, ring in both:
                    products(ring, [(tr["ba"], tr["aa"])], d, ("LT", l, i, d))
                bank = A.claim()
                pe.wait_ge(A.free, A.due)
                for q, h in hq:
                    c = CH * (i if q < 4 else BWD[i])
                    last = mm(pair(bank, q, h), Rv[64 * h:64 * h + 64, q % 4, c:c + CH],
                              eye[64 * h:64 * h + 64, 64 * h:64 * h + 64], True, True)
                last.then_inc(A.full, 1)
                A.done(("vt", l, i))
                for d, ring in both:
                    products(ring, [(tr["ka"], tr["aa"])], d, ("MT", l, i, d))
                transposes(tr["ba"])
                transposes(tr["ka"])
                if y:
                    for d, ring in both:
                        narrow_products(ring, [(tr["ba"], ra)], d)
                    for d, ring in both:
                        narrow_products(ring, [(tr["ka"], ra)], d)
                pe.wait_ge(A.free, A.jobs[("vt", l, i)])
                for d, ring in both:
                    pe.wait_ge(ring.free, ring.jobs[("MT", l, i, d)])
                    products(A, [(tr["aa"], tr["S"]), (tr["MT"], tr["vt"])], d, ("G", l, i, d))
                for n in range(5):
                    for d, ring in both:
                        pe.wait_ge(ring.free, ring.jobs[("XT", l, i, d, n - 1) if n else ("LT", l, i, d)])
                        products(ring, [(tr["LT"], tr["X"])], d, ("T1", l, i, d, n))
                    if n == 1 and i < 4:
                        pe.wait_ge(to_pe_v, seen(to_pe_v))
                        bank = V_.claim()
                        pe.wait_ge(V_.free, V_.due)
                        last = mm(bank, blk, tr["tmp"], True, True)
                        last.then_inc(V_.full, 1)
                        V_.done(("bonus", l, i))
                    for d, ring in both:
                        pe.wait_ge(ring.free, ring.jobs[("T1", l, i, d, n)])
                        if n < 4:
                            products(ring, [(tr["XT"], tr["T1"])], d)
                        products(ring, [(tr["T1"], tr["XT"])], d, ("XT", l, i, d, n))
                for d, ring in both:
                    pe.wait_ge(ring.free, ring.jobs[("XT", l, i, d, 4)])
                    pe.wait_ge(A.free, A.jobs[("G", l, i, d)])
                    narrow_products(A, [(tr["XT"], tr["G"])], d, ("U", l, i, d))
                for d, ring in both:
                    pe.wait_ge(A.free, A.jobs[("U", l, i, d)])
                    if y:
                        narrow_products(ring, [(tr["S"], ra), (tr["U"], tr["RBT"]), (tr["vt"], tr["RKT"])], d)
                for d, ring in both:
                    products(ring, [(tr["bt"], tr["U"]), (tr["kt"], tr["vt"])], d)

            def recurrence_output(l):
                c0 = C0s[l]
                for what in ("mean", "var"):
                    for j in range(4):
                        pe.wait_ge(to_pe_v, seen(to_pe_v))
                        ring = V_ if what == "mean" else A
                        bank = ring.claim()
                        pe.wait_ge(ring.free, ring.due)
                        src = YA[:, j, c0:T] if what == "mean" else tmpO[j % 2][:, c0:T]
                        last = mm(bank[:, c0:T], blk, src, True, True)
                        last.then_inc(ring.full, 1)
                        ring.done(("gn" + what, l, j))

            def rope(l, tiles):
                for n, x in enumerate(tiles):
                    bank = V_.claim()
                    pe.wait_ge(V_.free, V_.due)
                    last = mm(bank[:, 0:SEQ], perm, x[:, SEQ:T], True, True)
                    last.then_inc(V_.full, 1)
                    V_.done(("rope", l, n))

            def attention_inputs(l):
                c0 = C0s[l]
                w8 = lambda w, n: w[:, 0:KT * n].rearrange("p (k n) -> p k n", k=KT)
                pe.wait_ge(at_reloaded, 16 * (l + 1))
                pe.wait_ge(*landed())
                feature_major(w8(arrive(), 512), 4, c0, A, ("qs", l))
                release(A)
                pe.wait_ge(*landed())
                w = w8(arrive(), 256)
                feature_major(w, 1, 0, A, ("ks", l))
                bank = V_.claim()
                pe.wait_ge(V_.free, V_.due)
                for b in range(4):
                    for k in range(KT):
                        last = mm(bank[:, 128 * b:128 * b + 128], AT[:, k, 128 * b:128 * b + 128], w[:, k, 128:256],
                                  k == 0, k == KT - 1)
                last.then_inc(V_.full, 1)
                V_.done()
                release(V_)
                pe.wait_ge(*landed())
                feature_major(w8(arrive(), 512), 4, c0, A, ("qd", l))
                release(A)
                pe.wait_ge(*landed())
                feature_major(w8(arrive(), 512), 4, 0, A, ("kd", l))
                release(A)
                pe.wait_ge(*landed())
                w = w8(arrive(), 512)
                for b in range(4):
                    bank = V_.claim()
                    pe.wait_ge(V_.free, V_.due)
                    for k in range(KT):
                        last = mm(bank, AT[:, k, 128 * b:128 * b + 128], w[:, k, :], k == 0, k == KT - 1)
                    last.then_inc(V_.full, 1)
                    V_.done()
                release(V_)
                pe.wait_ge(A.free, A.jobs[(("kd", l), 3)])
                rope(l, rope_tiles)
                pe.wait_ge(V_.free, V_.jobs[("rope", l, 4)])
                bank = A.claim()
                pe.wait_ge(A.free, A.due)
                last = mm(bank, swap, Ks[:, 0, :], True, True)
                last.then_inc(A.full, 1)
                A.done(("k2", l))
                pe.wait_ge(A.free, A.jobs[("k2", l)])
                pe.wait_ge(to_pe_v, seen(to_pe_v))

            def attention(l):
                its = items(l)

                def scores(n):
                    kind, u, qb = its[n]
                    nk = SEQ if qb < 2 else T
                    qc = slice(128 * qb, 128 * qb + 128)
                    for c in range(1 if kind == "s" else 2):
                        h = u % 2 if kind == "s" else c
                        q = (Qs, Q1s)[h][:, u // 2, qc] if kind == "s" else (Qd, Q1d)[h][:, u, qc]
                        k = Ks[:, 0 if u // 4 == h else 1, 0:nk] if kind == "s" else Kd[:, u, 0:nk]
                        bank = S.claim()
                        pe.wait_ge(S.free, S.due)
                        last = mm(bank[:, 0:nk], q, k, True, True)
                        last.then_inc(S.full, 1)
                        S.done(("sc", l, n, c))

                def turn(n):
                    kind, u, qb = its[n]
                    pe.wait_ge(p_ready, seen(p_ready))
                    bank = A.claim()
                    pe.wait_ge(A.free, A.due)
                    for b in range(2 if qb < 2 else 4):
                        last = pe.transpose(bank[:, 128 * b:128 * b + 128], Pb[:, n % 2, 0, 128 * b:128 * b + 128], eye)
                    last.then_inc(A.full, 1)
                    A.done(("pt", l, n))

                def values(n):
                    kind, u, qb = its[n]
                    pe.wait_ge(A.free, A.jobs[("pt", l, n)])
                    bank = V_.claim()
                    pe.wait_ge(V_.free, V_.due)
                    nb = 2 if qb < 2 else 4
                    for b in range(nb):
                        if kind == "s":
                            h, g = u % 2, u // 4
                            last = mm(bank[64 * h:64 * h + 64, 0:128], Vt[:, b, 64 * g:64 * g + 64],
                                      PTb[:, n % 2, 128 * b:128 * b + 128], b == 0, b == nb - 1)
                        else:
                            last = mm(bank[:, 0:128], Vt[:, b, 128 + 128 * u:256 + 128 * u],
                                      PTb[:, n % 2, 128 * b:128 * b + 128], b == 0, b == nb - 1)
                    last.then_inc(V_.full, 1)
                    V_.done(("pv", l, n))

                scores(0)
                for n in range(len(its) + 2):
                    if n + 1 < len(its) and its[n + 1][0] == "s":
                        scores(n + 1)
                    if 1 <= n <= len(its):
                        turn(n - 1)
                    if n + 1 < len(its) and its[n + 1][0] == "d":
                        scores(n + 1)
                    if n >= 2:
                        values(n - 2)
                for j in range(4):
                    pe.wait_ge(to_pe_a, seen(to_pe_a))
                    bank = A.claim()
                    pe.wait_ge(A.free, A.due)
                    last = mm(bank[:, C0s[l]:T], ones, SQd[:, j, C0s[l]:T], True, True)
                    last.then_inc(A.full, 1)
                    A.done()

            def merge(l):
                c0 = C0s[l]
                pe.wait_ge(V_.free, V_.made)
                for b, y in enumerate((YA, YB, YC)):
                    if b == 2:
                        pe.wait_ge(to_pe_v, seen(to_pe_v))
                    pe.wait_ge(*landed())
                    g = arrive().rearrange("p (k n) -> p k n", k=KT)
                    pe.wait_ge(*landed())
                    p = arrive().rearrange("p (k n) -> p k n", k=4)
                    for j in range(KT):
                        if j == 4:
                            release(V_)
                            pe.wait_ge(*landed())
                            g = arrive().rearrange("p (k n) -> p k n", k=KT)
                        bank = A.claim()
                        pe.wait_ge(A.free, A.due)
                        for k in range(KT):
                            last = mm(bank[:, c0:T], g[:, k, 128 * (j % 4):128 * (j % 4) + 128], AT[:, k, c0:T],
                                      k == 0, k == KT - 1)
                        last.then_inc(A.full, 1)
                        A.done()
                        bank = V_.claim()
                        pe.wait_ge(V_.free, V_.due)
                        for k in range(4):
                            last = mm(bank[:, c0:T], p[:, k, 128 * j:128 * j + 128], y[:, k, c0:T], k == 0, k == 3)
                        last.then_inc(V_.full, 1)
                        V_.done(("merge", l, b, j))
                    release(V_)
                    release(V_)
                pe.wait_ge(V_.free, V_.jobs[("merge", l, 2, KT - 1)])
                for j in range(2):
                    pe.wait_ge(*landed())
                    w = arrive().rearrange("p (k n) -> p k n", k=KT)
                    feature_major(w, 4, c0, A, ("wo", l, j), src=MG)
                    release(A)
                squares_sum(l, KT, c0, SQ, lambda k: pe.wait_ge(A.free, A.jobs[(("wo", l, k // 4), k % 4)]))

            def norm(c0):
                squares_sum(0, KT, c0, AT, lambda k: pe.wait_ge(sq_ready, seen(sq_ready)))

            def ffn(l):
                for j in range(FT // 2):
                    pe.wait_ge(*landed())
                    w = arrive().rearrange("p (g k n) -> p g k n", g=2, k=KT)
                    for i in range(2):
                        for g, ring in enumerate((A, V_)):
                            bank = ring.claim()
                            pe.wait_ge(ring.free, ring.due)
                            for k in range(KT):
                                if (j, i, g) == (0, 0, 0):
                                    pe.wait_ge(at_ready, seen(at_ready))
                                last = mm(bank, w[:, g, k, 128 * i:128 * i + 128], AT[:, k, :], k == 0, k == KT - 1)
                            last.then_inc(ring.full, 1)
                            ring.done(("hid", l, 2 * j + i))
                    release(V_)
                pe.wait_ge(V_.free, V_.jobs[("hid", l, FT - 1)])
                for j in range(KT):
                    pe.wait_ge(*landed())
                    w = arrive()[:, 0:FT * 128].rearrange("p (k n) -> p k n", k=FT)
                    bank = A.claim()
                    pe.wait_ge(A.free, A.due)
                    for k in range(FT):
                        last = mm(bank, w[:, k, :], hid[:, k, :], k == 0, k == FT - 1)
                    last.then_inc(A.full, 1)
                    A.done(("dn", l, j))
                    release(A)
                squares_sum(l, KT, 0, AT, lambda k: pe.wait_ge(A.free, A.jobs[("dn", l, k)]))

            def moe(l):
                pe.wait_ge(at_ready, seen(at_ready, KT))
                pe.wait_ge(*landed())
                w = arrive()[:, 0:KT * NE].rearrange("p (k n) -> p k n", k=KT)
                bank = V_.claim()
                pe.wait_ge(V_.free, V_.due)
                for b in range(2):
                    for k in range(KT):
                        last = mm(bank[:, NE * b:NE * b + NE], AT[:, k, SEQ + 128 * b:SEQ + 128 * b + 128], w[:, k, :],
                                  k == 0, k == KT - 1)
                last.then_inc(V_.full, 1)
                V_.done()
                release(V_)
                for b in range(2):
                    for k4 in range(2):
                        bank = V_.claim()
                        pe.wait_ge(V_.free, V_.due)
                        for k in range(4):
                            last = pe.transpose(bank[:, 128 * k:128 * k + 128],
                                                AT[:, 4 * k4 + k, SEQ + 128 * b:SEQ + 128 * b + 128], eye)
                        last.then_inc(V_.full, 1)
                        V_.done()
                pe.wait_ge(to_pe_v, seen(to_pe_v))
                sel = [rt[:, b, 48:56] for b in range(2)]
                bank = V_.claim()
                pe.wait_ge(V_.free, V_.due)
                mm(bank[:, 0:8], tb("tri"), sel[0], True, True)
                mm(bank[:, 8:16], ones, sel[0], True, False)
                mm(bank[:, 8:16], tb("tri"), sel[1], False, True)
                mm(bank[:, 16:24], ones, sel[0], True, False)
                last = mm(bank[:, 16:24], ones, sel[1], False, True)
                last.then_inc(V_.full, 1)
                V_.done()
                experts(0, A, V_, S, W)
                pe.wait_ge(flag_ready, 1)
                crowded = pe.value_load(flag[0:1, 0:1], min_val=0, max_val=1)
                with pe.If(crowded > 0):
                    pe.wait_ge(A.free, A.made)
                    pe.wait_ge(V_.free, V_.made)
                    pe.wait_ge(S.free, S.made)
                    experts(1, A2, V2, S2, W2)
                    pe.wait_ge(A2.free, A2.made)
                    pe.wait_ge(V2.free, V2.made)
                    pe.wait_ge(S2.free, S2.made)
                bank = A.claim()
                pe.wait_ge(A.free, A.due)
                for k in range(KT):
                    pe.wait_ge(sq_ready, seen(sq_ready))
                    last = mm(bank[:, SEQ:T], ones, AT[:, k, SEQ:T], k == 0, k == KT - 1)
                last.then_inc(A.full, 1)
                A.done()

            def experts(p, A, V_, S, W):
                def gather(e):
                    pe.wait_ge(to_pe_v, seen(to_pe_v))
                    for k4 in range(2):
                        bank = V_.claim()
                        pe.wait_ge(V_.free, V_.due)
                        for k in range(4):
                            for b in range(2):
                                c = 128 * (4 * k4 + k)
                                last = mm(bank[:, 128 * k:128 * k + 128], Atok[:, b, c:c + 128],
                                          Psel[:, e % 2, b, :], b == 0, b == 1)
                        last.then_inc(V_.full, 1)
                        V_.done(("gather", p, e))

                def turn(e):
                    bank = V_.claim()
                    pe.wait_ge(V_.free, V_.due)
                    for b in range(2):
                        last = pe.transpose(bank[:, 128 * b:128 * b + 128], Pw[:, b, :], eye)
                    last.then_inc(V_.full, 1)
                    V_.done(("pwt", p, e))

                def combine(e):
                    pe.wait_ge(S.free, S.jobs[("y", p, e)])
                    pe.wait_ge(V_.free, V_.jobs[("pwt", p, e)])
                    for k2 in range(4):
                        bank = V_.claim()
                        pe.wait_ge(V_.free, V_.due)
                        for k in range(2):
                            c = 128 * (2 * k2 + k)
                            last = mm(bank[:, SEQ * k:SEQ * k + SEQ], Ysb[:, c:c + 128], PwT[:, e % 2, :], True, True)
                        last.then_inc(V_.full, 1)
                        V_.done(("combine", p, e))

                gather(0)
                for e in range(NE):
                    pe.wait_ge(V_.free, V_.jobs[("gather", p, e)])
                    for j in range(ET // 2):
                        pe.wait_ge(*W.landed())
                        w = W.arrive().rearrange("p (g k n) -> p g k n", g=2, k=KT)
                        for g, ring in enumerate((A, V_)):
                            bank = ring.claim()
                            pe.wait_ge(ring.free, ring.due)
                            for i in range(2):
                                for k in range(KT):
                                    last = mm(bank[:, CAP * i:CAP * i + CAP], w[:, g, k, 128 * i:128 * i + 128],
                                              XE[:, e % 2, k, :], k == 0, k == KT - 1)
                            last.then_inc(ring.full, 1)
                            ring.done(("hid", p, e, j))
                        W.release(V_)
                        if e and j == 1:
                            combine(e - 1)
                    if e < NE - 1:
                        gather(e + 1)
                    pe.wait_ge(to_pe_v, seen(to_pe_v))
                    turn(e)
                    pe.wait_ge(V_.free, V_.jobs[("hid", p, e, ET // 2 - 1)])
                    ys = []
                    for h in range(2):
                        ys.append(S.banks[(S.made + h) % 2])
                        pe.wait_ge(S.free, max(0, S.made + h - 1))
                    for j in range(ET // 4):
                        pe.wait_ge(*W.landed())
                        w = W.arrive().rearrange("p (k n) -> p k n", k=4)
                        for k in range(4):
                            f_ = 4 * j + k
                            for h in range(2):
                                last = mm(ys[h], hidm[:, f_, :], w[:, k, 512 * h:512 * h + 512], f_ == 0, f_ == ET - 1)
                                if f_ == ET - 1:
                                    last.then_inc(S.full, 1)
                                    S.done(("y", p, e))
                        if j < ET // 4 - 1:
                            last.then_inc(down_step[p], 1)
                            W.released.append((down_step[p], (ET // 4 - 1) * e + j + 1))
                        else:
                            W.release(S)
                combine(NE - 1)
            for l in range(2):
                ada(l)
                norm(0)
                recurrence_inputs(l)
                S.start(("steps", l))
                for i in range(NCH):
                    recurrence_step(l, i)
                recurrence_output(l)
                attention_inputs(l)
                S.start(("scores", l))
                attention(l)
                merge(l)
                norm(C0s[l])
                (ffn if l == 0 else moe)(l)

        @block.scalar
        def _(act):
            seen = Seen()
            act.dma_start(vec[:, :], io["vectors"]).then_inc(vectors_in, 16)
            act.dma_start(tab[:, :], io["tables"]).then_inc(consts_in, 16)
            act.dma_start(rep[:, :, :], io["repeated"]).then_inc(consts_in, 16)
            act.dma_start(HT[:, :, :], io["xt"].rearrange("(k p) t -> p k t", p=128)).then_inc(x_in, 16)
            act.wait_ge(vectors_in, 16)
            act.wait_ge(coef_ready, 1)
            own = {}

            def a(ins, s, wait=False):
                own[s.name] = own.get(s.name, 0) + 1
                ins.then_inc(s, 1)
                if wait:
                    act.wait_ge(s, own[s.name])

            def f(out, in_, func, **k):
                return act.activation(out, in_, func, **k)

            def free(ins, name=None):
                ins.then_inc(A.free, 1)
                if name is not None:
                    marks[name] = A.taken

            a(f(silc[:, :, :].rearrange("p k s -> p (k s)"), vec[:, 2 * VEC_L:2 * VEC_L + 16], ACT.Silu), silc_ready)

            def ada(l):
                for j in range(12):
                    bank = A.take()
                    act.wait_ge(A.full, A.taken)
                    if j >= 2:
                        act.wait_ge(V_.full, V_.jobs[("turn", l, j - 2)])
                    free(f(rowb[0:2, j % 2, :], bank[0:2, :], ACT.Copy))

            def root(c0, n, eps_col, name):
                bank = A.take()
                act.wait_ge(A.full, A.taken)
                free(f(RS[:, 0, c0:T], bank[:, c0:T], ACT.Sqrt, scale=1.0 / n, bias=cvec[:, eps_col:eps_col + 1]), name)

            def norm(l, c0, which):
                if l == 0 and which == "mix":
                    act.wait_ge(x_in, 16)
                    act.wait_ge(consts_in, 32)
                for k in range(KT):
                    if l or which == "ffn":
                        act.wait_ge(h_ready, seen(h_ready))
                    a(f(AT[:, k, c0:T], HT[:, k, c0:T], ACT.Square), sq_ready)
                root(c0, D, 0, ("root", l, which))
                for k in range(KT):
                    for s in range(c0 // SEQ, 2):
                        act.wait_ge(at_scaled, seen(at_scaled))
                        ins = f(AT[:, k, SEQ * s:SEQ * s + SEQ], AT[:, k, SEQ * s:SEQ * s + SEQ], ACT.Identity,
                                bias=mods[:, (0 if which == "mix" else 24) + k, s:s + 1])
                    a(ins, at_ready)

            def recurrence_inputs(l):
                if l:
                    act.wait_ge(spilled, 16)
                for j in range(4):
                    bank = A.take()
                    act.wait_ge(A.full, A.taken)
                    if j:
                        act.wait_ge(to_act, seen(to_act))
                    free(f(RS[:, 0, :], bank[:, :], ACT.Sqrt, scale=64.0), ("kkroot", l, j))
                act.wait_ge(to_act, seen(to_act))
                act.wait_ge(V_.free, V_.jobs[(("rw", l, 3), 0)])
                f(thw[0:64, :], wdin[0:64, :], ACT.Tanh)
                a(f(thw1[64:128, :], wdin[64:128, :], ACT.Tanh), to_pe_a)
                for d in range(2):
                    for j in range(4):
                        bank = A.take()
                        act.wait_ge(A.full, A.taken)
                        n = 4 * d + j
                        if n >= 2:
                            act.wait_ge(to_act, seen(to_act))
                        free(f(sgt[n % 2], bank[:, :], ACT.Sigmoid, bias=V(l, "w0", n)), ("sg", l, n))
                for d in range(2):
                    for j in range(4):
                        bank = A.take()
                        act.wait_ge(A.full, A.taken)
                        n = 4 * d + j
                        free(f(Ra[:, d, j, :], bank[:, :], ACT.Sigmoid, bias=V(l, "a0", n)), ("rate", l, n))
                act.wait_ge(V_.free, V_.jobs[(("rw", l, 3), 2)])
                a(f(sgd, gdin, ACT.Sigmoid), to_pe_a)
                act.wait_ge(to_act, seen(to_act, 2))
                marks[("sgd", l)] = own[to_pe_a.name]
                decays(l, 0)
                for j in range(4):
                    bank = A.take()
                    act.wait_ge(A.full, A.taken)
                    free(f(YB[:, j, :], bank[:, :], ACT.Copy), ("g", l, j))

            def decays(l, i):
                act.wait_ge(to_act, seen(to_act))
                for d in range(2):
                    qs = slice(4 * d, 4 * d + 4)
                    inc = slice(1, CW) if d == 0 else slice(0, CH)
                    exc = slice(0, CH) if d == 0 else slice(1, CW)
                    v = lambda n: tr[n].rearrange("p (q w) -> p q w", q=8)[:, qs, :]
                    f(v("E1" + str(i % 2)), CC[:, qs, inc], ACT.Exp, scale=-KAPPA)
                    f(v("E2"), CC[:, qs, exc], ACT.Exp, scale=-KAPPA)
                    f(v("E3"), CC[:, qs, inc], ACT.Exp, scale=KAPPA)
                    c = i if d == 0 else BWD[i]
                    f(eS[:, i % 2, 0, qs], Rc[:, d, :, c, 32], ACT.Exp, scale=-KAPPA)
                    e = CH if d == 0 else 0
                    ins = f(eS[:, i % 2, 1, qs], CC[:, qs, e], ACT.Exp, scale=-KAPPA)
                a(ins, to_dve)

            def recurrence_step(l, i):
                bank = A.take()
                act.wait_ge(A.full, A.taken)
                for h in range(2):
                    ins = f(head_blocks(tr["vt"], h, 0, 8), bank[64 * h:64 * h + 64, :].rearrange("p (q w) -> p q w", q=8),
                            ACT.Copy)
                free(ins)
                for n in ("bt", "kt"):
                    for d in range(2):
                        bank = A.take()
                        act.wait_ge(A.full, A.taken)
                        free(f(tr[n][:, 512 * d:512 * d + 512], bank[:, :], ACT.Copy))
                if i == 0:
                    act.wait_ge(g_spilled, 16 * (l + 1))
                for d in range(2):
                    bank = A.take()
                    act.wait_ge(A.full, A.taken)
                    g = tr["G"].rearrange("p (q w) -> p q w", q=8)
                    for h in range(2):
                        ins = f(g[64 * h:64 * h + 64, 4 * d:4 * d + 4, :], head_blocks(bank, h, 0, 4), ACT.Copy)
                    free(ins)
                if i < NCH - 1:
                    decays(l, i + 1)
                for d in range(2):
                    bank = A.take()
                    act.wait_ge(A.full, A.taken)
                    u = bank[:, 256 * d:256 * d + 256].rearrange("p (q w) -> p q w", q=4)
                    for h in range(2):
                        ins = f(head_blocks(tr["U"], h, 4 * d, 4 * d + 4), u[64 * h:64 * h + 64, :, :], ACT.Copy)
                    free(ins)

            def recurrence_output(l):
                c0 = C0s[l]
                for j in range(4):
                    bank = A.take()
                    act.wait_ge(A.full, A.taken)
                    if j:
                        act.wait_ge(to_act, seen(to_act))
                    free(f(RS[:, 0, c0:T], bank[:, c0:T], ACT.Sqrt, bias=cvec[:, 1:2]), ("gnroot", l, j))
                act.wait_ge(to_act, seen(to_act))

            def attention_inputs(l):
                c0 = C0s[l]
                for dst, c in [(Qs[:, j, :], c0) for j in range(4)] + [(Ks[:, 0, :], 0)] + \
                              [(Qd[:, j, :], c0) for j in range(4)] + [(Kd[:, j, :], 0) for j in range(4)]:
                    bank = A.take()
                    act.wait_ge(A.full, A.taken)
                    free(f(dst[:, c:T], bank[:, c:T], ACT.Copy))
                bank = A.take()
                act.wait_ge(A.full, A.taken)
                free(f(Ks[:, 1, :], bank[:, :], ACT.Copy))
                for q0, q1, n in ((Qs, Q1s, 3), (Qd, Q1d, 8)):
                    act.wait_ge(V_.free, V_.jobs[("rope", l, n)])
                    a(f(q1[64:128, :, c0:T], q0[64:128, :, c0:T], ACT.Copy), to_dve)
                act.wait_ge(lam_in, seen(lam_in))
                a(f(cvec[:, 4:6], cvec[:, 4:6], ACT.Exp), lam_out)

            def attention(l):
                its = items(l)
                for n in range(len(its) + 1):
                    if n < len(its):
                        kind, u, qb = its[n]
                        nk = SEQ if qb < 2 else T
                        for c in range(1 if kind == "s" else 2):
                            bank = S.take()
                            act.wait_ge(S.full, S.taken)
                            act.wait_ge(m_ready, seen(m_ready))
                            if n >= 2:
                                act.wait_ge(A.full, A.jobs[("pt", l, n - 2)])
                            f(Pb[:, n % 2, c, 0:nk], bank[:, 0:nk], ACT.Exp, scale=HD ** -0.5,
                              bias=st[:, n % 4, c, 1:2], accum_out=st[:, n % 4, c, 2:3]).then_inc(S.free, 1)
                            marks[("exp", l, n, c)] = S.taken
                        if kind == "s":
                            a(f(st[:, n % 4, 0, 3:4], st[:, n % 4, 0, 1:2], ACT.Exp, bias=rep[:, l, u:u + 1]),
                              es_ready)
                    if n >= 1:
                        kind, u, qb = its[n - 1]
                        nk = SEQ if qb < 2 else T
                        bank = A.take()
                        act.wait_ge(A.full, A.taken)
                        if n >= 3:
                            act.wait_ge(V_.full, V_.jobs[("pv", l, n - 3)])
                        free(f(PTb[:, (n - 1) % 2, 0:nk], bank[:, 0:nk], ACT.Copy))
                c0 = C0s[l]
                for j in range(4):
                    if j == 0:
                        act.wait_ge(to_act, seen(to_act))
                    a(f(SQd[:, j, c0:T], YC[:, j, c0:T], ACT.Square), to_pe_a)
                for j in range(4):
                    bank = A.take()
                    act.wait_ge(A.full, A.taken)
                    if j:
                        act.wait_ge(to_act, seen(to_act))
                    free(f(RS[:, 0, c0:T], bank[:, c0:T], ACT.Sqrt, scale=1.0 / 128, bias=cvec[:, 2:3]),
                         ("dfroot", l, j))
                act.wait_ge(to_act, seen(to_act))

            def merge(l):
                c0 = C0s[l]
                n = 0
                for b in range(3):
                    for j in range(KT):
                        bank = A.take()
                        act.wait_ge(A.full, A.taken)
                        if n >= 2:
                            act.wait_ge(V_.free, V_.jobs[("merge", l, (n - 2) // KT, (n - 2) % KT)])
                        free(f(sgb[:, n % 2, c0:T], bank[:, c0:T], ACT.Sigmoid), ("sgb", l, n))
                        n += 1
                copies(l, c0, SQ, "mix")

            def copies(l, c0, sq, which):
                for k in range(KT):
                    bank = A.take()
                    act.wait_ge(A.full, A.taken)
                    f(MO[:, k, c0:T], bank[:, c0:T], ACT.Copy)
                    free(f(sq[:, k, c0:T], bank[:, c0:T], ACT.Square))
                root(c0, D, 0, ("postroot", l, which))

            def ffn(l):
                for n in range(FT):
                    bank = A.take()
                    act.wait_ge(A.full, A.taken)
                    if n >= 2:
                        act.wait_ge(V_.free, V_.jobs[("hid", l, n - 2)])
                    free(f(htmp[:, n % 2, :], bank[:, :], ACT.Silu), ("silu", l, n))
                copies(l, 0, AT, "ffn")

            def moe(l):
                for b in range(2):
                    act.wait_ge(lam_in, seen(lam_in))
                    a(f(rt[:, b, 27:28], rt[:, b, 26:27], ACT.Exp), lam_out)
                experts(0, A, V_, S)
                act.wait_ge(flag_ready, 1)
                crowded = act.value_load(flag[0:1, 0:1], min_val=0, max_val=1)
                with act.If(crowded > 0):
                    experts(1, A2, V2, S2)
                act.wait_ge(to_act, seen(to_act))
                for k in range(KT):
                    a(f(AT[:, k, SEQ:T], FA[:, k, :], ACT.Square), sq_ready)
                root(SEQ, D, 0, ("postroot", l, "ffn"))

            def experts(p, A, V_, S):
                for e in range(NE):
                    for j in range(ET // 2):
                        bank = A.take()
                        act.wait_ge(A.full, A.taken)
                        m = e * (ET // 2) + j - 2
                        if m >= 0:
                            act.wait_ge(V_.free, V_.jobs[("hid", p, m // (ET // 2), m % (ET // 2))])
                        f(htm[:, j % 2, :], bank[:, 0:2 * CAP], ACT.Silu).then_inc(A.free, 1)
                        marks[("silu", p, e, j)] = A.taken
                    if e:
                        act.wait_ge(V_.full, V_.jobs[("combine", p, e - 1)])
                    for h in range(2):
                        bank = S.take()
                        act.wait_ge(S.full, S.taken)
                        f(Ysb[:, 512 * h:512 * h + 512], bank[:, :], ACT.Copy).then_inc(S.free, 1)
            for l in range(2):
                ada(l)
                norm(l, 0, "mix")
                recurrence_inputs(l)
                for i in range(NCH):
                    recurrence_step(l, i)
                recurrence_output(l)
                attention_inputs(l)
                S.begin(("scores", l))
                attention(l)
                merge(l)
                norm(l, C0s[l], "ffn")
                (ffn if l == 0 else moe)(l)


        @block.vector
        def _(dve):
            seen = Seen()
            own = {}

            chain = [dve_step]

            def v(ins, s=None, wait=True):
                s = s or chain[0]
                own[s.name] = own.get(s.name, 0) + 1
                ins.then_inc(s, 1)
                if wait:
                    dve.wait_ge(s, own[s.name])

            def vf(ins, wait=True):
                ins.then_inc(V_.free, 1)
                if wait:
                    dve.wait_ge(V_.free, V_.taken)

            TT, TS, STT = dve.tensor_tensor, dve.tensor_scalar, dve.scalar_tensor_tensor
            dve.wait_ge(vectors_in, 16)
            v(dve.memset(cvec[:, 0:1], 1e-6))
            v(dve.memset(cvec[:, 1:2], 64e-5))
            v(dve.memset(cvec[:, 2:3], 1e-5), coef_ready)
            dve.wait_ge(consts_in, 32)
            dve.wait_ge(x_in, 16)

            def ada(l):
                for j in range(12):
                    bank = V_.take()
                    dve.wait_ge(V_.full, V_.taken)
                    vf(TT(mods[:, 4 * j:4 * j + 4, :], bank[:, 0:8].rearrange("p (i s) -> p i s", s=2),
                          V(l, "ada_b")[:, 4 * j:4 * j + 4].unsqueeze(2).to_broadcast([128, 4, 2]), ALU.add))
                for n, (m, g, add) in enumerate(((8, "pre_mix", 1.0), (16, "post_mix", 0.0), (32, "pre_ffn", 1.0),
                                                 (40, "post_ffn", 0.0))):
                    v(STT(coef[:, n, :, :], mods[:, m:m + 8, :], add,
                          V(l, g).unsqueeze(2).to_broadcast([128, 8, 2]), ALU.add, ALU.mult))

            def norm(l, c0, which):
                dve.wait_ge(A.free, marks[("root", l, which)])
                v(dve.reciprocal(RS[:, 1, c0:T], RS[:, 0, c0:T]))
                ci = 0 if which == "mix" else 2
                for k in range(KT):
                    for s in range(c0 // SEQ, 2):
                        c = slice(SEQ * s, SEQ * s + SEQ)
                        v(STT(AT[:, k, c], HT[:, k, c], coef[:, ci, k, s:s + 1], RS[:, 1, c], ALU.mult, ALU.mult),
                          at_scaled, wait=False)

            def recurrence_inputs(l):
                if l:
                    dve.wait_ge(spilled, 16)
                v(TT(muc[:, :], V(l, "mu_p"), V(l, "mu_n"), ALU.add))
                v(TS(muc[:, :], muc[:, :], -1.0, 1.0, ALU.mult, ALU.add))
                dst = [Rr[:, j, :] for j in range(4)] + [Rk[:, j, :] for j in range(4)] + \
                      [Rv[:, j, :] for j in range(4)] + [wdin, adin, gdin]
                for n in range(RT_TILES):
                    bank = V_.take()
                    dve.wait_ge(V_.full, V_.taken)
                    x = dst[n]
                    v(TS(x, bank[:, :], muc[:, n:n + 1], None, ALU.mult))
                    x2 = x.rearrange("p (s t) -> p s t", s=2)
                    b2 = bank[:, :].rearrange("p (s t) -> p s t", s=2)
                    v(STT(x2[:, :, 1:SEQ], b2[:, :, 0:SEQ - 1], V(l, "mu_p", n), x2[:, :, 1:SEQ], ALU.mult, ALU.add))
                    vf(STT(x2[:, :, 0:SEQ - 1], b2[:, :, 1:SEQ], V(l, "mu_n", n), x2[:, :, 0:SEQ - 1], ALU.mult,
                           ALU.add))
                    if n == 7:
                        for j in range(4):
                            v(TS(Rkk[:, j, :], Rk[:, j, :], V(l, "k_k", j), None, ALU.mult))
                            v(TT(tmpT[j], Rkk[:, j, :], Rkk[:, j, :], ALU.mult), to_pe_v)
                    if n == 13:
                        v(dve.tensor_copy(adin1[64:128, :], adin[64:128, :]))
                        v(dve.memset(adin[64:128, :], 0.0), wait=False)
                        v(dve.memset(adin1[0:64, :], 0.0), wait=False)
                    if n >= 11:
                        j = n - 11
                        dve.wait_ge(A.free, marks[("kkroot", l, j)])
                        v(TS(RS[:, 1, :], RS[:, 0, :], 1e-12, None, ALU.max), to_act)
                        v(dve.reciprocal(RS[:, 1, :], RS[:, 1, :]))
                        v(TT(Rkk[:, j, :], Rkk[:, j, :], RS[:, 1, :], ALU.mult))
                        if j == 0:
                            v(dve.memset(thw[64:128, :], 0.0), wait=False)
                            v(dve.memset(thw1[0:64, :], 0.0), wait=False)
                v(dve.memset(onesw, 1.0))
                v(dve.memset(YA[:, :, :], 0.0))
                for d in range(2):
                    v(dve.memset(Rc[:, d, :, :, 0 if d == 0 else CH], 0.0))
                for n in range(8):
                    d, j = n // 4, n % 4
                    dve.wait_ge(A.free, marks[("sg", l, n)])
                    sg = sgt[n % 2]
                    for c in range(NCH):
                        lo, hi = CH * c, CH * c + CH
                        if d == 0:
                            o, i_ = Rc[:, d, j, c, 1:CW], sg[:, lo:hi]
                        else:
                            o, i_ = Rc[:, d, j, c, CH - 1::-1], (sg[:, hi - 1:lo - 1:-1] if lo else sg[:, hi - 1::-1])
                        ins = dve.tensor_tensor_scan(o, onesw, i_, 0.0, ALU.mult, ALU.add)
                        if c < NCH - 1:
                            v(ins, wait=False)
                        else:
                            v(ins, to_act)
                dve.wait_ge(A.free, marks[("rate", l, 7)])
                v(TS(cv2, V(l, "k_a"), -2.0, 2.0, ALU.mult, ALU.add))

            def bonus_in(l, j):
                t = tr["tmp"]
                v(TT(t, Ra[:, 0, j, :], Ra[:, 1, j, :], ALU.add))
                v(TS(t, t, V(l, "k_a", j), cv2[:, j:j + 1], ALU.mult, ALU.add))
                v(TT(t, t, Rk[:, j, :], ALU.mult))
                v(STT(t, t, V(l, "r_k", j), Rr[:, j, :], ALU.mult, ALU.mult), to_pe_v)

            def bonus_out(j):
                bank = V_.take()
                dve.wait_ge(V_.full, V_.taken)
                STT(YC[:, j, :], bank[:, :], 64.0, Rv[:, j, :], ALU.mult, ALU.mult).then_inc(V_.free, 1)

            def chunks_of(i):
                return i, BWD[i]

            def centre(l, i):
                for d in range(2):
                    c = chunks_of(i)[d]
                    ins = TT(CC[:, 4 * d:4 * d + 4, :], Rc[:, d, :, c, :],
                             Rc[:, d, :, c, 32:33].to_broadcast([128, 4, CW]), ALU.subtract)
                    v(ins, dve_step if d == 0 else to_act)

            def operands(l, i):
                y = not (l == 1 and i < 4)
                dve.wait_ge(to_dve, seen(to_dve))
                ka = V(l, "k_a").unsqueeze(2).to_broadcast([128, 4, CH])
                for d in range(2):
                    c = slice(CH * chunks_of(i)[d], CH * chunks_of(i)[d] + CH)
                    qs = slice(4 * d, 4 * d + 4)
                    g = lambda n: tr[n].rearrange("p (q w) -> p q w", q=8)[:, qs, :]
                    kb, bb = (tr["tmp"][:, 256 * k:256 * k + 256].rearrange("p (q w) -> p q w", q=4) for k in (0, 1))
                    v(STT(kb, Ra[:, d, :, c], -1.0, ka, ALU.add, ALU.mult), wait=False)
                    v(TT(bb, Rkk[:, :, c], Ra[:, d, :, c], ALU.mult))
                    v(STT(kb, kb, 1.0, Rk[:, :, c], ALU.add, ALU.mult))
                    if y:
                        e1 = g("E1" + str(i % 2))
                        v(TT(e1, Rr[:, :, c], e1, ALU.mult), wait=False)
                    for h in range(2):
                        ps = slice(64 * h, 64 * h + 64)
                        o = lambda n: head_blocks(tr[n], h, 4 * d, 4 * d + 4)
                        v(STT(o("aa"), Rkk[ps, :, c], -1.0, g("E2")[ps, :, :], ALU.mult, ALU.mult), wait=False)
                        v(TT(o("ba"), bb[ps, :, :], g("E3")[ps, :, :], ALU.mult), wait=False)
                        last = (d, h) == (1, 1)
                        v(TT(o("ka"), kb[ps, :, :], g("E3")[ps, :, :], ALU.mult), to_pe_v if last else dve_step,
                          wait=not last and h == 1)

            def recurrence_step(l, i):
                y = not (l == 1 and i < 4)
                mk = lambda m, d: masks[:, m, d, :].unsqueeze(1).to_broadcast([128, 8, 64])
                eyes = eye.unsqueeze(1).to_broadcast([128, 4, 128])

                def half(x, d):
                    return x[:, 512 * d:512 * d + 512]

                def b64(x):
                    return x.rearrange("p (q w) -> p q w", w=64)

                def b128(x):
                    return x.rearrange("p (q w) -> p q w", w=128)

                def masked(n, m):
                    for d, ring in both:
                        bank = ring.take()
                        dve.wait_ge(ring.full, ring.taken)
                        TT(b64(half(tr[n], d)), b64(bank[:, :]), mk(m, d), ALU.mult).then_inc(ring.free, 1)

                def masked_narrow(n, m):
                    for d, ring in both:
                        bank = ring.take()
                        dve.wait_ge(ring.full, ring.taken)
                        c = slice(256 * d, 256 * d + 256)
                        TT(b64(tr[n][:, c]), b64(bank[:, c]), mk(m, d)[:, 0:4, :], ALU.mult).then_inc(ring.free, 1)

                if i == 0:
                    dve.wait_ge(at_spilled, 16 * (l + 1))
                    centre(l, 0)
                    for n in ("aa", "ba", "ka", "S"):
                        v(dve.memset(tr[n], 0.0), wait=False)
                    dve.wait_ge(to_pe_a, marks[("sgd", l)])
                    v(dve.memset(tr["vt"], 0.0))
                    operands(l, 0)
                for d, ring in both:
                    bank = ring.take()
                    dve.wait_ge(ring.full, ring.taken)
                    x = half(tr["X"], d)
                    v(TT(b64(x), b64(bank[:, :]), mk(M_LEVEL, d), ALU.mult))
                    TT(b128(x), b128(x), eyes, ALU.add).then_inc(ring.free, 1)
                for d, ring in both:
                    bank = ring.take()
                    dve.wait_ge(ring.full, ring.taken)
                    x = half(tr["XT"], d)
                    v(TT(b64(x), b64(bank[:, :]), mk(M_PAIR_T, d), ALU.mult))
                    v(TT(b128(x), b128(x), eyes, ALU.add), wait=False)
                    TT(b64(half(tr["LT"], d)), b64(bank[:, :]), mk(M_STRICT_T, d), ALU.mult).then_inc(ring.free, 1)
                masked("MT", M_STRICT_T)
                if i == 0:
                    dve.wait_ge(g_spilled, 16 * (l + 1))
                if y:
                    masked_narrow("RBT", M_INCL_T)
                    masked_narrow("RKT", M_INCL_T)
                if i < NCH - 1:
                    centre(l, i + 1)
                if i < 4:
                    bonus_in(l, i)
                for n in range(5):
                    masked("T1", M_LEVEL + 1 + n)
                    if n == 1 and i < 4:
                        bonus_out(i)
                    for d, ring in both:
                        if n < 4:
                            bank = ring.take()
                            dve.wait_ge(ring.full, ring.taken)
                            TT(half(tr["X"], d), bank[:, :], half(tr["X"], d), ALU.add).then_inc(ring.free, 1)
                        bank = ring.take()
                        dve.wait_ge(ring.full, ring.taken)
                        TT(half(tr["XT"], d), bank[:, :], half(tr["XT"], d), ALU.add).then_inc(ring.free, 1)
                if i < NCH - 1:
                    operands(l, i + 1)
                if y:
                    for d, ring in both:
                        c = slice(CH * chunks_of(i)[d], CH * chunks_of(i)[d] + CH)
                        bank = ring.take()
                        dve.wait_ge(ring.full, ring.taken)
                        TT(YA[:, :, c], b64(bank[:, 256 * d:256 * d + 256]), YA[:, :, c], ALU.add).then_inc(ring.free, 1)
                if i < NCH - 1:
                    v(TT(eS[:, i % 2, 1, :], eS[:, i % 2, 1, :], eS[:, (i + 1) % 2, 0, :], ALU.mult))
                for d, ring in both:
                    bank = ring.take()
                    dve.wait_ge(ring.full, ring.taken)
                    TT(half(tr["S"], d), bank[:, :], half(tr["S"], d), ALU.add).then_inc(ring.free, 1)
                    if i < NCH - 1:
                        dve.wait_ge(ring.free, ring.taken)
                        v(TT(b128(half(tr["S"], d)), b128(half(tr["S"], d)),
                             eS[:, i % 2, 1, 4 * d:4 * d + 4].unsqueeze(2).to_broadcast([128, 4, 128]), ALU.mult),
                          wait=False)

            def recurrence_output(l):
                c0 = C0s[l]
                dve.wait_ge(V_.free, V_.taken)
                dve.wait_ge(S.free, S.taken)
                v(dve.memset(cvec[:, 3:4], 0.0), to_pool)
                for j in range(4):
                    v(dve.memset(cvec[:, 3:4], 0.0), to_pe_v)
                for j in range(4):
                    bank = V_.take()
                    dve.wait_ge(V_.full, V_.taken)
                    vf(TT(YA[:, j, c0:T], YA[:, j, c0:T], bank[:, c0:T], ALU.subtract))
                for j in range(4):
                    if j >= 2:
                        dve.wait_ge(A.full, A.jobs[("gnvar", l, j - 2)])
                    v(TT(tmpO[j % 2][:, c0:T], YA[:, j, c0:T], YA[:, j, c0:T], ALU.mult), to_pe_v)
                dve.wait_ge(g_reloaded, 16 * (l + 1))
                for j in range(4):
                    y = YA[:, j, c0:T]
                    dve.wait_ge(A.free, marks[("gnroot", l, j)])
                    v(dve.reciprocal(RS[:, 1, c0:T], RS[:, 0, c0:T]), to_act)
                    v(TT(y, y, RS[:, 1, c0:T], ALU.mult))
                    v(TS(y, y, V(l, "ln_g", j), V(l, "ln_b", j), ALU.mult, ALU.add))
                    v(TT(y, y, YC[:, j, c0:T], ALU.add))
                    v(TT(YB[:, j, c0:T], y, YB[:, j, c0:T], ALU.mult))

            def attention_inputs(l):
                bank = V_.take()
                dve.wait_ge(V_.full, V_.taken)
                vf(dve.tensor_copy(Vt[:, :, 0:128], bank[:, :].rearrange("p (b n) -> p b n", b=4)), wait=False)
                for b in range(4):
                    bank = V_.take()
                    dve.wait_ge(V_.full, V_.taken)
                    vf(dve.tensor_copy(Vt[:, b, 128:640], bank[:, :]), wait=False)
                cs, sn = tb("cos"), tb("sin")
                for n, x in enumerate(rope_tiles):
                    bank = V_.take()
                    dve.wait_ge(V_.full, V_.taken)
                    v(TT(rtmp[:, 0, 0:SEQ], bank[:, 0:SEQ], sn, ALU.mult))
                    v(TT(x[:, SEQ:T], x[:, SEQ:T], cs, ALU.mult))
                    vf(TT(x[:, SEQ:T], x[:, SEQ:T], rtmp[:, 0, 0:SEQ], ALU.add))
                for q0, q1, s in ((Qs, Q1s, dve_step), (Qd, Q1d, to_pe_v)):
                    v(dve.memset(q1[0:64, :, C0s[l]:T], 0.0), wait=False)
                    dve.wait_ge(to_dve, seen(to_dve))
                    v(dve.memset(q0[64:128, :, C0s[l]:T], 0.0), s)
                lv = rep[:, l, 8:264].rearrange("p (i n) -> p i n", i=4)
                for i in range(2):
                    v(TT(rtmp[:, 1, 0:64], lv[:, 2 * i, :], lv[:, 2 * i + 1, :], ALU.mult))
                    v(dve.tensor_reduce(cvec[:, 4 + i:5 + i], rtmp[:, 1, 0:64], AX.X, ALU.add))
                v(TS(sink8, rep[:, l, 0:8], HD ** 0.5, None, ALU.mult))
                v(TS(cvec[:, 7:8], V(l, "subln", 0), 1.0 - LAM[l], None, ALU.mult), lam_in)

            def attention(l):
                its = items(l)
                dve.wait_ge(lam_out, seen(lam_out))
                v(STT(cvec[:, 6:7], cvec[:, 4:5], LAM[l], cvec[:, 5:6], ALU.add, ALU.subtract))

                def maxima(n):
                    kind, u, qb = its[n]
                    nk = SEQ if qb < 2 else T
                    for c in range(1 if kind == "s" else 2):
                        dve.wait_ge(S.full, S.jobs[("sc", l, n, c)])
                        bank = S.banks[(S.jobs[("sc", l, n, c)] - 1) % 2]
                        if kind == "s" and qb >= 2:
                            k0 = 384 if qb == 2 else 256
                            w = slice(k0, k0 + 128)
                            b0 = 0 if qb == 2 else 128
                            v(TT(bank[:, w], bank[:, w], tb("band")[:, b0:b0 + 128], ALU.add))
                        m = st[:, n % 4, c, 0:1]
                        v(dve.tensor_reduce(m, bank[:, 0:nk], AX.X, ALU.max))
                        if kind == "s":
                            v(TT(m, m, sink8[:, u:u + 1], ALU.max))
                        v(TS(st[:, n % 4, c, 1:2], m, -(HD ** -0.5), None, ALU.mult), m_ready)

                def normalise(n):
                    kind, u, qb = its[n]
                    nk = SEQ if qb < 2 else T
                    s0, s1 = st[:, n % 4, 0, :], st[:, n % 4, 1, :]
                    p0, p1 = Pb[:, n % 2, 0, 0:nk], Pb[:, n % 2, 1, 0:nk]
                    dve.wait_ge(S.free, marks[("exp", l, n, 0 if kind == "s" else 1)])
                    if kind == "s":
                        dve.wait_ge(es_ready, seen(es_ready))
                        v(TT(s0[:, 2:3], s0[:, 2:3], s0[:, 3:4], ALU.add))
                        v(dve.reciprocal(s0[:, 3:4], s0[:, 2:3]))
                        v(TS(p0, p0, s0[:, 3:4], None, ALU.mult), p_ready)
                    else:
                        v(dve.reciprocal(s0[:, 3:4], s0[:, 2:3]), wait=False)
                        v(dve.reciprocal(s1[:, 3:4], s1[:, 2:3]))
                        v(TS(p1, p1, s1[:, 3:4], cvec[:, 6:7], ALU.mult, ALU.mult))
                        v(STT(p0, p0, s0[:, 3:4], p1, ALU.mult, ALU.subtract), p_ready)

                def empty(n):
                    kind, u, qb = its[n]
                    bank = V_.take()
                    dve.wait_ge(V_.full, V_.taken)
                    qc = slice(128 * qb, 128 * qb + 128)
                    if kind == "s":
                        h = u % 2
                        ins = dve.tensor_copy(YA[64 * h:64 * h + 64, u // 2, qc], bank[64 * h:64 * h + 64, 0:128])
                    else:
                        ins = dve.tensor_copy(YC[:, u, qc], bank[:, 0:128])
                    vf(ins, wait=False)

                for n in range(len(its) + 3):
                    if n < len(its):
                        maxima(n)
                    if 1 <= n <= len(its):
                        normalise(n - 1)
                    if n >= 3:
                        empty(n - 3)
                c0 = C0s[l]
                dve.wait_ge(V_.free, V_.taken)
                v(dve.memset(cvec[:, 3:4], 0.0), to_act)
                for j in range(4):
                    dve.wait_ge(A.free, marks[("dfroot", l, j)])
                    v(dve.reciprocal(RS[:, 1, c0:T], RS[:, 0, c0:T]), to_act)
                    ins = STT(YC[:, j, c0:T], YC[:, j, c0:T], cvec[:, 7:8], RS[:, 1, c0:T], ALU.mult, ALU.mult)
                    v(ins, dve_step if j < 3 else to_pe_v)

            def merge(l):
                c0 = C0s[l]
                n = 0
                for b in range(3):
                    for j in range(KT):
                        dve.wait_ge(A.free, marks[("sgb", l, n)])
                        bank = V_.take()
                        dve.wait_ge(V_.full, V_.taken)
                        if b == 0:
                            vf(TT(MG[:, j, c0:T], sgb[:, n % 2, c0:T], bank[:, c0:T], ALU.mult))
                        else:
                            v(TT(mtmp[:, c0:T], sgb[:, n % 2, c0:T], bank[:, c0:T], ALU.mult))
                            vf(TT(MG[:, j, c0:T], MG[:, j, c0:T], mtmp[:, c0:T], ALU.add))
                        n += 1
                dve.wait_ge(reloaded, 16 * (l + 1))
                post(l, c0, "mix", lambda k, c: MO[:, k, c])

            def post(l, c0, which, src):
                dve.wait_ge(A.free, marks[("postroot", l, which)])
                v(dve.reciprocal(RS[:, 1, c0:T], RS[:, 0, c0:T]))
                ci = 1 if which == "mix" else 3
                for k in range(KT):
                    for s in range(c0 // SEQ, 2):
                        c = slice(SEQ * s, SEQ * s + SEQ)
                        x = src(k, c)
                        v(STT(x, x, coef[:, ci, k, s:s + 1], RS[:, 1, c], ALU.mult, ALU.mult))
                        v(TT(HT[:, k, c], HT[:, k, c], x, ALU.add), dve_step if s == 0 else h_ready)

            def ffn(l):
                for n in range(FT):
                    dve.wait_ge(A.free, marks[("silu", l, n)])
                    bank = V_.take()
                    dve.wait_ge(V_.full, V_.taken)
                    vf(TT(hid[:, n, :], htmp[:, n % 2, :], bank[:, :], ALU.mult), wait=False)
                post(l, 0, "ffn", lambda k, c: MO[:, k, c])

            def moe(l):
                bank = V_.take()
                dve.wait_ge(V_.full, V_.taken)
                v(dve.tensor_copy(rt[:, 0, 0:8], bank[:, 0:NE]))
                vf(dve.tensor_copy(rt[:, 1, 0:8], bank[:, NE:2 * NE]))
                for b in range(2):
                    r = rt[:, b, :]
                    v(dve.max(r[:, 16:24], r[:, 0:8]))
                    v(dve.max_index(rti[:, b, :], r[:, 16:24], r[:, 0:8]))
                    v(dve.tensor_copy(r[:, 24:26], rti[:, b, 0:2]))
                    v(TT(r[:, 26:27], r[:, 17:18], r[:, 16:17], ALU.subtract), lam_in)
                    dve.wait_ge(lam_out, seen(lam_out))
                    v(TS(r[:, 28:29], r[:, 27:28], 1.0, None, ALU.add))
                    v(dve.reciprocal(r[:, 29:30], r[:, 28:29]))
                    v(TT(r[:, 30:31], r[:, 29:30], r[:, 27:28], ALU.mult))
                    v(TS(r[:, 32:40], tb("iota")[:, 0:8], r[:, 24:25], None, ALU.is_equal))
                    v(TS(r[:, 40:48], tb("iota")[:, 0:8], r[:, 25:26], None, ALU.is_equal))
                    v(TS(r[:, 8:16], r[:, 32:40], r[:, 29:30], None, ALU.mult))
                    v(STT(r[:, 8:16], r[:, 40:48], r[:, 30:31], r[:, 8:16], ALU.mult, ALU.add))
                    v(TT(r[:, 48:56], r[:, 32:40], r[:, 40:48], ALU.add), dve_step if b == 0 else to_pe_v)
                for b in range(2):
                    for k4 in range(2):
                        bank = V_.take()
                        dve.wait_ge(V_.full, V_.taken)
                        vf(dve.tensor_copy(Atok[:, b, 512 * k4:512 * k4 + 512], bank[:, :]), wait=False)
                bank = V_.take()
                dve.wait_ge(V_.full, V_.taken)
                v(dve.tensor_copy(rt[:, 0, 56:64], bank[:, 0:8]))
                v(dve.tensor_copy(rt[:, 1, 56:64], bank[:, 8:16]))
                vf(dve.tensor_reduce(cvec[:, 20:21], bank[:, 16:24], AX.X, ALU.max))
                v(TS(flag[0:1, 0:1], cvec[0:1, 20:21], float(CAP), None, ALU.is_gt), flag_ready)
                experts(0, A, V_)
                crowded = dve.value_load(flag[0:1, 0:1], min_val=0, max_val=1)
                with dve.If(crowded > 0):
                    chain[0] = dve_step2
                    for b in range(2):
                        v(TS(rt[:, b, 56:64], rt[:, b, 56:64], -float(CAP), None, ALU.add))
                    experts(1, A2, V2)
                    chain[0] = dve_step
                v(dve.memset(cvec[:, 3:4], 0.0), to_act)
                post(l, SEQ, "ffn", lambda k, c: FA[:, k, :])

            def experts(p, A, V_):
                def take():
                    return V_.take()

                def emptied(ins, wait=False):
                    ins.then_inc(V_.free, 1)
                    if wait:
                        dve.wait_ge(V_.free, V_.taken)

                def select(e):
                    for b in range(2):
                        r = rt[:, b, :]
                        ins = TS(Psel[:, e % 2, b, :], tb("iota"), r[:, 56 + e:57 + e], r[:, 48 + e:49 + e],
                                 ALU.is_equal, ALU.mult)
                        v(ins, chain[0] if b == 0 else to_pe_v)

                def weigh(e):
                    for b in range(2):
                        r = rt[:, b, :]
                        v(TS(Pw[:, b, :], tb("iota"), r[:, 56 + e:57 + e], r[:, 8 + e:9 + e], ALU.is_equal, ALU.mult),
                          chain[0] if b == 0 else to_pe_v)

                def gathered(e):
                    for k4 in range(2):
                        bank = take()
                        dve.wait_ge(V_.full, V_.taken)
                        emptied(dve.tensor_copy(XE[:, e % 2, 4 * k4:4 * k4 + 4, :],
                                                bank[:, :].rearrange("p (k t) -> p k t", k=4)))

                def combined(e):
                    for k2 in range(4):
                        bank = take()
                        dve.wait_ge(V_.full, V_.taken)
                        b3 = bank[:, :].rearrange("p (k t) -> p k t", k=2)
                        x = FA[:, 2 * k2:2 * k2 + 2, :]
                        if p == 0 and e == 0:
                            emptied(dve.tensor_copy(x, b3))
                        else:
                            emptied(TT(x, x, b3, ALU.add))

                select(0)
                gathered(0)
                for e in range(NE):
                    if e < NE - 1:
                        select(e + 1)
                    for j in range(ET // 2):
                        dve.wait_ge(A.free, marks[("silu", p, e, j)])
                        bank = take()
                        dve.wait_ge(V_.full, V_.taken)
                        emptied(TT(hidm[:, 2 * j:2 * j + 2, :], htm[:, j % 2, :].rearrange("p (i t) -> p i t", i=2),
                                   bank[:, 0:2 * CAP].rearrange("p (i t) -> p i t", i=2), ALU.mult))
                        if e and j == 1:
                            combined(e - 1)
                        if j == 2:
                            weigh(e)
                    if e < NE - 1:
                        gathered(e + 1)
                    bank = take()
                    dve.wait_ge(V_.full, V_.taken)
                    emptied(dve.tensor_copy(PwT[:, e % 2, :], bank[:, 0:SEQ]))
                combined(NE - 1)
                dve.wait_ge(V_.free, V_.taken)
            for l in range(2):
                ada(l)
                norm(l, 0, "mix")
                recurrence_inputs(l)
                S.begin(("steps", l))
                for i in range(NCH):
                    recurrence_step(l, i)
                recurrence_output(l)
                attention_inputs(l)
                attention(l)
                merge(l)
                norm(l, C0s[l], "ffn")
                (ffn if l == 0 else moe)(l)

        @block.gpsimd
        def _(pool):
            xt = io["xt"].rearrange("(k p) t -> p k t", p=128)
            g_dram = g_spill.rearrange("(j p) t -> p j t", p=128)
            at_dram = at_spill.rearrange("(k p) t -> p k t", p=128)

            def spill_input(l):
                pool.wait_ge(at_ready, KT * (1 + 2 * l))
                pool.dma_start(at_dram, AT[:, :, :]).then_inc(at_spilled, 16)
                pool.wait_ge(A.free, marks[("g", l, 3)])
                pool.dma_start(g_dram, YB[:, :, :]).then_inc(g_spilled, 16)

            def reload_input(l):
                pool.wait_ge(at_spilled, 16 * (l + 1))
                pool.dma_start(AT[:, :, :], at_dram).then_inc(at_reloaded, 16)
                pool.wait_ge(g_spilled, 16 * (l + 1))
                pool.dma_start(YB[:, :, :], g_dram).then_inc(g_reloaded, 16)

            spill_input(0)
            pool.wait_ge(to_pool, 1)
            reload_input(0)
            pool.dma_start(HT[:, :, :], xt).then_inc(reloaded, 16)
            pool.wait_ge(h_ready, 2 * KT)
            pool.dma_start(spill.rearrange("(k p) t -> p k t", p=128), HT[:, :, SEQ:T]).then_inc(spilled, 16)
            spill_input(1)
            pool.wait_ge(spilled, 16)
            pool.wait_ge(to_pool, 2)
            reload_input(1)
            pool.dma_start(HT[:, :, SEQ:T], spill.rearrange("(k p) t -> p k t", p=128)).then_inc(reloaded, 16)
            pool.wait_ge(h_ready, 4 * KT)
            pool.dma_start(out.rearrange("(k p) t -> p k t", p=128), HT[:, :, SEQ:T]).then_inc(stored, 16)
            pool.wait_ge(stored, 16)

        @block.sync
        def _(sp):
            def load(W, count):
                for n in range(count):
                    if n >= SLOTS:
                        s, value = W.released[n - SLOTS]
                        sp.wait_ge(s, value)
                    for at, src in W.chunks[n]:
                        size = src.shape[1] * src.shape[2]
                        dst = WR[:, n % SLOTS, at:at + size].rearrange("p (k n) -> p k n", k=src.shape[1])
                        sp.dma_start(dst, src).then_inc(W.sems[n % SLOTS], 16)

            load(W, W.arrived)
            sp.wait_ge(flag_ready, 1)
            crowded = sp.value_load(flag[0:1, 0:1], min_val=0, max_val=1)
            with sp.If(crowded > 0):
                sp.wait_ge(*W.released[-1])
                load(W2, W2.arrived)


NAMES = ["w_in", "ada_w", "rwkv_w_up", "rwkv_a_up", "rwkv_g_up", "proj_swa", "proj_rwkv", "proj_diff", "w_out",
         "ffn_w_gate", "ffn_w_up", "ffn_w_down", "router_w", "moe_w_gate", "moe_w_up", "moe_w_down"]


def layout(inputs):
    a = {n: np.ascontiguousarray(inputs[n]) for n in NAMES}
    f = np.float32
    cols = lambda x: np.asarray(x, f).reshape(-1, 128).T
    vs = []
    for l in range(2):
        for n in ("pre_mix_g", "post_mix_g", "pre_ffn_g", "post_ffn_g", "ada_b", "rwkv_mu_prev", "rwkv_mu_next",
                  "rwkv_w0", "rwkv_a0", "rwkv_k_k", "rwkv_k_a", "rwkv_r_k", "rwkv_lnx_g", "rwkv_lnx_b",
                  "diff_subln_g"):
            vs.append(cols(inputs[n][l]))
    cc = np.stack([cols(inputs["c_ctx"]), cols(inputs["c"])], 2).reshape(128, 16)
    a["vectors"] = np.ascontiguousarray(np.concatenate(vs + [cc], 1))
    rep = np.concatenate([np.asarray(inputs["swa_sink"], f), np.asarray(inputs["diff_lambda"], f).reshape(2, 256)], 1)
    a["repeated"] = np.ascontiguousarray(np.broadcast_to(rep[None], (128, 2, 264)))
    a["xt"] = np.ascontiguousarray(np.concatenate([np.asarray(inputs["ctx"][0]).T, np.asarray(inputs["x"][0]).T], 1))
    a["tables"] = tables()
    return a


def kernel(**inputs):
    import concourse.bacc as bacc
    from concourse.bass_utils import run_bass_kernel_spmd

    nc = bacc.Bacc("TRN2", target_bir_lowering=False, num_devices=1)
    arrays = layout(inputs)
    io = {n: nc.dram_tensor("in_" + n, a.shape, mybir.dt.float32, kind="ExternalInput").ap() for n, a in arrays.items()}
    out = nc.dram_tensor("result", (D, SEQ), mybir.dt.float32, kind="ExternalOutput").ap()
    trunk(nc, io, out)
    r = run_bass_kernel_spmd(nc, [{"in_" + n: a for n, a in arrays.items()}], core_ids=[0])
    return np.ascontiguousarray(r.results[0]["result"].T)[None]
```
